# Optimizing a Trainium2 kernel written in Bass

```python
import math
import jax, jax.numpy as jnp
from jax import lax
import numpy as np

D_MODEL = 1024
BATCH = 1
SEQ = 2048
DEPTH = 1

GLA_HEADS = 4
GLA_DK = 64
GLA_DV = 128
GLA_RANK = 16
GLA_TAU = 16.0
GLA_CHUNK = 64
DIFF_HEADS = 4
DIFF_DQK = 64
DIFF_DV = 128
Q_BLOCK = 128
MEM_LEN = 256
CROSS_HEADS = 4
CROSS_DH = D_MODEL // CROSS_HEADS
N_GROUPS = 4
EXPERTS_PER_GROUP = 4
N_EXPERTS = N_GROUPS * EXPERTS_PER_GROUP
TOP_K = 2
D_EXPERT = 512
MOE_BLOCK = 128
EPS = 1e-6

GLA_QK_W = GLA_HEADS * GLA_DK
GLA_V_W = GLA_HEADS * GLA_DV
DIFF_QK_W = DIFF_HEADS * 2 * DIFF_DQK
DIFF_V_W = DIFF_HEADS * DIFF_DV
D_MIX = GLA_V_W + DIFF_V_W
IN_SPLITS = (GLA_QK_W, GLA_QK_W, GLA_V_W, GLA_RANK, GLA_V_W, DIFF_QK_W, DIFF_QK_W, DIFF_V_W)
D_IN = sum(IN_SPLITS)

kernel_name = "hybrid_gla_diffattn_hmoe_block"

def rmsnorm(x, g):
    xf = x.astype(jnp.float32)
    y = xf * lax.rsqrt(jnp.mean(xf * xf, axis=-1, keepdims=True) + EPS)
    return (y * g.astype(jnp.float32)).astype(x.dtype)

def alibi_slopes(n_heads):
    return jnp.asarray(2.0 ** (-8.0 * np.arange(1, n_heads + 1) / n_heads), dtype=jnp.float32)

def gla_chunked(q, k, v, log_a):
    b_, s_, h_, dk = q.shape
    dv = v.shape[-1]
    n = s_ // GLA_CHUNK

    def chunks(t):
        return t.reshape(b_, n, GLA_CHUNK, h_, t.shape[-1]).transpose(0, 3, 1, 2, 4)

    q, k, v, la = chunks(q), chunks(k), chunks(v), chunks(log_a)
    cum = jnp.cumsum(la, axis=3)
    cum_last = cum[:, :, :, -1:, :]
    q_e = q * jnp.exp(cum)
    k_e = k * jnp.exp(-cum)
    k_s = k * jnp.exp(cum_last - cum)
    causal = jnp.tril(jnp.ones((GLA_CHUNK, GLA_CHUNK), dtype=bool))
    att = jnp.where(causal, jnp.einsum('bhncd,bhnsd->bhncs', q_e, k_e), 0.0)
    o_intra = jnp.einsum('bhncs,bhnse->bhnce', att, v)
    kv = jnp.einsum('bhncd,bhnce->bhnde', k_s, v)
    decay = jnp.exp(cum_last[:, :, :, 0, :])

    def step(state, inp):
        dec, kv_n = inp
        return dec[..., None] * state + kv_n, state

    _, s_prev = lax.scan(step, jnp.zeros((b_, h_, dk, dv), q.dtype),
                         (jnp.moveaxis(decay, 2, 0), jnp.moveaxis(kv, 2, 0)))
    s_prev = jnp.moveaxis(s_prev, 0, 2)
    o = o_intra + jnp.einsum('bhncd,bhnde->bhnce', q_e, s_prev)
    return o.transpose(0, 2, 3, 1, 4).reshape(b_, s_, h_, dv)

def diff_attention(q, k, v, lam):
    b_, h_, _, s_, dqk = q.shape
    nb = s_ // Q_BLOCK
    slopes = alibi_slopes(h_)
    pos = jnp.arange(s_)
    scale = dqk ** -0.5
    q_blocks = jnp.moveaxis(q.reshape(b_, h_, 2, nb, Q_BLOCK, dqk), 3, 0)
    starts = jnp.arange(nb) * Q_BLOCK

    def block(args):
        qb, t0 = args
        t = t0 + jnp.arange(Q_BLOCK)
        dist = (t[:, None] - pos[None, :]).astype(jnp.float32)
        s = jnp.einsum('bhmqd,bhmkd->bhmqk', qb, k).astype(jnp.float32) * scale
        s = s - slopes[None, :, None, None, None] * dist
        s = jnp.where(dist >= 0, s, -jnp.inf)
        p = jax.nn.softmax(s, axis=-1)
        attn = p[:, :, 0] - lam * p[:, :, 1]
        return jnp.einsum('bhqk,bhkd->bhqd', attn.astype(v.dtype), v)

    o = lax.map(block, (q_blocks, starts))
    return o.transpose(1, 0, 3, 2, 4).reshape(b_, s_, h_, v.shape[-1])

def hybrid_mixer(h, w_in, w_gla_a2, b_gla_a, gla_norm_g, diff_norm_g,
                 lambda_q1, lambda_k1, lambda_q2, lambda_k2, w_out, lambda_init):
    b_, s_, _ = h.shape
    split_idx = [int(i) for i in np.cumsum(IN_SPLITS)[:-1]]
    q_g, k_g, v_g, a_lr, r_g, q_d, k_d, v_d = jnp.split(h @ w_in, split_idx, axis=-1)

    log_a = jax.nn.log_sigmoid((a_lr @ w_gla_a2 + b_gla_a).astype(jnp.float32)) / GLA_TAU
    o_g = gla_chunked(
        q_g.reshape(b_, s_, GLA_HEADS, GLA_DK).astype(jnp.float32) * (GLA_DK ** -0.5),
        k_g.reshape(b_, s_, GLA_HEADS, GLA_DK).astype(jnp.float32),
        v_g.reshape(b_, s_, GLA_HEADS, GLA_DV).astype(jnp.float32),
        log_a.reshape(b_, s_, GLA_HEADS, GLA_DK))
    o_g = rmsnorm(o_g, gla_norm_g).astype(h.dtype) * jax.nn.silu(r_g).reshape(b_, s_, GLA_HEADS, GLA_DV)
    o_g = o_g.reshape(b_, s_, GLA_V_W)

    lam = (jnp.exp(jnp.sum(lambda_q1.astype(jnp.float32) * lambda_k1.astype(jnp.float32)))
           - jnp.exp(jnp.sum(lambda_q2.astype(jnp.float32) * lambda_k2.astype(jnp.float32)))
           + lambda_init)
    qd = q_d.reshape(b_, s_, DIFF_HEADS, 2, DIFF_DQK).transpose(0, 2, 3, 1, 4)
    kd = k_d.reshape(b_, s_, DIFF_HEADS, 2, DIFF_DQK).transpose(0, 2, 3, 1, 4)
    vd = v_d.reshape(b_, s_, DIFF_HEADS, DIFF_DV).transpose(0, 2, 1, 3)
    o_d = diff_attention(qd, kd, vd, lam)
    o_d = (rmsnorm(o_d, diff_norm_g) * (1.0 - lambda_init)).reshape(b_, s_, DIFF_V_W)

    return jnp.concatenate([o_g, o_d], axis=-1) @ w_out

def memory_cross_attention(h, mem_n, w_cq, w_ckv, w_co):
    b_, s_, _ = h.shape
    q = (h @ w_cq).reshape(b_, s_, CROSS_HEADS, CROSS_DH)
    k, v = jnp.split(mem_n @ w_ckv, 2, axis=-1)
    k = k.reshape(b_, -1, CROSS_HEADS, CROSS_DH)
    v = v.reshape(b_, -1, CROSS_HEADS, CROSS_DH)
    s = jnp.einsum('bshd,bmhd->bhsm', q, k).astype(jnp.float32) * (CROSS_DH ** -0.5)
    p = jax.nn.softmax(s, axis=-1).astype(v.dtype)
    o = jnp.einsum('bhsm,bmhd->bshd', p, v).reshape(b_, s_, D_MODEL)
    return o @ w_co

def hierarchical_moe(h, w_rg, b_rg, w_re, b_re, w_g, w_u, w_d):
    t_ = h.shape[0]
    p_grp = jax.nn.softmax((h @ w_rg + b_rg).astype(jnp.float32), axis=-1)
    p_g, g_sel = lax.top_k(p_grp, 1)
    p_g, g_sel = p_g[:, 0], g_sel[:, 0]
    logits_e = (h @ w_re + b_re).astype(jnp.float32).reshape(t_, N_GROUPS, EXPERTS_PER_GROUP)
    p_in = jax.nn.softmax(logits_e[jnp.arange(t_), g_sel], axis=-1)
    w_top, i_top = lax.top_k(p_in, TOP_K)
    gate = p_g[:, None] * w_top / jnp.sum(w_top, axis=-1, keepdims=True)
    e_id = g_sel[:, None] * EXPERTS_PER_GROUP + i_top

    a_ = t_ * TOP_K
    e_flat = e_id.reshape(a_)
    tok_flat = jnp.arange(a_) // TOP_K
    gate_flat = gate.reshape(a_)
    order = jnp.argsort(e_flat)
    e_s, tok_s, gate_s = e_flat[order], tok_flat[order], gate_flat[order]
    counts = jax.ops.segment_sum(jnp.ones((a_,), jnp.int32), e_flat, num_segments=N_EXPERTS)
    padded = ((counts + MOE_BLOCK - 1) // MOE_BLOCK) * MOE_BLOCK
    pad_end = jnp.cumsum(padded)
    pad_start = pad_end - padded
    start = jnp.cumsum(counts) - counts
    dest = pad_start[e_s] + (jnp.arange(a_) - start[e_s])
    n_blocks = (a_ + MOE_BLOCK - 1) // MOE_BLOCK + N_EXPERTS
    n_rows = n_blocks * MOE_BLOCK
    xs = jnp.zeros((n_rows, h.shape[1]), h.dtype).at[dest].set(h[tok_s])
    blk_e = jnp.minimum(jnp.searchsorted(pad_end, jnp.arange(n_blocks) * MOE_BLOCK, side='right'),
                        N_EXPERTS - 1)

    def expert_block(args):
        xb, e = args
        hid = jax.nn.silu(xb @ w_g[e]) * (xb @ w_u[e])
        return hid @ w_d[e]

    ys = lax.map(expert_block, (xs.reshape(n_blocks, MOE_BLOCK, -1), blk_e)).reshape(n_rows, -1)
    contrib = ys[dest] * gate_s[:, None].astype(ys.dtype)
    return jax.ops.segment_sum(contrib, tok_s, num_segments=t_)

def setup_inputs(seed: int = 0) -> dict:
    key = jax.random.key(seed)
    ks = jax.random.split(key, 27)
    L = DEPTH

    def nrm(k, shape, scale):
        return jax.random.normal(k, shape, jnp.float32) * scale

    def gain(k, shape):
        return 1.0 + nrm(k, shape, 0.02)

    return {
        "x": nrm(ks[0], (BATCH, SEQ, D_MODEL), 1.0),
        "mem": nrm(ks[1], (BATCH, MEM_LEN, D_MODEL), 1.0),
        "norm_mix_g": gain(ks[2], (L, D_MODEL)),
        "w_in": nrm(ks[3], (L, D_MODEL, D_IN), D_MODEL ** -0.5),
        "w_gla_a2": nrm(ks[4], (L, GLA_RANK, GLA_QK_W), GLA_RANK ** -0.5),
        "b_gla_a": nrm(ks[5], (L, GLA_QK_W), 0.1),
        "gla_norm_g": gain(ks[6], (L, GLA_DV)),
        "diff_norm_g": gain(ks[7], (L, DIFF_DV)),
        "lambda_q1": nrm(ks[8], (L, DIFF_DQK), 0.1),
        "lambda_k1": nrm(ks[9], (L, DIFF_DQK), 0.1),
        "lambda_q2": nrm(ks[10], (L, DIFF_DQK), 0.1),
        "lambda_k2": nrm(ks[11], (L, DIFF_DQK), 0.1),
        "w_out": nrm(ks[12], (L, D_MIX, D_MODEL), D_MIX ** -0.5),
        "norm_cross_g": gain(ks[13], (L, D_MODEL)),
        "norm_mem_g": gain(ks[14], (L, D_MODEL)),
        "w_cq": nrm(ks[15], (L, D_MODEL, D_MODEL), D_MODEL ** -0.5),
        "w_ckv": nrm(ks[16], (L, D_MODEL, 2 * D_MODEL), D_MODEL ** -0.5),
        "w_co": nrm(ks[17], (L, D_MODEL, D_MODEL), D_MODEL ** -0.5),
        "norm_ffn_g": gain(ks[18], (L, D_MODEL)),
        "w_router_grp": nrm(ks[19], (L, D_MODEL, N_GROUPS), D_MODEL ** -0.5),
        "b_router_grp": nrm(ks[20], (L, N_GROUPS), 0.01),
        "w_router_exp": nrm(ks[21], (L, D_MODEL, N_EXPERTS), D_MODEL ** -0.5),
        "b_router_exp": nrm(ks[22], (L, N_EXPERTS), 0.01),
        "w_e_gate": nrm(ks[23], (L, N_EXPERTS, D_MODEL, D_EXPERT), D_MODEL ** -0.5),
        "w_e_up": nrm(ks[24], (L, N_EXPERTS, D_MODEL, D_EXPERT), D_MODEL ** -0.5),
        "w_e_down": nrm(ks[25], (L, N_EXPERTS, D_EXPERT, D_MODEL), D_EXPERT ** -0.5),
        "norm_final_g": gain(ks[26], (D_MODEL,)),
    }

def reference(x, mem, norm_mix_g, w_in, w_gla_a2, b_gla_a, gla_norm_g, diff_norm_g,
              lambda_q1, lambda_k1, lambda_q2, lambda_k2, w_out, norm_cross_g, norm_mem_g,
              w_cq, w_ckv, w_co, norm_ffn_g, w_router_grp, b_router_grp, w_router_exp,
              b_router_exp, w_e_gate, w_e_up, w_e_down, norm_final_g):
    b_, s_, d_ = x.shape
    for layer in range(DEPTH):
        lambda_init = 0.8 - 0.6 * math.exp(-0.3 * layer)
        x = x + hybrid_mixer(rmsnorm(x, norm_mix_g[layer]), w_in[layer], w_gla_a2[layer],
                             b_gla_a[layer], gla_norm_g[layer], diff_norm_g[layer],
                             lambda_q1[layer], lambda_k1[layer], lambda_q2[layer],
                             lambda_k2[layer], w_out[layer], lambda_init)
        x = x + memory_cross_attention(rmsnorm(x, norm_cross_g[layer]),
                                       rmsnorm(mem, norm_mem_g[layer]),
                                       w_cq[layer], w_ckv[layer], w_co[layer])
        y = hierarchical_moe(rmsnorm(x, norm_ffn_g[layer]).reshape(b_ * s_, d_),
                             w_router_grp[layer], b_router_grp[layer], w_router_exp[layer],
                             b_router_exp[layer], w_e_gate[layer], w_e_up[layer], w_e_down[layer])
        x = x + y.reshape(b_, s_, d_)
    return rmsnorm(x, norm_final_g)


_drawn_inputs = setup_inputs


def setup_inputs(seed=0):
    import zlib

    import numpy as np

    out = dict(_drawn_inputs(seed))
    spreads = {}
    factors = {'gla_norm_g': 4.543,
     'diff_norm_g': 2.988,
     'lambda_k1': 7.682,
     'lambda_q2': 8.0,
     'norm_cross_g': 8.0,
     'norm_mem_g': 7.878,
     'b_router_grp': 61.512,
     'b_router_exp': 45.336,
     'norm_final_g': 7.837,
     'norm_ffn_g': 8.0}
    for name, (base, spread) in spreads.items():
        noise = np.random.default_rng([zlib.crc32(name.encode()), seed]).standard_normal(out[name].shape)
        drawn = base * np.exp(spread * noise) if base else spread * noise
        out[name] = __import__('jax').numpy.asarray(drawn.astype(out[name].dtype))
    for name, factor in factors.items():
        out[name] = (out[name] * factor).astype(out[name].dtype)
    return out
```

```python
from contextlib import ExitStack

import concourse.bass as bass
from concourse import mybir

F32 = mybir.dt.float32
BF16 = mybir.dt.bfloat16
I32 = mybir.dt.int32
U8 = mybir.dt.uint8
ALU = mybir.AluOpType
ACT = mybir.ActivationFunctionType
AX = mybir.AxisListType.X

P = 128
D = 1024
KC = D // P
SEQ = 2048
NT = SEQ // P
HEADS = 4
GLA_DK, DV, CHUNK, RANK = 64, 128, 64, 16
GLA_QK, GLA_V = HEADS * GLA_DK, HEADS * DV
DQK = 64
MEM = 256
DH = D // HEADS
GROUPS, PER_GROUP = 4, 4
EXPERTS = GROUPS * PER_GROUP
DE = 512
NBLK = 2 * SEQ // P + EXPERTS
EPS = 1e-6
LAMBDA_INIT = 0.2
NEG = -1e30
CQ, CK = 0, GLA_QK
CV = 2 * GLA_QK
CA = CV + GLA_V
CR = CA + RANK
CDQ = CR + GLA_V
CDK = CDQ + HEADS * 2 * DQK
CDV = CDK + HEADS * 2 * DQK


def alloc(nc, ctx, phase):
    sems = []

    def sb(name, shape, dt=F32):
        return ctx.enter_context(nc.sbuf_tensor(f"{phase}_{name}", shape, dt))

    def ps(name, shape, dt=F32):
        return ctx.enter_context(nc.psum_tensor(f"{phase}_{name}", shape, dt))

    def sem(name):
        sems.append(nc.alloc_semaphore(name=f"{phase}_{name}"))
        return sems[-1]

    def clear():
        if sems:
            nc.clear_and_free_semaphores(sems)
            nc.all_engine_barrier()

    ctx.callback(clear)
    return sb, ps, sem


class Order:

    def __init__(self, eng, sem):
        self.eng, self.sem, self.base, self.n = eng, sem, 0, 0

    def at(self, base):
        self.base, self.n = base, 0

    def __call__(self, ins):
        self.n += 1
        ins.then_inc(self.sem, 1)
        self.eng.wait_ge(self.sem, self.base + self.n)


def constants(nc, c):
    with ExitStack() as ctx:
        _, _, sem = alloc(nc, ctx, "const")
        made, loaded = sem("const_made"), sem("gains_loaded")
        with nc.Block() as block:
            @block.gpsimd
            def _(pool):
                o = Order(pool, made)
                o(pool.memset(c.ident[:], 0.0))
                o(pool.affine_select(out=c.ident[:], in_=c.ident[:], compare_op=ALU.not_equal, fill=1.0,
                                     base=0, pattern=[[-1, P]], channel_multiplier=1))
                o(pool.tensor_copy(c.identb[:], c.ident[:]))
                o(pool.memset(c.maskb[:], 0.0))
                o(pool.affine_select(out=c.maskb[:], in_=c.maskb[:], compare_op=ALU.is_ge, fill=NEG,
                                     base=0, pattern=[[-1, P]], channel_multiplier=1))
                o(pool.memset(c.half[:], -0.5))
                o(pool.memset(c.eps[:], EPS))

            @block.sync
            def _(sp):
                n = 0
                for tile, gain in c.gains:
                    with nc.allow_non_contiguous_dma("small column loads"):
                        sp.dma_start(tile, gain).then_inc(loaded, 16)
                    n += 1
                sp.wait_ge(loaded, 16 * n)


def norm_phase(nc, c, x, hT):
    with ExitStack() as ctx:
        sb, ps, sem = alloc(nc, ctx, "norm")
        xin = [sb(f"xin{u}", [P, D]) for u in range(2)]
        xn = [sb(f"xn{u}", [P, D]) for u in range(2)]
        sq = [sb(f"sq{u}", [P, D], BF16) for u in range(2)]
        ss = [sb(f"ss{u}", [P, 1]) for u in range(2)]
        ms = [sb(f"ms{u}", [P, 1]) for u in range(2)]
        rs = [sb(f"rs{u}", [P, 1]) for u in range(2)]
        tp = [[ps(f"tp{u}{k}", [P, 4, P]) for k in range(2)] for u in range(2)]
        x_in = [sem(f"x_in{u}") for u in range(2)]
        x_free, sum_ok, rs_ok, xn_ok = (sem(n) for n in ("x_free", "sum_ok", "rs_ok", "xn_ok"))
        turned, low_out, high_out, ms_ok = (sem(n) for n in ("turned", "low_out", "high_out", "ms_ok"))
        with nc.Block() as block:
            @block.sync
            def _(sp):
                with sp.Fori(0, NT // 2) as pair:
                    for u in range(2):
                        t = 2 * pair + u
                        sp.wait_ge(x_free, t + 1)
                        sp.dma_start(xin[u][:], x[bass.ds(t * P, P), :]).then_inc(x_in[u], 16)

            @block.scalar
            def _(act):
                with act.Fori(0, NT // 2) as pair:
                    for u in range(2):
                        t = 2 * pair + u
                        act.wait_ge(x_in[u], 16 * (pair + 1))
                        act.activation(sq[u][:], xin[u][:], ACT.Square, scale=D ** -0.5,
                                       accum_out=ss[u][:]).then_inc(sum_ok, 1)
                        act.wait_ge(turned, 2 * t + 3)
                        for k in range(4):
                            last = act.activation(hT[:, 4 + k, bass.ds(t * P, P)], tp[u][1][:, k, :], ACT.Copy,
                                                  scale=c.g_mix[:, 4 + k:5 + k])
                        last.then_inc(high_out, 1)

            @block.gpsimd
            def _(pool):
                with pool.Fori(0, NT // 2) as pair:
                    for u in range(2):
                        t = 2 * pair + u
                        pool.wait_ge(sum_ok, t + 1)
                        pool.tensor_tensor(ms[u][:], ss[u][:], c.eps[:, 0:1], ALU.add).then_inc(ms_ok, 1)
                        pool.wait_ge(ms_ok, t + 1)
                        pool.tensor_tensor(rs[u][:], ms[u][:], c.half[:, 0:1], ALU.pow).then_inc(rs_ok, 1)

            @block.vector
            def _(dve):
                dve.sem_inc(x_free, 2)
                with dve.Fori(0, NT // 2) as pair:
                    for u in range(2):
                        t = 2 * pair + u
                        dve.wait_ge(rs_ok, t + 1)
                        dve.wait_ge(turned, 2 * t + 1)
                        dve.tensor_scalar(xn[u][:], xin[u][:], rs[u][:, 0:1], None, ALU.mult).then_inc(xn_ok, 1)
                        dve.wait_ge(xn_ok, t + 1)
                        dve.sem_inc(x_free, 1)
                        dve.wait_ge(turned, 2 * t + 2)
                        dve.tensor_tensor(hT[:, 0:4, bass.ds(t * P, P)], tp[u][0][:],
                                          c.g_mix[:, 0:4].unsqueeze(2).to_broadcast([P, 4, P]), ALU.mult).then_inc(low_out, 1)

            @block.tensor
            def _(pe):
                pe.sem_inc(turned, 1)
                pe.sem_inc(low_out, 2)
                pe.sem_inc(high_out, 2)
                with pe.Fori(0, NT // 2) as pair:
                    for u in range(2):
                        t = 2 * pair + u
                        pe.wait_ge(xn_ok, t + 1)
                        pe.wait_ge(low_out, t + 1)
                        pe.wait_ge(high_out, t + 1)
                        for k in range(KC):
                            last = pe.transpose(tp[u][k // 4][:, k % 4, :], xn[u][:, k * P:(k + 1) * P], c.ident[:])
                            if k % 4 == 3:
                                last.then_inc(turned, 1)


def gate_phase(nc, c, hT, w_in, w_a2, b_a, ep, en, decay):
    N = 512
    with ExitStack() as ctx:
        sb, ps, sem = alloc(nc, ctx, "gate")
        wa, wa2, bcol = sb("wa", [P, KC, RANK]), sb("wa2", [RANK, GLA_QK]), sb("bcol", [P, 2])
        low = sb("low", [RANK, 2, N])
        cum, keep = sb("cum", [P, 2, SEQ]), sb("keep", [P, SEQ])
        lowps, zps = ps("lowps", [RANK, 2, N]), ps("zps", [P, 4, N])
        wa_in, low_mm, low_out, z_mm, z_out = (sem(n) for n in ("wa_in", "low_mm", "low_out", "z_mm", "z_out"))
        keep_ok, mag_ok, soft_ok, sums_ok, exps_ok = (sem(n) for n in ("keep_ok", "mag_ok", "soft_ok", "sums_ok", "exps_ok"))
        dve_step, act_step = sem("dve_step"), sem("act_step")
        z, soft = ep, en
        with nc.Block() as block:
            @block.sync
            def _(sp):
                with nc.allow_non_contiguous_dma("16 columns of w_in; a bias as columns"):
                    sp.dma_start(wa[:], w_in[:, CA:CA + RANK].rearrange("(k p) r -> p k r", p=P)).then_inc(wa_in, 16)
                    sp.dma_start(wa2[:], w_a2).then_inc(wa_in, 16)
                    sp.dma_start(bcol[:], b_a.rearrange("(k p) -> p k", p=P)).then_inc(wa_in, 16)

            @block.gpsimd
            def _(pool):
                pool.memset(keep[:], 1.0).then_inc(keep_ok, 1)
                pool.wait_ge(keep_ok, 1)
                pool.memset(keep[:].rearrange("p (n s) -> p n s", s=CHUNK)[:, :, 0:1], 0.0).then_inc(keep_ok, 1)

            @block.tensor
            def _(pe):
                def gate_input(g):
                    pe.wait_ge(low_out, g + 1)
                    for pair in range(2):
                        last = pe.matmul(zps[:, 2 * (g % 2) + pair, :], wa2[:, pair * P:(pair + 1) * P], low[:, g % 2, :],
                                         start=True, stop=True)
                    last.then_inc(z_mm, 1)

                pe.wait_ge(wa_in, 48)
                for g in range(SEQ // N):
                    if g >= 2:
                        pe.wait_ge(low_out, g - 1)
                    for k in range(KC):
                        last = pe.matmul(lowps[:, g % 2, :], wa[:, k, :], hT[:, k, g * N:(g + 1) * N],
                                         start=(k == 0), stop=(k == KC - 1))
                    last.then_inc(low_mm, 1)
                    if g >= 1:
                        if g >= 3:
                            pe.wait_ge(z_out, g - 2)
                        gate_input(g - 1)
                pe.wait_ge(z_out, 2)
                gate_input(SEQ // N - 1)

            @block.scalar
            def _(act):
                for g in range(SEQ // N):
                    act.wait_ge(low_mm, g + 1)
                    if g >= 2:
                        act.wait_ge(z_mm, g - 1)
                    act.activation(low[:, g % 2, :], lowps[:, g % 2, :], ACT.Copy).then_inc(low_out, 1)
                act.wait_ge(mag_ok, 1)
                act.activation(soft[:], soft[:], ACT.Exp).then_inc(act_step, 1)
                act.wait_ge(act_step, 1)
                act.activation(soft[:], soft[:], ACT.Ln, bias=1.0).then_inc(soft_ok, 1)
                for pair in range(2):
                    act.wait_ge(sums_ok, pair + 1)
                    act.activation(ep[:, pair, :], cum[:, pair, :], ACT.Exp, scale=1.0 / 16.0).then_inc(exps_ok, 1)
                    act.activation(en[:, pair, :], cum[:, pair, :], ACT.Exp, scale=-1.0 / 16.0)

            @block.vector
            def _(dve):
                o = Order(dve, dve_step)
                dve.wait_ge(wa_in, 48)
                for g in range(SEQ // N):
                    dve.wait_ge(z_mm, g + 1)
                    for pair in range(2):
                        last = dve.tensor_scalar(z[:, pair, g * N:(g + 1) * N], zps[:, 2 * (g % 2) + pair, :],
                                                 bcol[:, pair:pair + 1], None, ALU.add)
                    last.then_inc(z_out, 1)
                dve.wait_ge(z_out, SEQ // N)
                o(dve.tensor_scalar(cum[:], z[:], 0.0, None, ALU.min))
                o(dve.tensor_tensor(z[:], cum[:], z[:], ALU.subtract))
                dve.tensor_tensor(soft[:], z[:], cum[:], ALU.add).then_inc(mag_ok, 1)
                dve.wait_ge(soft_ok, 1)
                o(dve.tensor_tensor(z[:], cum[:], soft[:], ALU.subtract))
                dve.wait_ge(keep_ok, 2)
                for pair in range(2):
                    dve.tensor_tensor_scan(cum[:, pair, :], keep[:], z[:, pair, :], 0.0, ALU.mult,
                                           ALU.add).then_inc(sums_ok, 1)
                dve.wait_ge(exps_ok, 2)
                ends = ep[:].rearrange("p a (t n s) -> p a t n s", n=2, s=CHUNK)
                for half in range(2):
                    for chunk in range(2):
                        dve.tensor_copy(decay[chunk * 64:chunk * 64 + 64, half::2, :],
                                        ends[half * 64:half * 64 + 64, :, :, chunk, CHUNK - 1])


def gla_phase(nc, c, hT, w_in, w_a2, b_a, gain, mixed):
    with ExitStack() as outer:
        sb, ps, sem = alloc(nc, outer, "gla")
        ep, en = sb("ep", [P, 2, SEQ]), sb("en", [P, 2, SEQ])
        decay = sb("decay", [P, HEADS, NT])
        gate_phase(nc, c, hT, w_in, w_a2, b_a, ep, en, decay)
        wqk, wvr, gb = sb("w_qk", [P, KC, 2 * GLA_QK]), sb("w_vr", [P, KC, 2 * GLA_V]), sb("gb", [P, DV])
        hs = sb("hs", [P, KC, P])
        qe = [sb(f"qe{u}", [P, 2, P]) for u in range(2)]
        ke = [sb(f"ke{u}", [P, 2, P]) for u in range(2)]
        ks = [sb(f"ks{u}", [P, 2, P]) for u in range(2)]
        q2 = [sb(f"q2{u}", [P, HEADS, P]) for u in range(2)]
        k2 = [sb(f"k2{u}", [P, HEADS, P]) for u in range(2)]
        at = [sb(f"at{u}", [P, 2, 2, P]) for u in range(2)]
        v = [sb(f"v{u}", [P, GLA_V]) for u in range(2)]
        gs = [sb(f"gs{u}", [P, GLA_V]) for u in range(2)]
        st = [sb(f"st{u}", [P, HEADS, DV]) for u in range(2)]
        fin = [sb(f"fin{u}", [P, GLA_V]) for u in range(2)]
        sq, tmp = sb("sq", [P, GLA_V]), sb("tmp", [P, HEADS, DV])
        seen = sb("seen", [P, P], I32)
        ss = [sb(f"ss{u}", [P, HEADS]) for u in range(2)]
        ms = [sb(f"ms{u}", [P, HEADS]) for u in range(2)]
        rs = [sb(f"rs{u}", [P, HEADS]) for u in range(2)]
        qkps, vps, rps = ps("qkps", [P, 4, P]), ps("vps", [P, GLA_V]), ps("rps", [P, GLA_V])
        aps, ktps = ps("aps", [P, 2, 512]), ps("ktps", [P, HEADS, GLA_DK])
        kvps, ops = ps("kvps", [P, HEADS, DV]), ps("ops", [P, HEADS, DV])

        w_in_ok, set_ok, pool_set = sem("w_in_ok"), sem("set_ok"), sem("pool_set")
        staged, pool_go = sem("staged"), sem("pool_go")
        vr_mm, qk_mm = sem("vr_mm"), sem("qk_mm")
        v_out, r_out, gated = sem("v_out"), sem("r_out"), sem("gated")
        qk_out, split_q, split_k = sem("qk_out"), sem("split_q"), sem("split_k")
        scores, turned, masked = sem("scores"), sem("turned"), sem("masked")
        kv_mm, mid_ok, carried = sem("kv_mm"), sem("mid_ok"), sem("carried")
        o_mm, sq_ok, sum_ok, eps_ok, rs_ok = sem("o_mm"), sem("sq_ok"), sem("sum_ok"), sem("eps_ok"), sem("rs_ok")
        o_out, finished, dve_step, dve_go = sem("o_out"), sem("finished"), sem("dve_step"), sem("dve_go")
        stored = [sem(f"stored{u}") for u in range(2)]

        with nc.Block() as block:
            @block.sync
            def _(sp):
                kin = w_in.rearrange("(k p) n -> p k n", p=P)
                sp.dma_start(wvr[:, :, 0:GLA_V], kin[:, :, CV:CV + GLA_V]).then_inc(w_in_ok, 16)
                sp.dma_start(wvr[:, :, GLA_V:], kin[:, :, CR:CR + GLA_V]).then_inc(w_in_ok, 16)
                sp.dma_start(wqk[:], kin[:, :, CQ:CQ + 2 * GLA_QK]).then_inc(w_in_ok, 16)
                sp.dma_start(gb[:], gain.partition_broadcast(P)).then_inc(w_in_ok, 16)

                def store(t, u):
                    sp.wait_ge(finished, t + 2)
                    sp.dma_start(mixed[bass.ds(t * P, P), 0:GLA_V], fin[u][:]).then_inc(stored[u], 16)

                with sp.Fori(0, NT // 2) as pair:
                    for u in range(2):
                        store(2 * pair + u, u)
                for u in range(2):
                    sp.wait_ge(stored[u], 16 * (NT // 2))

            @block.gpsimd
            def _(pool):
                o = Order(pool, pool_set)
                o(pool.memset(seen[:], 1))
                o(pool.affine_select(out=seen[:], in_=seen[:], compare_op=ALU.is_ge, fill=0, base=0,
                                     pattern=[[1, P]], channel_multiplier=-1))
                o(pool.memset(seen[0:CHUNK, CHUNK:], 0))
                for u in range(2):
                    pool.memset(q2[u][:], 0.0)
                    pool.memset(k2[u][:], 0.0)
                    o(pool.memset(at[u][:], 0.0))
                o(pool.memset(st[0][:], 0.0))
                pool.sem_inc(set_ok, 1)
                pool.sem_inc(gated, 1)
                pool.wait_ge(w_in_ok, 64)

                def stage(t):
                    pool.wait_ge(qk_mm, t)
                    pool.sem_inc(pool_go, 1)
                    pool.tensor_copy(hs[:], hT[:, :, bass.ds(t * P, P)]).then_inc(staged, 1)

                def gate(t, u):
                    pool.wait_ge(r_out, t + 2)
                    pool.tensor_tensor(gs[u][:].rearrange("p (h e) -> p h e", e=DV),
                                       gs[u][:].rearrange("p (h e) -> p h e", e=DV),
                                       gb[:].unsqueeze(1).to_broadcast([P, HEADS, DV]), ALU.mult).then_inc(gated, 1)

                def rsqrt(t, u):
                    pool.wait_ge(sum_ok, t + 1)
                    pool.tensor_tensor(ms[u][:], ss[u][:], c.eps[:], ALU.add).then_inc(eps_ok, 1)
                    pool.wait_ge(eps_ok, t + 1)
                    pool.tensor_tensor(rs[u][:], ms[u][:], c.half[:], ALU.pow).then_inc(rs_ok, 1)

                pool.tensor_copy(hs[:], hT[:, :, 0:P]).then_inc(staged, 1)
                gate(0, 0)
                stage(1)
                with pool.Fori(0, NT // 2 - 1) as pair:
                    for u in range(2):
                        t = 2 * pair + u
                        gate(t + 1, 1 - u)
                        stage(t + 2)
                        rsqrt(t, u)
                gate(NT - 1, 1)
                rsqrt(NT - 2, 0)
                rsqrt(NT - 1, 1)

            @block.scalar
            def _(act):
                act.sem_inc(v_out, 1)
                act.sem_inc(r_out, 1)
                act.wait_ge(set_ok, 1)

                def values(t, u):
                    act.wait_ge(vr_mm, t + 1)
                    act.activation(v[u][:], vps[:], ACT.Copy).then_inc(v_out, 1)
                    act.activation(gs[u][:], rps[:], ACT.Silu).then_inc(r_out, 1)

                def split(t, u):
                    act.wait_ge(qk_out, t + 2)
                    for half in range(2):
                        for chunk in range(2):
                            cols = slice(chunk * CHUNK, (chunk + 1) * CHUNK)
                            last = act.activation(q2[u][chunk * 64:chunk * 64 + 64, half::2, cols],
                                                  qe[u][half * 64:half * 64 + 64, :, cols], ACT.Copy)
                    last.then_inc(split_q, 1)

                def square(t):
                    act.wait_ge(o_mm, t + 1)
                    act.wait_ge(finished, t + 1)
                    act.activation(sq[:], ops[:].rearrange("p h e -> p (h e)"), ACT.Square,
                                   scale=DV ** -0.5).then_inc(sq_ok, 1)

                values(0, 0)
                split(0, 0)
                with act.Fori(0, NT // 2 - 1) as pair:
                    for u in range(2):
                        t = 2 * pair + u
                        act.wait_ge(finished, t + 1)
                        values(t + 1, 1 - u)
                        split(t + 1, 1 - u)
                        square(t)
                act.wait_ge(finished, NT - 1)
                values(NT - 1, 1)
                split(NT - 1, 1)
                square(NT - 2)
                square(NT - 1)

            @block.vector
            def _(dve):
                for s in (masked, split_k, carried, qk_out, o_out, finished):
                    dve.sem_inc(s, 1)
                dve.wait_ge(set_ok, 1)
                o = Order(dve, dve_step)

                def project_out(t, u):
                    dve.wait_ge(qk_mm, t + 1)
                    here = bass.ds(t * P, P)
                    dve.scalar_tensor_tensor(out=qe[u][:], in0=qkps[:, 0:2, :], scalar=GLA_DK ** -0.5,
                                             in1=ep[:, :, here], op0=ALU.mult, op1=ALU.mult)
                    o(dve.tensor_tensor(ke[u][:], qkps[:, 2:4, :], en[:, :, here], ALU.mult))
                    for pair in range(2):
                        ends = ep[:, pair, here].rearrange("p (n s) -> p n s", s=CHUNK)[:, :, CHUNK - 1:CHUNK]
                        last = dve.tensor_tensor(ks[u][:, pair, :].rearrange("p (n s) -> p n s", s=CHUNK),
                                                 ke[u][:, pair, :].rearrange("p (n s) -> p n s", s=CHUNK),
                                                 ends.to_broadcast([P, 2, CHUNK]), ALU.mult)
                    last.then_inc(qk_out, 1)

                def chunk_work(t, u):
                    dve.wait_ge(scores, t + 1)
                    dve.sem_inc(dve_go, 1)
                    dve.copy_predicated(at[u][:].rearrange("p a b q -> p (a b) q"),
                                        seen[:].unsqueeze(1).to_broadcast([P, 4, P]),
                                        aps_view).then_inc(masked, 1)
                    dve.wait_ge(turned, t + 1)
                    dve.tensor_copy(k2[u][0:CHUNK, :, 0:64], ktps[0:CHUNK, :, :])
                    dve.tensor_copy(k2[u][CHUNK:P, :, 64:P], ktps[CHUNK:P, :, :]).then_inc(split_k, 1)

                def decayed(lo, t, u):
                    return dve.tensor_tensor(tmp[lo:lo + 64, :, :], st[u][lo:lo + 64, :, :],
                                             decay_now(t)[lo:lo + 64].to_broadcast([64, HEADS, DV]), ALU.mult)

                def decay_now(t):
                    return decay[:, :, bass.ds(t, 1)]

                def middle(t, u):
                    dve.wait_ge(kv_mm, t + 1)
                    o(decayed(0, t, u))
                    dve.tensor_tensor(st[u][64:P, :, :], tmp[0:64, :, :], kvps[0:64, :, :], ALU.add).then_inc(mid_ok, 1)

                def carry(t, u):
                    dve.wait_ge(mid_ok, t + 1)
                    o(decayed(64, t, u))
                    dve.tensor_tensor(st[1 - u][0:64, :, :], tmp[64:P, :, :], kvps[64:P, :, :], ALU.add).then_inc(carried, 1)
                    dve.wait_ge(carried, t + 2)

                def finish(t, u, pair):
                    dve.wait_ge(sq_ok, t + 1)
                    dve.tensor_reduce(ss[u][:], sq[:].rearrange("p (h e) -> p h e", e=DV), AX, ALU.add).then_inc(sum_ok, 1)
                    dve.wait_ge(rs_ok, t + 1)
                    dve.wait_ge(gated, t + 2)
                    if pair is not None:
                        dve.wait_ge(stored[u], 16 * pair)
                    dve.tensor_tensor(fin[u][:].rearrange("p (h e) -> p h e", e=DV), ops[:],
                                      rs[u][:].unsqueeze(2).to_broadcast([P, HEADS, DV]), ALU.mult).then_inc(o_out, 1)
                    dve.wait_ge(o_out, t + 2)
                    dve.tensor_tensor(fin[u][:], fin[u][:], gs[u][:], ALU.mult).then_inc(finished, 1)

                aps_view = aps[:, :, 0:2 * P].rearrange("p a (b q) -> p a b q", b=2)

                def step(t, u, pair, last=False):
                    chunk_work(t, u)
                    middle(t, u)
                    if not last:
                        project_out(t + 1, 1 - u)
                    carry(t, u)
                    finish(t, u, pair)

                project_out(0, 0)
                step(0, 0, None)
                step(1, 1, None)
                with dve.Fori(1, NT // 2 - 1) as pair:
                    for u in range(2):
                        o.at(1 + 3 * (2 * pair + u))
                        step(2 * pair + u, u, pair)
                o.at(1 + 3 * (NT - 2))
                step(NT - 2, 0, NT // 2 - 1)
                step(NT - 1, 1, NT // 2 - 1, last=True)

            @block.tensor
            def _(pe):
                def values(t):
                    pe.wait_ge(staged, t + 1)
                    pe.wait_ge(v_out, t + 1)
                    pe.wait_ge(r_out, t + 1)
                    for k in range(KC):
                        pe.matmul(vps[:], hs[:, k, :], wvr[:, k, 0:GLA_V], start=(k == 0), stop=(k == KC - 1))
                    for k in range(KC):
                        last = pe.matmul(rps[:], hs[:, k, :], wvr[:, k, GLA_V:], start=(k == 0), stop=(k == KC - 1))
                    last.then_inc(vr_mm, 1)

                def queries(t):
                    pe.wait_ge(qk_out, t + 1)
                    for m in range(4):
                        for k in range(KC):
                            last = pe.matmul(qkps[:, m, :], wqk[:, k, m * P:(m + 1) * P], hs[:, k, :],
                                             start=(k == 0), stop=(k == KC - 1))
                    last.then_inc(qk_mm, 1)

                def score(t, u):
                    pe.wait_ge(qk_out, t + 2)
                    pe.wait_ge(masked, t + 1)
                    for half in range(2):
                        rows = slice(half * 64, half * 64 + 64)
                        for pair in range(2):
                            last = pe.matmul(aps[:, half, pair * P:(pair + 1) * P], ke[u][rows, pair, :],
                                             qe[u][rows, pair, :], start=True, stop=True)
                    last.then_inc(scores, 1)
                    pe.wait_ge(split_k, t + 1)
                    for pair in range(2):
                        last = pe.transpose(ktps[:, 2 * pair:2 * pair + 2, :].rearrange("p h d -> p (h d)"), ks[u][:, pair, :],
                                            c.ident[:])
                    last.then_inc(turned, 1)

                def outer_products(t, u):
                    pe.wait_ge(split_k, t + 2)
                    pe.wait_ge(v_out, t + 2)
                    pe.wait_ge(carried, t + 1)
                    for h in range(HEADS):
                        last = pe.matmul(kvps[:, h, :], k2[u][:, h, :], v[u][:, h * DV:(h + 1) * DV], start=True, stop=True)
                    last.then_inc(kv_mm, 1)

                def outputs(t, u):
                    pe.wait_ge(masked, t + 2)
                    pe.wait_ge(split_q, t + 1)
                    pe.wait_ge(mid_ok, t + 1)
                    pe.wait_ge(o_out, t + 1)
                    for h in range(HEADS):
                        pe.matmul(ops[:, h, :], at[u][:, h % 2, h // 2, :], v[u][:, h * DV:(h + 1) * DV],
                                  start=True, stop=False)
                        last = pe.matmul(ops[:, h, :], q2[u][:, h, :], st[u][:, h, :], start=False, stop=True)
                    last.then_inc(o_mm, 1)

                def step(t, u, last=False):
                    score(t, u)
                    if not last:
                        values(t + 1)
                    outer_products(t, u)
                    if not last:
                        queries(t + 1)
                    outputs(t, u)

                pe.wait_ge(set_ok, 1)
                pe.wait_ge(w_in_ok, 64)
                values(0)
                queries(0)
                with pe.Fori(0, NT // 2 - 1) as pair:
                    for u in range(2):
                        step(2 * pair + u, u)
                step(NT - 2, 0)
                step(NT - 1, 1, last=True)


def diff_phase(nc, c, hT, w_in, gain, lambdas, mixed):
    W = 512
    BANKS = 4

    def chunks(i):
        return (i * P + P + W - 1) // W

    def first(i):
        return sum(chunks(j) for j in range(i))

    def portion(i, part):
        half = (chunks(i) + 1) // 2
        return range(half) if part == 0 else range(half, chunks(i))

    def width(i, k):
        return min(W, (i + 1) * P - k * W)

    ALL = first(NT)
    assert (2 * ALL) % BANKS == 0 and ALL % 4 == 0
    jobs = [(w, g, e) for g in range(4) for w, e in (("q", "act"), ("k", "dve"))]
    jobs += [("v", g, "dve" if g % 2 == 0 else "act") for g in range(4)]
    mine = {e: [j for j, job in enumerate(jobs) if job[2] == e] for e in ("act", "dve")}
    EACH = len(mine["act"])
    assert EACH == len(mine["dve"])

    with ExitStack() as ctx:
        sb, ps, sem = alloc(nc, ctx, "diff")
        wd = sb("wd", [P, KC, 3, P])
        qT = [sb(f"qT{m}", [P, SEQ]) for m in range(2)]
        kT = [sb(f"kT{m}", [P, SEQ]) for m in range(2)]
        v = sb("v", [P, NT, DV])
        pr = [[sb(f"pr{u}{m}", [P, SEQ]) for m in range(2)] for u in range(2)]
        aT = sb("aT", [P, 4, 4, P])
        qmul, kmul = sb("qmul", [P, 1]), sb("kmul", [P, 1])
        lam, lsum, lexp, neglam = sb("lam", [P, 4, DQK]), sb("lsum", [P, 2]), sb("lexp", [P, 2]), sb("neglam", [P, 1])
        lprod, ldif = sb("lprod", [P, DQK]), sb("ldif", [P, 1])
        gd, gdb, part = sb("gd", [P, DV]), sb("gdb", [P, DV]), sb("part", [P, 1])
        mx = [sb(f"mx{u}", [P, 2, 4]) for u in range(2)]
        top = [sb(f"top{u}", [P, 2]) for u in range(2)]
        ntop = [sb(f"ntop{u}", [P, 2]) for u in range(2)]
        ls = [sb(f"ls{u}", [P, 2, 4]) for u in range(2)]
        l = [sb(f"l{u}", [P, 2]) for u in range(2)]
        r = [sb(f"r{u}", [P, 2]) for u in range(2)]
        mixw = [sb(f"mixw{u}", [P, 1]) for u in range(2)]
        sq = [sb(f"sq{u}", [P, DV]) for u in range(2)]
        ss = [sb(f"ss{u}", [P, 1]) for u in range(2)]
        f = [[sb(f"f{u}{n}", [P, 1]) for n in range(4)] for u in range(2)]
        fin = [sb(f"fin{u}", [P, DV]) for u in range(2)]
        sps, tps, ops = ps("sps", [P, BANKS, W]), ps("tps", [P, 2, 4, P]), ps("ops", [P, 2, 512])

        small_in, ramps, lam_ok, lexp_ok, set_dve, set_pool = (sem(n) for n in (
            "small_in", "ramps", "lam_ok", "lexp_ok", "set_dve", "set_pool"))
        w_ok = sem("w_ok")
        proj_mm, q_out, kv_out, alibi_ok = sem("proj_mm"), sem("q_out"), sem("kv_out"), sem("alibi_ok")
        score_mm, max_ok, exp_ok, joined = sem("score_mm"), sem("max_ok"), sem("exp_ok"), sem("joined")
        turned, a_out, pv_mm = sem("turned"), sem("a_out"), sem("pv_mm")
        sq_ok, scale_ok, finished = sem("sq_ok"), sem("scale_ok"), sem("finished")
        dve_step, pool_step = sem("dve_step"), sem("pool_step")
        stored = [sem(f"stored{u}") for u in range(2)]
        copied = {"act": q_out, "dve": kv_out}

        def done(h, per, n):
            return h * per + n + 1

        with nc.Block() as block:
            @block.sync
            def _(sp):
                sp.dma_start(gdb[:], gain.partition_broadcast(P)).then_inc(small_in, 16)
                for n, vec in enumerate(lambdas):
                    sp.dma_start(lam[:, n, :], vec.partition_broadcast(P)).then_inc(small_in, 16)
                kin = w_in.rearrange("(k p) n -> p k n", p=P)

                def weights(h):
                    for n, col in enumerate((CDQ, CDK, CDV)):
                        sp.dma_start(wd[:, :, n, :], kin[:, :, bass.ds(h * P + col, P)]).then_inc(w_ok, 16)

                def store(h, i):
                    sp.wait_ge(finished, done(h, NT, i + 1))
                    sp.dma_start(mixed[i * P:(i + 1) * P, bass.ds(h * DV + GLA_V, DV)], fin[i % 2][:]).then_inc(stored[i % 2], 16)

                weights(0)
                with sp.Fori(0, HEADS - 1) as h:
                    sp.wait_ge(proj_mm, done(h, len(jobs), len(jobs)))
                    weights(h + 1)
                    for i in range(NT):
                        store(h, i)
                for i in range(NT):
                    store(HEADS - 1, i)
                for u in range(2):
                    sp.wait_ge(stored[u], 16 * HEADS * NT // 2)

            @block.gpsimd
            def _(pool):
                o = Order(pool, pool_step)
                pool.sem_inc(alibi_ok, 1)
                pool.sem_inc(scale_ok, 1)
                o(pool.memset(part[:], 1.0 / DV))
                two = slice(64, 66)
                for m in range(2):
                    pool.iota(qT[m][two, :], [[-1, SEQ]], base=0, channel_multiplier=0, allow_small_or_imprecise_dtypes=True)
                    o(pool.iota(kT[m][two, :], [[1, SEQ]], base=0, channel_multiplier=0, allow_small_or_imprecise_dtypes=True))
                pool.memset(qmul[two, :], 1.0)
                o(pool.memset(kmul[two, :], 1.0))
                for tile, row, fill in ((qT[0], 0, 1.0), (qT[1], 0, 1.0), (kT[0], 1, 1.0), (kT[1], 1, 1.0),
                                        (qmul, 1, 0.25), (kmul, 0, 0.25)):
                    n = tile.shape[1]
                    o(pool.affine_select(out=tile[two, :], in_=tile[two, :], compare_op=ALU.not_equal, fill=fill, base=-row,
                                         pattern=[[0, n]], channel_multiplier=1))
                START = o.n

                def scale(h, i, u):
                    pool.wait_ge(sq_ok, done(h, NT, i + 1))
                    a, b, d, e = f[u]
                    o(pool.tensor_tensor(a[:], ss[u][:], part[:], ALU.mult))
                    o(pool.tensor_tensor(b[:], a[:], c.eps[:, 0:1], ALU.add))
                    o(pool.tensor_tensor(d[:], b[:], c.half[:, 0:1], ALU.pow))
                    pool.tensor_tensor(e[:], d[:], r[u][:, 0:1], ALU.mult).then_inc(scale_ok, 1)

                with pool.Fori(0, HEADS) as h:
                    o.at(START + h * (3 * NT + 4))
                    pool.wait_ge(proj_mm, done(h, len(jobs), 1))
                    pool.wait_ge(scale_ok, done(h, NT, 0))
                    for m in range(2):
                        o(pool.tensor_tensor(qT[m][two, :], qT[m][two, :], qmul[two, :].to_broadcast([2, SEQ]), ALU.mult))
                        o(pool.tensor_tensor(kT[m][two, :], kT[m][two, :], kmul[two, :].to_broadcast([2, SEQ]), ALU.mult))
                    pool.sem_inc(alibi_ok, 1)
                    for i in range(NT):
                        scale(h, i, i % 2)

            @block.scalar
            def _(act):
                for s in (q_out, exp_ok, a_out, sq_ok):
                    act.sem_inc(s, 1)
                act.wait_ge(lam_ok, 1)
                act.activation(lexp[:], lsum[:], ACT.Exp).then_inc(lexp_ok, 1)

                def exps(h, i, m):
                    u = i % 2
                    act.wait_ge(max_ok, done(h, 2 * NT, 2 * i + m + 1))
                    if m == 0:
                        act.wait_ge(turned, done(h, ALL, first(i - 1) if i >= 2 else 0))
                    for k in range(chunks(i)):
                        s = 2 * first(i) + m * chunks(i) + k
                        w = width(i, k)
                        act.activation(pr[u][m][:, k * W:k * W + w], sps[:, s % BANKS, 0:w], ACT.Exp,
                                       bias=ntop[u][:, m:m + 1], accum_out=ls[u][:, m, k:k + 1]).then_inc(exp_ok, 1)

                def copies(h, i, part):
                    for k in portion(i, part):
                        g = first(i) + k
                        act.wait_ge(turned, done(h, ALL, g + 1))
                        act.wait_ge(pv_mm, done(h, ALL, max(g - 3, 0)))
                        n = width(i, k) // P
                        act.activation(aT[:, g % 4, 0:n, :], tps[:, g % 2, 0:n, :], ACT.Copy).then_inc(a_out, 1)

                def square(h, i):
                    u = i % 2
                    act.wait_ge(pv_mm, done(h, ALL, first(i + 1)))
                    act.wait_ge(finished, done(h, NT, max(i - 1, 0)))
                    act.activation(sq[u][:], ops[:, i % 2, 0:DV], ACT.Square, scale=r[u][:, 0:1],
                                   accum_out=ss[u][:]).then_inc(sq_ok, 1)

                with act.Fori(0, HEADS) as h:
                    for j in mine["act"]:
                        what, g, _ = jobs[j]
                        act.wait_ge(proj_mm, done(h, len(jobs), j + 1))
                        bank = sps[:, j % BANKS, :]
                        if what == "q":
                            for m in range(2):
                                last = act.activation(qT[m][0:DQK, g * W:(g + 1) * W], bank[m * 64:m * 64 + 64, :], ACT.Copy,
                                                      scale=DQK ** -0.5)
                        else:
                            last = act.activation(v[:, 4 * g:4 * g + 4, :].rearrange("p t d -> p (t d)"), bank, ACT.Copy)
                        last.then_inc(q_out, 1)
                    for i in range(NT + 2):
                        if i < NT:
                            exps(h, i, 0)
                        if 1 <= i <= NT:
                            copies(h, i - 1, 0)
                        if i < NT:
                            exps(h, i, 1)
                        if 1 <= i <= NT:
                            copies(h, i - 1, 1)
                        if i >= 2:
                            square(h, i - 2)

            @block.vector
            def _(dve):
                for s in (kv_out, max_ok, joined, finished):
                    dve.sem_inc(s, 1)
                o = Order(dve, dve_step)
                dve.wait_ge(small_in, 16 * 5)
                for n in range(2):
                    o(dve.tensor_tensor_reduce(lprod[:], lam[:, 2 * n, :], lam[:, 2 * n + 1, :], 1.0, 0.0, ALU.mult, ALU.add,
                                               lsum[:, n:n + 1]))
                dve.sem_inc(lam_ok, 1)
                dve.wait_ge(lexp_ok, 1)
                o(dve.tensor_tensor(ldif[:], lexp[:, 1:2], lexp[:, 0:1], ALU.subtract))
                o(dve.tensor_scalar(neglam[:], ldif[:], -LAMBDA_INIT, None, ALU.add))
                o(dve.tensor_scalar(gd[:], gdb[:], 1.0 - LAMBDA_INIT, None, ALU.mult))
                START = o.n

                def maxima(h, i, m):
                    u = i % 2
                    for k in range(chunks(i)):
                        s = 2 * first(i) + m * chunks(i) + k
                        dve.wait_ge(score_mm, done(h, 2 * ALL, s + 1))
                        last = dve.tensor_reduce(mx[u][:, m, k:k + 1], sps[:, s % BANKS, 0:width(i, k)], AX, ALU.max)
                    o(last)
                    o(dve.tensor_reduce(top[u][:, m:m + 1], mx[u][:, m, 0:chunks(i)], AX, ALU.max))
                    dve.tensor_scalar(ntop[u][:, m:m + 1], top[u][:, m:m + 1], -1.0, None, ALU.mult).then_inc(max_ok, 1)

                def join(h, i):
                    u = i % 2
                    dve.wait_ge(exp_ok, done(h, 2 * ALL, 2 * first(i + 1)))
                    o(dve.tensor_reduce(l[u][:], ls[u][:, :, 0:chunks(i)], AX, ALU.add))
                    o(dve.reciprocal(r[u][:], l[u][:]))
                    o(dve.scalar_tensor_tensor(out=mixw[u][:], in0=l[u][:, 0:1], scalar=neglam[:, 0:1], in1=r[u][:, 1:2],
                                               op0=ALU.mult, op1=ALU.mult))
                    for k in range(chunks(i)):
                        cols = slice(k * W, k * W + width(i, k))
                        dve.scalar_tensor_tensor(out=pr[u][0][:, cols], in0=pr[u][1][:, cols], scalar=mixw[u][:, 0:1],
                                                 in1=pr[u][0][:, cols], op0=ALU.mult, op1=ALU.add).then_inc(joined, 1)

                def finish(h, i):
                    u = i % 2
                    dve.wait_ge(scale_ok, done(h, NT, i + 1))
                    if i >= 2:
                        dve.wait_ge(stored[u], 16 * (h * (NT // 2) + i // 2))
                    dve.scalar_tensor_tensor(out=fin[u][:], in0=ops[:, i % 2, 0:DV], scalar=f[u][3][:, 0:1], in1=gd[:],
                                             op0=ALU.mult, op1=ALU.mult).then_inc(finished, 1)

                def head(h):
                    for j in mine["dve"]:
                        what, g, _ = jobs[j]
                        dve.wait_ge(proj_mm, done(h, len(jobs), j + 1))
                        bank = sps[:, j % BANKS, :]
                        if what == "k":
                            for m in range(2):
                                last = dve.tensor_copy(kT[m][0:DQK, g * W:(g + 1) * W], bank[m * 64:m * 64 + 64, :])
                        else:
                            last = dve.tensor_copy(v[:, 4 * g:4 * g + 4, :].rearrange("p t d -> p (t d)"), bank)
                        last.then_inc(kv_out, 1)
                    for i in range(NT + 2):
                        if i < NT:
                            maxima(h, i, 0)
                        if 1 <= i <= NT:
                            join(h, i - 1)
                        if i < NT:
                            maxima(h, i, 1)
                        if i >= 2:
                            finish(h, i - 2)

                head(0)
                PER = o.n - START
                with dve.Fori(1, HEADS) as h:
                    for u in range(2):
                        dve.wait_ge(stored[u], 16 * (NT // 2) * h)
                    o.at(START + h * PER)
                    head(h)

            @block.tensor
            def _(pe):
                for s in (proj_mm, score_mm, turned, pv_mm):
                    pe.sem_inc(s, 1)

                def project(h):
                    pe.wait_ge(w_ok, 48 * (h + 1))
                    pe.wait_ge(exp_ok, done(h, 2 * ALL, 0))
                    for j, (what, g, _) in enumerate(jobs):
                        if j >= BANKS:
                            e = jobs[j - BANKS][2]
                            pe.wait_ge(copied[e], done(h, EACH, mine[e].index(j - BANKS) + 1))
                        bank = sps[:, j % BANKS, :]
                        if what == "v":
                            for t in range(4):
                                for k in range(KC):
                                    last = pe.matmul(bank[:, t * DV:(t + 1) * DV], hT[:, k, (4 * g + t) * P:(4 * g + t + 1) * P],
                                                     wd[:, k, 2, :], start=(k == 0), stop=(k == KC - 1))
                        else:
                            for k in range(KC):
                                last = pe.matmul(bank, wd[:, k, "qk".index(what), :], hT[:, k, g * W:(g + 1) * W],
                                                 start=(k == 0), stop=(k == KC - 1))
                        last.then_inc(proj_mm, 1)

                def scores(h, i, m):
                    for k in range(chunks(i)):
                        s = 2 * first(i) + m * chunks(i) + k
                        w = width(i, k)
                        if s >= BANKS:
                            pe.wait_ge(exp_ok, done(h, 2 * ALL, s - BANKS + 1))
                        diag = k == chunks(i) - 1
                        if diag:
                            pe.matmul(sps[:, s % BANKS, w - P:w], c.identb[:], c.maskb[:], start=True, stop=False,
                                      skip_group_check=True)
                        last = pe.matmul(sps[:, s % BANKS, 0:w], qT[m][0:66, i * P:(i + 1) * P], kT[m][0:66, k * W:k * W + w],
                                         start=not diag, stop=True, skip_group_check=diag)
                        last.then_inc(score_mm, 1)

                def turn(h, i, k):
                    g = first(i) + k
                    pe.wait_ge(joined, done(h, ALL, g + 1))
                    pe.wait_ge(a_out, done(h, ALL, max(g - 1, 0)))
                    for b in range(width(i, k) // P):
                        last = pe.transpose(tps[:, g % 2, b, :], pr[i % 2][0][:, k * W + b * P:k * W + (b + 1) * P], c.ident[:])
                    last.then_inc(turned, 1)

                def weigh(h, i, k):
                    g = first(i) + k
                    pe.wait_ge(a_out, done(h, ALL, g + 1))
                    if k == 0:
                        pe.wait_ge(finished, done(h, NT, max(i - 1, 0)))
                    for b in range(width(i, k) // P):
                        t = 4 * k + b
                        last = pe.matmul(ops[:, i % 2, 0:DV], aT[:, g % 4, b, :], v[:, t, :], start=(t == 0), stop=(t == i))
                    last.then_inc(pv_mm, 1)

                with pe.Fori(0, HEADS) as h:
                    project(h)
                    for e in ("act", "dve"):
                        pe.wait_ge(copied[e], done(h, EACH, EACH))
                    pe.wait_ge(alibi_ok, done(h, 1, 1))
                    before = None
                    for i in range(NT + 1):
                        for part in range(2):
                            if i < NT:
                                scores(h, i, part)
                            if i >= 1:
                                for k in portion(i - 1, part):
                                    turn(h, i - 1, k)
                                    if before:
                                        weigh(h, *before)
                                    before = (i - 1, k)
                    weigh(h, *before)


def memory_phase(nc, c, mem, w_cq, w_ckv, w_co, wqk, wvo):
    MT = MEM // P
    PER_HEAD = DH // P
    with ExitStack() as ctx:
        sb, ps, sem = alloc(nc, ctx, "fold")
        xin = [sb(f"xin{t}", [P, D]) for t in range(MT)]
        sq = sb("sq", [P, MT, D])
        ss, ms, rs = (sb(n, [P, MT]) for n in ("ss", "ms", "rs"))
        memT = sb("memT", [P, KC, MEM])
        wch = [sb(f"wch{u}", [P, KC, P]) for u in range(2)]
        kvT = sb("kvT", [P, 2 * KC, MEM])
        wqT = [sb(f"wqT{d}", [P, KC, P]) for d in range(2)]
        vT = sb("vT", [P, PER_HEAD, MEM])
        wo = sb("wo", [P, KC, D])
        tps = ps("tps", [P, 2, 4, P])
        kvps = [ps(f"kvps{u}", [P, 512]) for u in range(2)]
        fps = ps("fps", [P, 4, 512])
        mem_in, wo_in = sem("mem_in"), sem("wo_in")
        w_ok = [sem(f"w_ok{u}") for u in range(2)]
        sum_ok, eps_ok, rs_ok, scaled = sem("sum_ok"), sem("eps_ok"), sem("rs_ok"), sem("scaled")
        turned, t_act, t_dve = sem("turned"), sem("t_act"), sem("t_dve")
        kv_mm, kv_out, fold_mm, f_act, f_dve, v_ok = (sem(n) for n in ("kv_mm", "kv_out", "fold_mm", "f_act", "f_dve", "v_ok"))
        kin, qin = (w.rearrange("(k p) n -> p k n", p=P) for w in (w_ckv, w_cq))
        with nc.Block() as block:
            @block.sync
            def _(sp):
                for t in range(MT):
                    sp.dma_start(xin[t][:], mem[t * P:(t + 1) * P, :]).then_inc(mem_in, 16)
                with sp.Fori(0, KC) as pair:
                    for u in range(2):
                        m = 2 * pair + u
                        sp.wait_ge(kv_mm, m + 1)
                        sp.dma_start(wch[u][:], kin[:, :, bass.ds(m * P, P)]).then_inc(w_ok[u], 16)
                for u in range(2):
                    sp.wait_ge(kv_mm, 2 * KC + u + 1)
                    sp.dma_start(wch[u][:], qin[:, :, u * P:(u + 1) * P]).then_inc(w_ok[u], 16)
                with sp.Fori(1, HEADS) as h:
                    for u in range(2):
                        sp.wait_ge(turned, 2 * (2 * h + u + MT) - 2)
                        sp.dma_start(wch[u][:], qin[:, :, bass.ds((2 * h + u) * P, P)]).then_inc(w_ok[u], 16)
                sp.dma_start(wo[:], w_co.rearrange("(k p) n -> p k n", p=P)).then_inc(wo_in, 16)

            @block.gpsimd
            def _(pool):
                pool.wait_ge(sum_ok, MT)
                pool.tensor_tensor(ms[:], ss[:], c.eps[:, 0:MT], ALU.add).then_inc(eps_ok, 1)
                pool.wait_ge(eps_ok, 1)
                pool.tensor_tensor(rs[:], ms[:], c.half[:, 0:MT], ALU.pow).then_inc(rs_ok, 1)

            @block.scalar
            def _(act):
                for s in (t_act, f_act, kv_out):
                    act.sem_inc(s, 1)
                act.wait_ge(mem_in, 16 * MT)
                for t in range(MT):
                    act.activation(sq[:, t, :], xin[t][:], ACT.Square, scale=D ** -0.5,
                                   accum_out=ss[:, t:t + 1]).then_inc(sum_ok, 1)
                for t in range(MT):
                    act.wait_ge(turned, 2 * t + 2)
                    for k in range(4):
                        last = act.activation(memT[:, 4 + k, t * P:(t + 1) * P], tps[:, 1, k, :], ACT.Copy,
                                              scale=c.g_mem[:, 4 + k:5 + k])
                    last.then_inc(t_act, 1)
                with act.Fori(0, KC) as pair:
                    for u in range(2):
                        m = 2 * pair + u
                        act.wait_ge(kv_mm, m + 3)
                        act.activation(kvT[:, bass.ds(m, 1), :].rearrange("p a n -> p (a n)"), kvps[u][:, 0:MEM],
                                       ACT.Copy).then_inc(kv_out, 1)
                with act.Fori(0, HEADS) as h:
                    for d in range(2):
                        act.wait_ge(turned, 2 * (2 * h + d + MT) + 2)
                        act.activation(wqT[d][:, 4:8, :], tps[:, 1, :, :], ACT.Copy).then_inc(t_act, 1)
                    act.wait_ge(fold_mm, h + 1)
                    for b in (2, 3):
                        last = act.activation(wqk[:, 2 * b:2 * b + 2, bass.ds(h * MEM, MEM)],
                                              fps[:, b, :].rearrange("p (r m) -> p r m", m=MEM), ACT.Copy, scale=DH ** -0.5)
                    last.then_inc(f_act, 1)
                with act.Fori(0, HEADS) as h:
                    act.wait_ge(fold_mm, h + HEADS + 1)
                    act.activation(wvo[:, bass.ds(2 * h + 1, 1), :].rearrange("p a n -> p (a n)"),
                                   fps[:, 2:4, :].rearrange("p b n -> p (b n)"), ACT.Copy).then_inc(f_act, 1)

            @block.vector
            def _(dve):
                dve.sem_inc(t_dve, 1)
                dve.sem_inc(f_dve, 1)
                dve.wait_ge(rs_ok, 1)
                for t in range(MT):
                    dve.tensor_scalar(xin[t][:], xin[t][:], rs[:, t:t + 1], None, ALU.mult).then_inc(scaled, 1)
                for t in range(MT):
                    dve.wait_ge(turned, 2 * t + 1)
                    dve.tensor_tensor(memT[:, 0:4, t * P:(t + 1) * P], tps[:, 0, :, :],
                                      c.g_mem[:, 0:4].unsqueeze(2).to_broadcast([P, 4, P]), ALU.mult).then_inc(t_dve, 1)
                with dve.Fori(0, HEADS) as h:
                    for d in range(2):
                        dve.wait_ge(turned, 2 * (2 * h + d + MT) + 1)
                        dve.tensor_copy(wqT[d][:, 0:4, :], tps[:, 0, :, :]).then_inc(t_dve, 1)
                    dve.wait_ge(fold_mm, h + 1)
                    for b in (0, 1):
                        last = dve.tensor_scalar(wqk[:, 2 * b:2 * b + 2, bass.ds(h * MEM, MEM)],
                                                 fps[:, b, :].rearrange("p (r m) -> p r m", m=MEM), DH ** -0.5, None, ALU.mult)
                    last.then_inc(f_dve, 1)
                dve.wait_ge(kv_out, 2 * KC + 1)
                with dve.Fori(0, HEADS) as h:
                    dve.wait_ge(fold_mm, h + HEADS)
                    dve.tensor_copy(vT[:], kvT[:, bass.ds(KC + 2 * h, 2), :]).then_inc(v_ok, 1)
                    dve.wait_ge(fold_mm, h + HEADS + 1)
                    dve.tensor_copy(wvo[:, bass.ds(2 * h, 1), :].rearrange("p a n -> p (a n)"),
                                    fps[:, 0:2, :].rearrange("p b n -> p (b n)")).then_inc(f_dve, 1)

            @block.tensor
            def _(pe):
                pe.sem_inc(kv_mm, 2)

                def turn(blocks, n):
                    pe.wait_ge(t_act, n + 1)
                    pe.wait_ge(t_dve, n + 1)
                    for k, blk in enumerate(blocks):
                        last = pe.transpose(tps[:, k // 4, k % 4, :], blk, c.ident[:])
                        if k % 4 == 3:
                            last.then_inc(turned, 1)

                for t in range(MT):
                    pe.wait_ge(scaled, t + 1)
                    turn([xin[t][:, k * P:(k + 1) * P] for k in range(KC)], t)
                pe.wait_ge(t_act, MT + 1)
                pe.wait_ge(t_dve, MT + 1)
                with pe.Fori(0, KC) as pair:
                    for u in range(2):
                        m = 2 * pair + u
                        pe.wait_ge(w_ok[u], 16 * (pair + 1))
                        if u == 0:
                            pe.wait_ge(kv_out, m + 1)
                        for k in range(KC):
                            last = pe.matmul(kvps[u][:, 0:MEM], wch[u][:, k, :], memT[:, k, :], start=(k == 0), stop=(k == KC - 1))
                        last.then_inc(kv_mm, 1)
                pe.wait_ge(kv_out, 2 * KC + 1)
                with pe.Fori(0, HEADS) as h:
                    for d in range(2):
                        pe.wait_ge(w_ok[d], 16 * (h + KC + 1))
                        turn([wch[d][:, k, :] for k in range(KC)], 2 * h + d + MT)
                    pe.wait_ge(t_act, 2 * h + MT + 3)
                    pe.wait_ge(t_dve, 2 * h + MT + 3)
                    pe.wait_ge(f_act, h + 1)
                    pe.wait_ge(f_dve, h + 1)
                    for row in range(KC):
                        for d in range(2):
                            last = pe.matmul(fps[:, row // 2, (row % 2) * MEM:(row % 2 + 1) * MEM], wqT[d][:, row, :],
                                             kvT[:, bass.ds(2 * h + d, 1), :].rearrange("p a n -> p (a n)"),
                                             start=(d == 0), stop=(d == 1))
                    last.then_inc(fold_mm, 1)
                pe.wait_ge(wo_in, 16)
                with pe.Fori(0, HEADS) as h:
                    pe.wait_ge(v_ok, h + 1)
                    pe.wait_ge(f_act, h + HEADS + 1)
                    pe.wait_ge(f_dve, h + HEADS + 1)
                    for half in range(2):
                        for mt in range(MT):
                            for d in range(2):
                                last = pe.matmul(fps[:, 2 * mt + half, :], vT[:, d, mt * P:(mt + 1) * P],
                                                 wo[:, bass.ds(2 * h + d, 1), half * 512:(half + 1) * 512].rearrange(
                                                     "p a n -> p (a n)"), start=(d == 0), stop=(d == 1))
                    last.then_inc(fold_mm, 1)


def cross_phase(nc, c, x, mixed, w_out, wqk, wvo, w_rg, w_re, x3, h4, logits):
    H = 512
    NR = GROUPS + EXPERTS
    with ExitStack() as ctx:
        sb, ps, sem = alloc(nc, ctx, "cross")
        wo, wr = sb("wo", [P, KC, D]), sb("wr", [P, KC, NR])
        mixin = [sb(f"mixin{u}", [P, D]) for u in range(2)]
        xin = [sb(f"xin{u}", [P, D]) for u in range(2)]
        x2 = [sb(f"x2{u}", [P, D]) for u in range(2)]
        x3t = [sb(f"x3t{u}", [P, D]) for u in range(2)]
        xn4 = [sb(f"xn4{u}", [P, D]) for u in range(2)]
        oT, hT3, pT, hT4 = (sb(n, [P, KC, P]) for n in ("oT", "hT3", "pT", "hT4"))
        xn3, pr, sq = sb("xn3", [P, D]), sb("pr", [P, HEADS, MEM]), sb("sq", [P, D])
        top, ntop, l, rl = (sb(n, [P, HEADS]) for n in ("top", "ntop", "l", "rl"))
        ss3, ms3, rs3, ss4, ms4, rs4 = (sb(n, [P, 1]) for n in ("ss3", "ms3", "rs3", "ss4", "ms4", "rs4"))
        tA, tB, acc, sc = (ps(n, [P, 2, H]) for n in ("tA", "tB", "acc", "sc"))
        w_ok = sem("w_ok")
        in_ok = [sem(f"in_ok{u}") for u in range(2)]
        names = ("o_turned oT_dve oT_act s_mm max_ok exp_ok p_ok out_mm x2_ok ss3_ok ms3_ok rs3_ok xn3_ok p_turned pT_dve "
                 "pT_act h4_turned hT4_dve hT4_act co_mm x3_ok ss4_ok ms4_ok rs4_ok xn4_ok r_mm logits_ok h3_turned "
                 "hT3_dve hT3_act dve_step").split()
        s = {n: sem(n) for n in names}
        x3_out = [sem(f"x3_out{u}") for u in range(2)]
        h4_out = [sem(f"h4_out{u}") for u in range(2)]

        def upto(t):
            return t + 2

        def steps(eng, step):
            step(0, 0, 0, True, False, False)
            step(1, 1, 0, True, True, False)
            with eng.Fori(1, NT // 2) as pair:
                for u in range(2):
                    step(2 * pair + u, u, pair, True, True, True)
            step(NT, 0, NT // 2, False, True, True)
            step(NT + 1, 1, NT // 2, False, False, True)

        def lows(tile):
            return tile[:, 0, :].rearrange("p (k n) -> p k n", n=P)

        with nc.Block() as block:
            @block.sync
            def _(sp):
                sp.dma_start(wo[:], w_out.rearrange("(k p) n -> p k n", p=P)).then_inc(w_ok, 16)
                with nc.allow_non_contiguous_dma("routers' weights: 4 and 16 columns"):
                    sp.dma_start(wr[:, :, 0:GROUPS], w_rg.rearrange("(k p) n -> p k n", p=P)).then_inc(w_ok, 16)
                    sp.dma_start(wr[:, :, GROUPS:], w_re.rearrange("(k p) n -> p k n", p=P)).then_inc(w_ok, 16)

                def load(t, u):
                    rows = bass.ds(t * P, P)
                    sp.dma_start(mixin[u][:], mixed[rows, :]).then_inc(in_ok[u], 16)
                    sp.dma_start(xin[u][:], x[rows, :]).then_inc(in_ok[u], 16)

                def stores(t, u):
                    rows = bass.ds(t * P, P)
                    sp.wait_ge(s["x3_ok"], upto(t))
                    sp.dma_start(x3[rows, :], x3t[u][:]).then_inc(x3_out[u], 16)
                    sp.wait_ge(s["xn4_ok"], upto(t))
                    sp.dma_start(h4[rows, :], xn4[u][:]).then_inc(h4_out[u], 16)

                for out in x3_out + h4_out:
                    sp.sem_inc(out, 16)
                load(0, 0)
                load(1, 1)
                with sp.Fori(0, NT // 2 - 1) as pair:
                    for u in range(2):
                        t = 2 * pair + u
                        sp.wait_ge(s["x2_ok"], upto(t))
                        sp.wait_ge(s["o_turned"], upto(t))
                        load(t + 2, u)
                        stores(t, u)
                stores(NT - 2, 0)
                stores(NT - 1, 1)
                for u in range(2):
                    sp.wait_ge(x3_out[u], 16 * (NT // 2 + 1))
                    sp.wait_ge(h4_out[u], 16 * (NT // 2 + 1))

            @block.gpsimd
            def _(pool):
                for n in ("ms3_ok", "rs3_ok", "ms4_ok", "rs4_ok"):
                    pool.sem_inc(s[n], 1)

                def rsqrt(t, k, ss, ms, rs):
                    pool.wait_ge(s[f"ss{k}_ok"], upto(t))
                    pool.tensor_tensor(ms[:], ss[:], c.eps[:, 0:1], ALU.add).then_inc(s[f"ms{k}_ok"], 1)
                    pool.wait_ge(s[f"ms{k}_ok"], upto(t))
                    pool.tensor_tensor(rs[:], ms[:], c.half[:, 0:1], ALU.pow).then_inc(s[f"rs{k}_ok"], 1)

                def step(t, u, pair, a, b, d):
                    if a:
                        rsqrt(t, 3, ss3, ms3, rs3)
                    if b:
                        rsqrt(t - 1, 4, ss4, ms4, rs4)

                steps(pool, step)

            @block.scalar
            def _(act):
                for n in ("oT_act", "exp_ok", "ss3_ok", "pT_act", "hT4_act", "ss4_ok", "hT3_act"):
                    act.sem_inc(s[n], 1)

                def high(t, name, turned, used, dst, src, gain=None):
                    act.wait_ge(s[turned], upto(t))
                    act.wait_ge(s[used], upto(t - 1))
                    if gain is None:
                        act.activation(dst[:, 4:8, :].rearrange("p k n -> p (k n)"), src[:, 1, :],
                                       ACT.Copy).then_inc(s[name], 1)
                    else:
                        for k in range(4):
                            last = act.activation(dst[:, 4 + k, :], src[:, 1, k * P:(k + 1) * P], ACT.Copy,
                                                  scale=gain[:, 4 + k:5 + k])
                        last.then_inc(s[name], 1)

                def step(t, u, pair, a, b, d):
                    if a:
                        high(t, "oT_act", "o_turned", "out_mm", oT, tA)
                    if b:
                        act.wait_ge(s["max_ok"], upto(t - 1))
                        act.wait_ge(s["p_turned"], upto(t - 2))
                        for h in range(HEADS):
                            last = act.activation(pr[:, h, :], sc[:, h // 2, (h % 2) * MEM:(h % 2 + 1) * MEM], ACT.Exp,
                                                  bias=ntop[:, h:h + 1], accum_out=l[:, h:h + 1])
                        last.then_inc(s["exp_ok"], 1)
                    if a:
                        act.wait_ge(s["x2_ok"], upto(t))
                        act.activation(sq[:], x2[u][:], ACT.Square, scale=D ** -0.5, accum_out=ss3[:]).then_inc(s["ss3_ok"], 1)
                    if b:
                        high(t - 1, "pT_act", "p_turned", "co_mm", pT, tB)
                    if d:
                        high(t - 2, "hT4_act", "h4_turned", "r_mm", hT4, tA, c.g_ffn)
                    if b:
                        act.wait_ge(s["x3_ok"], upto(t - 1))
                        act.activation(sq[:], x3t[1 - u][:], ACT.Square, scale=D ** -0.5,
                                       accum_out=ss4[:]).then_inc(s["ss4_ok"], 1)
                    if a:
                        high(t, "hT3_act", "h3_turned", "s_mm", hT3, tB, c.g_cross)

                steps(act, step)

            @block.vector
            def _(dve):
                for n in ("oT_dve", "max_ok", "p_ok", "x2_ok", "xn3_ok", "pT_dve", "hT4_dve", "x3_ok", "xn4_ok", "logits_ok",
                          "hT3_dve"):
                    dve.sem_inc(s[n], 1)
                o = Order(dve, s["dve_step"])

                def low(t, name, turned, used, dst, src, gain=None):
                    dve.wait_ge(s[turned], upto(t))
                    dve.wait_ge(s[used], upto(t - 1))
                    if gain is None:
                        last = dve.tensor_copy(dst[:, 0:4, :], lows(src))
                    else:
                        last = dve.tensor_tensor(dst[:, 0:4, :], lows(src), gain[:, 0:4].unsqueeze(2).to_broadcast([P, 4, P]),
                                                 ALU.mult)
                    last.then_inc(s[name], 1)

                def step(t, u, pair, a, b, d):
                    o.at(2 * (t - 1) if b else 0)
                    if a:
                        low(t, "oT_dve", "o_turned", "out_mm", oT, tA)
                    if b:
                        dve.wait_ge(s["s_mm"], upto(t - 1))
                        o(dve.tensor_reduce(top[:], sc[:].rearrange("p a (b m) -> p (a b) m", m=MEM), AX, ALU.max))
                        dve.tensor_scalar(ntop[:], top[:], -1.0, None, ALU.mult).then_inc(s["max_ok"], 1)
                        dve.wait_ge(s["exp_ok"], upto(t - 1))
                        o(dve.reciprocal(rl[:], l[:]))
                        dve.tensor_tensor(pr[:], pr[:], rl[:].unsqueeze(2).to_broadcast([P, HEADS, MEM]),
                                          ALU.mult).then_inc(s["p_ok"], 1)
                    if a:
                        dve.wait_ge(in_ok[u], 32 * (pair + 1))
                        dve.wait_ge(s["out_mm"], upto(t))
                        dve.tensor_tensor(x2[u][:], acc[:].rearrange("p a n -> p (a n)"), xin[u][:],
                                          ALU.add).then_inc(s["x2_ok"], 1)
                    if b:
                        low(t - 1, "pT_dve", "p_turned", "co_mm", pT, tB)
                    if d:
                        low(t - 2, "hT4_dve", "h4_turned", "r_mm", hT4, tA, c.g_ffn)
                    if a:
                        dve.wait_ge(s["rs3_ok"], upto(t))
                        dve.wait_ge(s["h3_turned"], upto(t - 1))
                        dve.tensor_scalar(xn3[:], x2[u][:], rs3[:, 0:1], None, ALU.mult).then_inc(s["xn3_ok"], 1)
                    if b:
                        dve.wait_ge(s["co_mm"], upto(t - 1))
                        dve.wait_ge(x3_out[1 - u], 16 * (pair + u))
                        dve.tensor_tensor(x3t[1 - u][:], sc[:].rearrange("p a n -> p (a n)"), x2[1 - u][:],
                                          ALU.add).then_inc(s["x3_ok"], 1)
                    if d:
                        dve.wait_ge(s["r_mm"], upto(t - 2))
                        dve.tensor_copy(logits[:, bass.ds(t - 2, 1), :].rearrange("p a n -> p (a n)"),
                                        tA[:, 0, 0:NR]).then_inc(s["logits_ok"], 1)
                    if a:
                        low(t, "hT3_dve", "h3_turned", "s_mm", hT3, tB, c.g_cross)
                    if b:
                        dve.wait_ge(s["rs4_ok"], upto(t - 1))
                        dve.wait_ge(h4_out[1 - u], 16 * (pair + u))
                        dve.tensor_scalar(xn4[1 - u][:], x3t[1 - u][:], rs4[:, 0:1], None, ALU.mult).then_inc(s["xn4_ok"], 1)

                steps(dve, step)

            @block.tensor
            def _(pe):
                for n in ("o_turned", "s_mm", "out_mm", "p_turned", "h4_turned", "co_mm", "r_mm", "h3_turned"):
                    pe.sem_inc(s[n], 1)
                pe.wait_ge(w_ok, 48)

                def turn(name, dst, blocks):
                    for k, blk in enumerate(blocks):
                        last = pe.transpose(dst[:, k // 4, (k % 4) * P:(k % 4 + 1) * P], blk, c.ident[:])
                    last.then_inc(s[name], 1)

                def cut(tile):
                    return [tile[:, k * P:(k + 1) * P] for k in range(KC)]

                def product(name, dst, left, right):
                    for half in range(2):
                        for k in range(KC):
                            last = pe.matmul(dst[:, half, :], left[:, k, :], right[:, k, half * H:(half + 1) * H],
                                             start=(k == 0), stop=(k == KC - 1))
                    last.then_inc(s[name], 1)

                def step(t, u, pair, a, b, d):
                    if a:
                        pe.wait_ge(in_ok[u], 32 * (pair + 1))
                        pe.wait_ge(s["logits_ok"], upto(t - 3) if d else 1)
                        pe.wait_ge(s["oT_act"], upto(t - 1))
                        pe.wait_ge(s["oT_dve"], upto(t - 1))
                        turn("o_turned", tA, cut(mixin[u]))
                    if b:
                        pe.wait_ge(s["hT3_dve"], upto(t - 1))
                        pe.wait_ge(s["hT3_act"], upto(t - 1))
                        pe.wait_ge(s["x3_ok"], upto(t - 2))
                        product("s_mm", sc, hT3, wqk)
                    if a:
                        pe.wait_ge(s["oT_dve"], upto(t))
                        pe.wait_ge(s["oT_act"], upto(t))
                        pe.wait_ge(s["x2_ok"], upto(t - 1))
                        product("out_mm", acc, oT, wo)
                    if b:
                        pe.wait_ge(s["p_ok"], upto(t - 1))
                        pe.wait_ge(s["hT3_dve"], upto(t - 1))
                        pe.wait_ge(s["hT3_act"], upto(t - 1))
                        turn("p_turned", tB, cut(pr[:].rearrange("p h m -> p (h m)")))
                    if d:
                        pe.wait_ge(s["xn4_ok"], upto(t - 2))
                        if a:
                            pe.wait_ge(s["oT_dve"], upto(t))
                            pe.wait_ge(s["oT_act"], upto(t))
                        turn("h4_turned", tA, cut(xn4[u]))
                    if b:
                        pe.wait_ge(s["pT_dve"], upto(t - 1))
                        pe.wait_ge(s["pT_act"], upto(t - 1))
                        pe.wait_ge(s["exp_ok"], upto(t - 1))
                        product("co_mm", sc, pT, wvo)
                    if d:
                        pe.wait_ge(s["hT4_dve"], upto(t - 2))
                        pe.wait_ge(s["hT4_act"], upto(t - 2))
                        for k in range(KC):
                            last = pe.matmul(tA[:, 0, 0:NR], hT4[:, k, :], wr[:, k, :], start=(k == 0), stop=(k == KC - 1))
                        last.then_inc(s["r_mm"], 1)
                    if a:
                        pe.wait_ge(s["xn3_ok"], upto(t))
                        if b:
                            pe.wait_ge(s["pT_dve"], upto(t - 1))
                            pe.wait_ge(s["pT_act"], upto(t - 1))
                        turn("h3_turned", tB, cut(xn3))

                steps(pe, step)


def route_phase(nc, c, b_rg, b_re, logits, dest, gate, rows, table):
    NR = GROUPS + EXPERTS
    ROUND = 8
    with ExitStack() as ctx:
        sb, ps, sem = alloc(nc, ctx, "route")
        bias = sb("bias", [P, NR])
        lg = sb("lg", [P, NT, NR])
        rank = sb("rank", [P, PER_GROUP])
        thr, blk_id, row_id, keep, one = (sb("thr", [P, NT]), sb("blk_id", [P, NBLK]), sb("row_id", [P, P]),
                                          sb("keep", [P, EXPERTS, NT]), sb("one", [P, P]))
        before, token = sb("before", [P, P]), sb("token", [P, NT])
        t1 = [sb(f"t1_{n}", [P, NT]) for n in range(3)]
        t4 = [sb(f"t4_{n}", [P, NT, 4]) for n in range(4)]
        og, oe = sb("og", [P, NT, GROUPS]), sb("oe", [P, 2, NT, PER_GROUP])
        pg, e2, half_gate = sb("pg", [P, NT]), sb("e2", [P, NT]), sb("half_gate", [P, NT])
        t16 = sb("t16", [P, NT, GROUPS, PER_GROUP])
        pick = sb("pick", [P, 2, NT, EXPERTS])
        both = sb("both", [P, NT, EXPERTS])
        tot, cum, offs = (sb(n, [P, EXPERTS, NT]) for n in ("tot", "cum", "offs"))
        counts, nblk, endb, startr = (sb(n, [P, EXPERTS]) for n in ("counts", "nblk", "endb", "startr"))
        wide = sb("wide", [P, NBLK, EXPERTS])
        eb = sb("eb", [P, NBLK])
        place, part, destf = sb("place", [P, NT, EXPERTS]), sb("part", [P, NT, EXPERTS]), sb("destf", [P, NT, 2])
        hi_i, lo_i = sb("hi_i", [P, NT, 2], I32), sb("lo_i", [P, NT, 2], I32)
        hi, lo = sb("hi", [P, NT, 2]), sb("lo", [P, NT, 2])
        low_hot = [sb(f"low_hot{u}", [P, ROUND, P]) for u in range(2)]
        high_hot = sb("high_hot", [P, 2 * NT, NBLK])
        cps, rps = ps("cps", [P, 2, NT * EXPERTS]), ps("rps", [P, NBLK])
        bias_in, set_ok, ask_exp, exp_ok, count_ok, count_mm, hot_ok, hot_used, rows_mm, step_dve, step_pool = (
            sem(n) for n in ("bias_in", "set_ok", "ask_exp", "exp_ok", "count_ok", "count_mm", "hot_ok", "hot_used",
                             "rows_mm", "step_dve", "step_pool"))
        with nc.Block() as block:
            @block.sync
            def _(sp):
                sp.dma_start(bias[:, 0:GROUPS], b_rg.partition_broadcast(P)).then_inc(bias_in, 16)
                sp.dma_start(bias[:, GROUPS:], b_re.partition_broadcast(P)).then_inc(bias_in, 16)

            @block.gpsimd
            def _(pool):
                o = Order(pool, step_pool)
                real = dict(allow_small_or_imprecise_dtypes=True)
                o(pool.iota(rank[:], [[-1, PER_GROUP]], base=PER_GROUP, channel_multiplier=0, **real))
                o(pool.iota(thr[:], [[P, NT]], base=0, channel_multiplier=0, **real))
                o(pool.iota(blk_id[:], [[1, NBLK]], base=0, channel_multiplier=0, **real))
                o(pool.iota(row_id[:], [[1, P]], base=0, channel_multiplier=0, **real))
                o(pool.iota(token[:], [[P, NT]], base=0, channel_multiplier=1, **real))
                o(pool.memset(keep[:], 1.0))
                o(pool.memset(keep[:, :, 0:1], 0.0))
                o(pool.memset(one[:], 1.0))
                o(pool.affine_select(out=before[:], in_=one[:], compare_op=ALU.is_gt, fill=0.0, base=0,
                                     pattern=[[1, P]], channel_multiplier=-1))
                pool.sem_inc(set_ok, 1)

            @block.scalar
            def _(act):
                act.wait_ge(ask_exp, 1)
                act.activation(t4[1][:], t4[0][:], ACT.Exp).then_inc(exp_ok, 1)
                act.wait_ge(ask_exp, 2)
                act.activation(e2[:], t1[2][:], ACT.Exp).then_inc(exp_ok, 1)

            @block.tensor
            def _(pe):
                pe.wait_ge(count_ok, 1)
                flat = both[:].rearrange("p t e -> p (t e)")
                pe.matmul(cps[:, 0, :], before[:], flat, start=True, stop=True)
                pe.matmul(cps[:, 1, :], one[:], flat, start=True, stop=True).then_inc(count_mm, 1)
                for n in range(2 * NT):
                    if n % ROUND == 0:
                        pe.wait_ge(hot_ok, n // ROUND + 1)
                    last = pe.matmul(rps[:], low_hot[n // ROUND % 2][:, n % ROUND, :], high_hot[:, n, :],
                                     start=(n == 0), stop=(n == 2 * NT - 1))
                    if n % ROUND == ROUND - 1:
                        last.then_inc(hot_used, 1)

            @block.vector
            def _(dve):
                o = Order(dve, step_dve)

                def over(x, n):
                    return x.unsqueeze(2).to_broadcast([P, x.shape[1], n])

                def rows_of(x, n):
                    return x.unsqueeze(1).to_broadcast([P, n, x.shape[1]])

                def first_of(out, d, tmp, top):
                    o(dve.tensor_scalar(tmp[:], d[:], 0.0, None, ALU.is_ge))
                    o(dve.tensor_tensor(tmp[:], tmp[:], rows_of(rank[:], NT), ALU.mult))
                    o(dve.tensor_reduce(top[:], tmp[:], AX, ALU.max))
                    o(dve.tensor_tensor(out, tmp[:], over(top[:], 4), ALU.is_equal))

                dve.wait_ge(bias_in, 32)
                dve.wait_ge(set_ok, 1)
                o(dve.tensor_tensor(lg[:], logits[:], rows_of(bias[:], NT), ALU.add))
                o(dve.tensor_reduce(t1[0][:], lg[:, :, 0:GROUPS], AX, ALU.max))
                dve.tensor_tensor(t4[0][:], lg[:, :, 0:GROUPS], over(t1[0][:], GROUPS), ALU.subtract).then_inc(ask_exp, 1)
                dve.wait_ge(ask_exp, 1)
                first_of(og[:], t4[0], t4[2], t1[1])
                dve.wait_ge(exp_ok, 1)
                o(dve.tensor_reduce(t1[0][:], t4[1][:], AX, ALU.add))
                o(dve.reciprocal(pg[:], t1[0][:]))
                for g in range(GROUPS):
                    last = dve.tensor_tensor(t16[:, :, g, :], lg[:, :, GROUPS + g * PER_GROUP:GROUPS + (g + 1) * PER_GROUP],
                                             og[:, :, g:g + 1].to_broadcast([P, NT, PER_GROUP]), ALU.mult)
                o(last)
                o(dve.tensor_reduce(t4[3][:], t16[:].rearrange("p t g j -> p t j g"), AX, ALU.add))
                o(dve.tensor_reduce(t1[0][:], t4[3][:], AX, ALU.max))
                o(dve.tensor_tensor(t4[3][:], t4[3][:], over(t1[0][:], 4), ALU.subtract))
                first_of(oe[:, 0, :, :], t4[3], t4[2], t1[1])
                o(dve.scalar_tensor_tensor(out=t4[3][:], in0=oe[:, 0, :, :], scalar=NEG, in1=t4[3][:], op0=ALU.mult, op1=ALU.add))
                dve.tensor_reduce(t1[2][:], t4[3][:], AX, ALU.max).then_inc(ask_exp, 1)
                dve.wait_ge(ask_exp, 2)
                o(dve.tensor_tensor(t4[3][:], t4[3][:], over(t1[2][:], 4), ALU.subtract))
                first_of(oe[:, 1, :, :], t4[3], t4[2], t1[1])
                dve.wait_ge(exp_ok, 2)
                o(dve.tensor_scalar(t1[0][:], e2[:], 1.0, None, ALU.add))
                o(dve.reciprocal(half_gate[:], t1[0][:]))
                o(dve.tensor_tensor(half_gate[:], half_gate[:], pg[:], ALU.mult))
                dve.tensor_copy(gate[:, :, 0], half_gate[:])
                dve.tensor_tensor(gate[:, :, 1], half_gate[:], e2[:], ALU.mult)
                for k in range(2):
                    for g in range(GROUPS):
                        last = dve.tensor_tensor(pick[:, k, :, g * PER_GROUP:(g + 1) * PER_GROUP], oe[:, k, :, :],
                                                 og[:, :, g:g + 1].to_broadcast([P, NT, PER_GROUP]), ALU.mult)
                o(last)
                dve.tensor_tensor(both[:], pick[:, 0, :, :], pick[:, 1, :, :], ALU.add).then_inc(count_ok, 1)
                dve.wait_ge(count_mm, 1)
                o(dve.tensor_copy(tot[:], cps[:, 1, :].rearrange("p (t e) -> p e t", e=EXPERTS)))
                o(dve.tensor_tensor_scan(cum[:].rearrange("p e t -> p (e t)"), keep[:].rearrange("p e t -> p (e t)"),
                                         tot[:].rearrange("p e t -> p (e t)"), 0.0, ALU.mult, ALU.add))
                dve.tensor_copy(counts[:], cum[:, :, NT - 1])
                o(dve.tensor_tensor(offs[:], cum[:], tot[:], ALU.subtract))
                o(dve.tensor_tensor(tot[:], over(counts[:], NT), rows_of(thr[:], EXPERTS), ALU.is_gt))
                o(dve.tensor_reduce(nblk[:], tot[:], AX, ALU.add))
                o(dve.tensor_tensor_scan(endb[:], one[:, 0:EXPERTS], nblk[:], 0.0, ALU.mult, ALU.add))
                o(dve.tensor_tensor(startr[:], endb[:], nblk[:], ALU.subtract))
                o(dve.tensor_scalar(startr[:], startr[:], float(P), None, ALU.mult))
                o(dve.tensor_tensor(offs[:], offs[:], over(startr[:], NT), ALU.add))
                o(dve.tensor_tensor(place[:], cps[:, 0, :].rearrange("p (t e) -> p t e", e=EXPERTS),
                                    offs[:].rearrange("p e t -> p t e"), ALU.add))
                for k in range(2):
                    o(dve.tensor_tensor(part[:], place[:], pick[:, k, :, :], ALU.mult))
                    o(dve.tensor_reduce(destf[:, :, k:k + 1].rearrange("p t a -> p (t a)"), part[:], AX, ALU.add))
                o(dve.tensor_copy(dest[:], destf[:]))
                o(dve.tensor_scalar(hi_i[:], dest[:], 7, None, ALU.arith_shift_right))
                o(dve.tensor_scalar(lo_i[:], dest[:], P - 1, None, ALU.bitwise_and))
                o(dve.tensor_copy(hi[:], hi_i[:]))
                o(dve.tensor_copy(lo[:], lo_i[:]))
                hi_f, lo_f = (x[:].rearrange("p t k -> p (t k)") for x in (hi, lo))
                o(dve.tensor_tensor(high_hot[:], rows_of(blk_id[:], 2 * NT), over(hi_f, NBLK), ALU.is_equal))
                for k in range(2):
                    last = dve.tensor_tensor(high_hot[:].rearrange("p (t k) b -> p t k b", k=2)[:, :, k, :],
                                             high_hot[:].rearrange("p (t k) b -> p t k b", k=2)[:, :, k, :],
                                             over(token[:], NBLK), ALU.mult)
                o(last)
                for n in range(2 * NT // ROUND):
                    if n >= 2:
                        dve.wait_ge(hot_used, n - 1)
                    dve.tensor_tensor(low_hot[n % 2][:], rows_of(row_id[:], ROUND),
                                      over(lo_f[:, n * ROUND:(n + 1) * ROUND], P), ALU.is_equal).then_inc(hot_ok, 1)
                o(dve.tensor_tensor(wide[:], rows_of(endb[:], NBLK), over(blk_id[:], EXPERTS), ALU.is_le))
                o(dve.tensor_reduce(eb[:], wide[:], AX, ALU.add))
                o(dve.tensor_scalar(eb[:], eb[:], float(EXPERTS - 1), None, ALU.min))
                o(dve.tensor_copy(table[:, 0:NBLK], eb[:]))
                dve.tensor_scalar(table[:, NBLK:2 * NBLK], table[:, 0:NBLK], 1, None, ALU.bitwise_and)
                dve.tensor_copy(table[:, 2 * NBLK:], endb[:])
                dve.wait_ge(hot_used, 2 * NT // ROUND)
                dve.tensor_copy(rows[:], rps[:])


def expert_phase(nc, c, h4, w_gate, w_up, w_down, rows, table, ys):
    GU, DN = KC * DE, (DE // P) * D
    SLOT = 2 * GU + DN
    with ExitStack() as ctx:
        sb, ps, sem = alloc(nc, ctx, "exp")
        w = sb("w", [P, 2 * SLOT])
        xg = [sb(f"xg{u}", [P, D]) for u in range(2)]
        idx = [sb(f"idx{u}", [P, 1], I32) for u in range(2)]
        xT, hT = sb("xT", [P, KC, P]), sb("hT", [P, DE // P, P])
        sg, hid = sb("sg", [P, DE]), sb("hid", [P, DE])
        y = [sb(f"y{u}", [P, D]) for u in range(2)]
        xps, hps, gps, ups, yps = (ps("xps", [P, 2, 512]), ps("hps", [P, DE]), ps("gps", [P, DE]), ps("ups", [P, DE]),
                                   ps("yps", [P, 2, 512]))
        w_dma, w_ready, x_turned, x_low, x_high = (sem(n) for n in ("w_dma", "w_ready", "x_turned", "x_low", "x_high"))
        gu_mm, silu_ok, hid_ok, h_turned, hT_ok, down_mm, y_low, y_high, idx_ok, pool_go = (sem(n) for n in (
            "gu_mm", "silu_ok", "hid_ok", "h_turned", "hT_ok", "down_mm", "y_low", "y_high", "idx_ok", "pool_go"))
        x_in = [sem(f"x_in{u}") for u in range(2)]
        y_out = [sem(f"y_out{u}") for u in range(2)]

        def upto(b):
            return b + 2

        def cut(tile, n):
            return [tile[:, k * P:(k + 1) * P] for k in range(n)]

        with nc.Block() as block:
            @block.sync
            def _(sp):
                def load(e, slot):
                    at = slot * SLOT
                    for k, src in ((0, w_gate), (1, w_up)):
                        sp.dma_start(w[:, at + k * GU:at + (k + 1) * GU].rearrange("p (k n) -> p k n", n=DE),
                                     src[bass.ds(e, 1), :, :].rearrange("a (k p) n -> p (a k) n", p=P)).then_inc(w_dma, 16)
                    sp.dma_start(w[:, at + 2 * GU:at + SLOT].rearrange("p (k n) -> p k n", n=D),
                                 w_down[bass.ds(e, 1), :, :].rearrange("a (k p) n -> p (a k) n", p=P)).then_inc(w_dma, 16)
                    sp.wait_ge(w_dma, 48 * (e + 1))
                    sp.sem_inc(w_ready, 1)

                load(0, 0)
                load(1, 1)
                with sp.Fori(1, EXPERTS // 2) as pair:
                    for u in range(2):
                        e = 2 * pair + u
                        ended = sp.value_load(table[0:1, bass.ds(e - 2 + 2 * NBLK, 1)], min_val=0, max_val=NBLK)
                        sp.wait_ge(down_mm, ended + 1)
                        load(e, u)

            @block.gpsimd
            def _(pool):
                pool.sem_inc(pool_go, 1)

                def gather(b, u, wait=True):
                    if wait:
                        pool.wait_ge(x_turned, upto(b - 2))
                        pool.sem_inc(pool_go, 1)
                    pool.tensor_copy(idx[u][:], rows[:, bass.ds(b, 1)]).then_inc(idx_ok, 1)
                    pool.wait_ge(idx_ok, b + 1)
                    pool.sem_inc(pool_go, 1)
                    pool.indirect_dma_start(out=xg[u][:], out_offset=None, in_=h4[:, :],
                                            in_offset=bass.IndirectOffsetOnAxis(ap=idx[u][:, 0:1], axis=0)).then_inc(x_in[u], 16)

                gather(0, 0, wait=False)
                gather(1, 1, wait=False)
                with pool.Fori(0, NBLK // 2 - 1) as pair:
                    for u in range(2):
                        gather(2 * pair + u + 2, u)

            @block.scalar
            def _(act):
                for n in (x_high, silu_ok, y_high):
                    act.sem_inc(n, 1)

                def rows_in(b):
                    act.wait_ge(x_turned, upto(b))
                    for k in range(4):
                        last = act.activation(xT[:, 4 + k, :], xps[:, 1, k * P:(k + 1) * P], ACT.Copy, scale=c.g_ffn[:, 4 + k:5 + k])
                    last.then_inc(x_high, 1)

                def silu(b):
                    act.wait_ge(gu_mm, upto(b))
                    act.wait_ge(hid_ok, upto(b - 1))
                    act.activation(sg[:], gps[:], ACT.Silu).then_inc(silu_ok, 1)

                def result(b, u, pair):
                    act.wait_ge(down_mm, upto(b))
                    act.wait_ge(y_out[u], 16 * (pair + 1))
                    act.activation(y[u][:, 512:], yps[:, 1, :], ACT.Copy).then_inc(y_high, 1)
                    act.wait_ge(y_high, upto(b))
                    act.wait_ge(y_low, upto(b))
                    act.dma_start(ys[bass.ds(b * P, P), :], y[u][:]).then_inc(y_out[u], 16)

                for out in y_out:
                    act.sem_inc(out, 16)
                rows_in(0)
                silu(0)
                rows_in(1)
                silu(1)
                rows_in(2)
                result(0, 0, 0)
                with act.Fori(1, NBLK // 2 - 1) as pair:
                    for u in range(2):
                        b = 2 * pair + u
                        silu(b)
                        rows_in(b + 1)
                        result(b - 1, 1 - u, pair + u - 1)
                silu(NBLK - 2)
                rows_in(NBLK - 1)
                result(NBLK - 3, 1, NBLK // 2 - 2)
                silu(NBLK - 1)
                result(NBLK - 2, 0, NBLK // 2 - 1)
                result(NBLK - 1, 1, NBLK // 2 - 1)
                for out in y_out:
                    act.wait_ge(out, 16 * (NBLK // 2 + 1))

            @block.vector
            def _(dve):
                for n in (x_low, hid_ok, y_low, hT_ok):
                    dve.sem_inc(n, 1)

                def rows_in(b):
                    dve.wait_ge(x_turned, upto(b))
                    dve.tensor_tensor(xT[:, 0:4, :], xps[:, 0, :].rearrange("p (k n) -> p k n", n=P),
                                      c.g_ffn[:, 0:4].unsqueeze(2).to_broadcast([P, 4, P]), ALU.mult).then_inc(x_low, 1)

                def hidden(b):
                    dve.wait_ge(silu_ok, upto(b))
                    dve.wait_ge(h_turned, upto(b - 1))
                    dve.tensor_tensor(hid[:], sg[:], ups[:], ALU.mult).then_inc(hid_ok, 1)

                def hidden_in(b):
                    dve.wait_ge(h_turned, upto(b))
                    dve.tensor_copy(hT[:].rearrange("p k n -> p (k n)"), hps[:]).then_inc(hT_ok, 1)

                def result(b, u, pair):
                    dve.wait_ge(down_mm, upto(b))
                    dve.wait_ge(y_out[u], 16 * (pair + 1))
                    dve.tensor_copy(y[u][:, 0:512], yps[:, 0, :]).then_inc(y_low, 1)

                rows_in(0)
                hidden(0)
                rows_in(1)
                hidden_in(0)
                hidden(1)
                rows_in(2)
                result(0, 0, 0)
                hidden_in(1)
                with dve.Fori(1, NBLK // 2 - 1) as pair:
                    for u in range(2):
                        b = 2 * pair + u
                        hidden(b)
                        rows_in(b + 1)
                        result(b - 1, 1 - u, pair + u - 1)
                        hidden_in(b)
                hidden(NBLK - 2)
                rows_in(NBLK - 1)
                result(NBLK - 3, 1, NBLK // 2 - 2)
                hidden_in(NBLK - 2)
                hidden(NBLK - 1)
                result(NBLK - 2, 0, NBLK // 2 - 1)
                hidden_in(NBLK - 1)
                result(NBLK - 1, 1, NBLK // 2 - 1)

            @block.tensor
            def _(pe):
                for n in (x_turned, gu_mm, h_turned, down_mm):
                    pe.sem_inc(n, 1)

                def slot_of(b):
                    return pe.value_load(table[0:1, bass.ds(b + NBLK, 1)], min_val=0, max_val=1)

                def rows_turned(b, u, pair):
                    pe.wait_ge(x_in[u], 16 * (pair + 1))
                    pe.wait_ge(x_low, upto(b - 1))
                    pe.wait_ge(x_high, upto(b - 1))
                    for k, blk in enumerate(cut(xg[u], KC)):
                        last = pe.transpose(xps[:, k // 4, (k % 4) * P:(k % 4 + 1) * P], blk, c.ident[:])
                    last.then_inc(x_turned, 1)

                def gate_up(b):
                    expert = pe.value_load(table[0:1, bass.ds(b, 1)], min_val=0, max_val=EXPERTS - 1)
                    at = slot_of(b) * SLOT
                    pe.wait_ge(w_ready, expert + 1)
                    pe.wait_ge(x_low, upto(b))
                    pe.wait_ge(x_high, upto(b))
                    pe.wait_ge(hid_ok, upto(b - 1))
                    for n, dst in ((0, gps), (1, ups)):
                        for k in range(KC):
                            last = pe.matmul(dst[:], xT[:, k, :], w[:, bass.ds(at + n * GU + k * DE, DE)],
                                             start=(k == 0), stop=(k == KC - 1))
                    last.then_inc(gu_mm, 1)

                def hidden_turned(b):
                    pe.wait_ge(hid_ok, upto(b))
                    pe.wait_ge(hT_ok, upto(b - 1))
                    for k, blk in enumerate(cut(hid, DE // P)):
                        last = pe.transpose(hps[:, k * P:(k + 1) * P], blk, c.ident[:])
                    last.then_inc(h_turned, 1)

                def down(b):
                    at = slot_of(b) * SLOT
                    pe.wait_ge(hT_ok, upto(b))
                    pe.wait_ge(y_low, upto(b - 1))
                    pe.wait_ge(y_high, upto(b - 1))
                    for half in range(2):
                        for k in range(DE // P):
                            last = pe.matmul(yps[:, half, :], hT[:, k, :], w[:, bass.ds(at + 2 * GU + k * D + half * 512, 512)],
                                             start=(k == 0), stop=(k == DE // P - 1))
                    last.then_inc(down_mm, 1)

                rows_turned(0, 0, 0)
                gate_up(0)
                rows_turned(1, 1, 0)
                hidden_turned(0)
                gate_up(1)
                rows_turned(2, 0, 1)
                down(0)
                hidden_turned(1)
                with pe.Fori(1, NBLK // 2 - 1) as pair:
                    for u in range(2):
                        b = 2 * pair + u
                        gate_up(b)
                        rows_turned(b + 1, 1 - u, pair + u)
                        down(b - 1)
                        hidden_turned(b)
                gate_up(NBLK - 2)
                rows_turned(NBLK - 1, 1, NBLK // 2 - 1)
                down(NBLK - 3)
                hidden_turned(NBLK - 2)
                gate_up(NBLK - 1)
                down(NBLK - 2)
                hidden_turned(NBLK - 1)
                down(NBLK - 1)


def combine_phase(nc, c, x3, ys, dest, gate, gain, out):
    DEPTH = 4
    with ExitStack() as ctx:
        sb, ps, sem = alloc(nc, ctx, "comb")
        R = range(DEPTH)
        idx = [sb(f"idx{u}", [P, 2], I32) for u in R]
        xin, y0, y1, res = ([sb(f"{n}{u}", [P, D]) for u in R] for n in ("xin", "y0", "y1", "res"))
        gb, sq = sb("gb", [P, D]), sb("sq", [P, D])
        ss, ms, rs = ([sb(f"{n}{u}", [P, 1]) for u in R] for n in ("ss", "ms", "rs"))
        g_in, idx_ok, pool_go, sum_ok, ss_ok, ms_ok, rs_ok, done, part = (sem(n) for n in (
            "g_in", "idx_ok", "pool_go", "sum_ok", "ss_ok", "ms_ok", "rs_ok", "done", "part"))
        x_in, y0_in, y1_in, stored = ([sem(f"{n}{u}") for u in R] for n in ("x_in", "y0_in", "y1_in", "stored"))
        with nc.Block() as block:
            @block.sync
            def _(sp):
                sp.dma_start(gb[:], gain.partition_broadcast(P)).then_inc(g_in, 16)
                with sp.Fori(0, NT // DEPTH) as four:
                    for u in R:
                        t = DEPTH * four + u
                        sp.wait_ge(done, t + 1)
                        sp.dma_start(xin[u][:], x3[bass.ds(t * P, P), :]).then_inc(x_in[u], 16)

            @block.gpsimd
            def _(pool):
                def gather(t, u):
                    pool.wait_ge(done, t + 1)
                    pool.sem_inc(pool_go, 1)
                    pool.tensor_copy(idx[u][:], dest[:, bass.ds(t, 1), :].rearrange("p a k -> p (a k)")).then_inc(idx_ok, 1)
                    pool.wait_ge(idx_ok, t + 1)
                    pool.sem_inc(pool_go, 1)
                    for k, (dst, arrived) in enumerate(((y0, y0_in), (y1, y1_in))):
                        pool.indirect_dma_start(out=dst[u][:], out_offset=None, in_=ys[:, :],
                                                in_offset=bass.IndirectOffsetOnAxis(ap=idx[u][:, k:k + 1], axis=0)
                                                ).then_inc(arrived[u], 16)

                def rsqrt(t, u):
                    pool.wait_ge(ss_ok, t + 1)
                    pool.tensor_tensor(ms[u][:], ss[u][:], c.eps[:, 0:1], ALU.add).then_inc(ms_ok, 1)
                    pool.wait_ge(ms_ok, t + 1)
                    pool.tensor_tensor(rs[u][:], ms[u][:], c.half[:, 0:1], ALU.pow).then_inc(rs_ok, 1)

                for u in R:
                    gather(u, u)
                with pool.Fori(0, NT // DEPTH - 1) as four:
                    for u in R:
                        rsqrt(DEPTH * four + u, u)
                        gather(DEPTH * four + u + DEPTH, u)
                for u in R:
                    rsqrt(NT - DEPTH + u, u)

            @block.scalar
            def _(act):
                for s in stored:
                    act.sem_inc(s, 16)
                with act.Fori(0, NT // DEPTH) as four:
                    for u in R:
                        t = DEPTH * four + u
                        act.wait_ge(sum_ok, t + 1)
                        act.wait_ge(done, t + DEPTH)
                        act.activation(sq[:], res[u][:], ACT.Square, scale=D ** -0.5, accum_out=ss[u][:]).then_inc(ss_ok, 1)
                        act.wait_ge(done, t + DEPTH + 1)
                        act.dma_start(out[bass.ds(t * P, P), :], res[u][:]).then_inc(stored[u], 16)
                for s in stored:
                    act.wait_ge(s, 16 * (NT // DEPTH + 1))

            @block.vector
            def _(dve):
                dve.sem_inc(done, DEPTH)
                dve.wait_ge(g_in, 16)
                with dve.Fori(0, NT // DEPTH) as four:
                    for u in R:
                        t = DEPTH * four + u
                        dve.wait_ge(x_in[u], 16 * (four + 1))
                        dve.wait_ge(y0_in[u], 16 * (four + 1))
                        dve.scalar_tensor_tensor(out=y0[u][:], in0=y0[u][:], scalar=gate[:, bass.ds(t, 1), 0], in1=xin[u][:],
                                                 op0=ALU.mult, op1=ALU.add).then_inc(part, 1)
                        dve.wait_ge(part, t + 1)
                        dve.wait_ge(y1_in[u], 16 * (four + 1))
                        dve.wait_ge(stored[u], 16 * (four + 1))
                        dve.scalar_tensor_tensor(out=res[u][:], in0=y1[u][:], scalar=gate[:, bass.ds(t, 1), 1], in1=y0[u][:],
                                                 op0=ALU.mult, op1=ALU.add).then_inc(sum_ok, 1)
                        dve.wait_ge(rs_ok, t + 1)
                        dve.scalar_tensor_tensor(out=res[u][:], in0=res[u][:], scalar=rs[u][:, 0:1], in1=gb[:],
                                                 op0=ALU.mult, op1=ALU.mult).then_inc(done, 1)


def trunk(nc, x, mem, norm_mix_g, w_in, w_gla_a2, b_gla_a, gla_norm_g, diff_norm_g, lambda_q1, lambda_k1,
          lambda_q2, lambda_k2, w_out, norm_cross_g, norm_mem_g, w_cq, w_ckv, w_co, norm_ffn_g, w_router_grp,
          b_router_grp, w_router_exp, b_router_exp, w_e_gate, w_e_up, w_e_down, norm_final_g, out):
    x = x.rearrange("b s d -> (b s) d")
    mem = mem.rearrange("b s d -> (b s) d")
    out = out.rearrange("b s d -> (b s) d")
    w_in = w_in[0]
    mixed = nc.dram_tensor("mixed", (SEQ, D), F32).ap()
    x3 = nc.dram_tensor("x3", (SEQ, D), F32).ap()
    h4 = nc.dram_tensor("h4", (SEQ, D), F32).ap()
    ys = nc.dram_tensor("ys", (NBLK * P, D), F32).ap()
    with ExitStack() as ctx:
        sb, ps, sem = alloc(nc, ctx, "all")

        class c:
            ident = sb("ident", [P, P])
            identb = sb("identb", [P, P], BF16)
            maskb = sb("maskb", [P, P], BF16)
            half = sb("half", [P, HEADS])
            eps = sb("eps", [P, HEADS])
            g_mix = sb("g_mix", [P, KC])
            g_cross = sb("g_cross", [P, KC])
            g_mem = sb("g_mem", [P, KC])
            g_ffn = sb("g_ffn", [P, KC])
        c.gains = [(c.g_mix[:], norm_mix_g[0].rearrange("(k p) -> p k", p=P)),
                   (c.g_cross[:], norm_cross_g[0].rearrange("(k p) -> p k", p=P)),
                   (c.g_mem[:], norm_mem_g[0].rearrange("(k p) -> p k", p=P)),
                   (c.g_ffn[:], norm_ffn_g[0].rearrange("(k p) -> p k", p=P))]
        constants(nc, c)
        with ExitStack() as mix:
            hT = mix.enter_context(nc.sbuf_tensor("hT", [P, KC, SEQ], F32))
            norm_phase(nc, c, x, hT)
            gla_phase(nc, c, hT, w_in, w_gla_a2[0], b_gla_a[0], gla_norm_g[0], mixed)
            diff_phase(nc, c, hT, w_in, diff_norm_g[0], (lambda_q1[0], lambda_k1[0], lambda_q2[0], lambda_k2[0]), mixed)
        with ExitStack() as cross:
            logits = cross.enter_context(nc.sbuf_tensor("logits", [P, NT, GROUPS + EXPERTS], F32))
            with ExitStack() as fold:
                wqk = fold.enter_context(nc.sbuf_tensor("wqk", [P, KC, D], F32))
                wvo = fold.enter_context(nc.sbuf_tensor("wvo", [P, KC, D], F32))
                memory_phase(nc, c, mem, w_cq[0], w_ckv[0], w_co[0], wqk, wvo)
                cross_phase(nc, c, x, mixed, w_out[0], wqk, wvo, w_router_grp[0], w_router_exp[0], x3, h4, logits)
            dest = cross.enter_context(nc.sbuf_tensor("dest", [P, NT, 2], I32))
            gate = cross.enter_context(nc.sbuf_tensor("gate", [P, NT, 2], F32))
            rows = cross.enter_context(nc.sbuf_tensor("rows", [P, NBLK], I32))
            table = cross.enter_context(nc.sbuf_tensor("table", [P, 2 * NBLK + EXPERTS], I32))
            route_phase(nc, c, b_router_grp[0], b_router_exp[0], logits, dest, gate, rows, table)
            expert_phase(nc, c, h4, w_e_gate[0], w_e_up[0], w_e_down[0], rows, table, ys)
            combine_phase(nc, c, x3, ys, dest, gate, norm_final_g, out)


_INS = ["x", "mem", "norm_mix_g", "w_in", "w_gla_a2", "b_gla_a", "gla_norm_g", "diff_norm_g", "lambda_q1",
        "lambda_k1", "lambda_q2", "lambda_k2", "w_out", "norm_cross_g", "norm_mem_g", "w_cq", "w_ckv", "w_co",
        "norm_ffn_g", "w_router_grp", "b_router_grp", "w_router_exp", "b_router_exp", "w_e_gate", "w_e_up",
        "w_e_down", "norm_final_g"]


def kernel(**inputs):
    import numpy as _np
    import concourse.bacc as _bacc
    from concourse.bass_utils import run_bass_kernel_spmd as _run

    nc = _bacc.Bacc("TRN2", target_bir_lowering=False, num_devices=1)
    arrays, args = {}, []
    for name in _INS:
        a = _np.ascontiguousarray(inputs[name])
        arrays[f"in_{name}"] = a
        args.append(nc.dram_tensor(f"in_{name}", a.shape, mybir.dt.from_np(a.dtype), kind="ExternalInput").ap())
    out = nc.dram_tensor("out", (1, SEQ, D), F32, kind="ExternalOutput").ap()
    trunk(nc, *args, out)
    r = _run(nc, [arrays], core_ids=[0])
    return r.results[0]["out"]
```

```python
from contextlib import ExitStack

import concourse.bass as bass
from concourse import mybir

F32 = mybir.dt.float32
F32R = mybir.dt.float32r
BF16 = mybir.dt.bfloat16
I32 = mybir.dt.int32
U8 = mybir.dt.uint8
ALU = mybir.AluOpType
ACT = mybir.ActivationFunctionType
AX = mybir.AxisListType.X

P = 128
D = 1024
KC = D // P
SEQ = 2048
NT = SEQ // P
HEADS = 4
GLA_DK, DV, CHUNK, RANK = 64, 128, 64, 16
GLA_QK, GLA_V = HEADS * GLA_DK, HEADS * DV
DQK = 64
MEM = 256
DH = D // HEADS
GROUPS, PER_GROUP = 4, 4
EXPERTS = GROUPS * PER_GROUP
DE = 512
NBLK = (2 * SEQ + EXPERTS * (P - 1)) // P
EPS = 1e-6
LAMBDA_INIT = 0.2
NEG = -1e30
CQ, CK = 0, GLA_QK
CV = 2 * GLA_QK
CA = CV + GLA_V
CR = CA + RANK
CDQ = CR + GLA_V
CDK = CDQ + HEADS * 2 * DQK
CDV = CDK + HEADS * 2 * DQK


def alloc(nc, ctx, phase):
    sems = []

    def sb(name, shape, dt=F32):
        return ctx.enter_context(nc.sbuf_tensor(f"{phase}_{name}", shape, dt))

    def ps(name, shape, dt=F32):
        return ctx.enter_context(nc.psum_tensor(f"{phase}_{name}", shape, dt))

    def sem(name):
        sems.append(nc.alloc_semaphore(name=f"{phase}_{name}"))
        return sems[-1]

    def clear():
        if sems:
            nc.clear_and_free_semaphores(sems)
            nc.all_engine_barrier()

    ctx.callback(clear)
    return sb, ps, sem


class Order:

    def __init__(self, eng, sem):
        self.eng, self.sem, self.base, self.n = eng, sem, 0, 0

    def at(self, base):
        self.base, self.n = base, 0

    def __call__(self, ins):
        self.n += 1
        ins.then_inc(self.sem, 1)
        self.eng.wait_ge(self.sem, self.base + self.n)


def constants(nc, c):
    with ExitStack() as ctx:
        _, _, sem = alloc(nc, ctx, "const")
        made, loaded = sem("const_made"), sem("gains_loaded")
        with nc.Block() as block:
            @block.gpsimd
            def _(pool):
                o = Order(pool, made)
                o(pool.memset(c.ident[:], 0.0))
                o(pool.affine_select(out=c.ident[:], in_=c.ident[:], compare_op=ALU.not_equal, fill=1.0,
                                     base=0, pattern=[[-1, P]], channel_multiplier=1))
                o(pool.tensor_copy(c.identb[:], c.ident[:]))
                o(pool.tensor_copy(c.identr[:], c.ident[:]))
                o(pool.memset(c.maskb[:], 0.0))
                o(pool.affine_select(out=c.maskb[:], in_=c.maskb[:], compare_op=ALU.is_ge, fill=NEG,
                                     base=0, pattern=[[-1, P]], channel_multiplier=1))
                o(pool.memset(c.half[:], -0.5))
                o(pool.memset(c.eps[:], EPS))

            @block.sync
            def _(sp):
                n = 0
                for tile, gain in c.gains:
                    with nc.allow_non_contiguous_dma("small column loads"):
                        sp.dma_start(tile, gain).then_inc(loaded, 16)
                    n += 1
                sp.wait_ge(loaded, 16 * n)


def norm_phase(nc, c, x, hT):
    with ExitStack() as ctx:
        sb, ps, sem = alloc(nc, ctx, "norm")
        xin = [sb(f"xin{u}", [P, D]) for u in range(2)]
        xn = [sb(f"xn{u}", [P, D]) for u in range(2)]
        sq = [sb(f"sq{u}", [P, D], BF16) for u in range(2)]
        ss = [sb(f"ss{u}", [P, 1]) for u in range(2)]
        ms = [sb(f"ms{u}", [P, 1]) for u in range(2)]
        rs = [sb(f"rs{u}", [P, 1]) for u in range(2)]
        tp = [[ps(f"tp{u}{k}", [P, 4, P]) for k in range(2)] for u in range(2)]
        x_in = [sem(f"x_in{u}") for u in range(2)]
        x_free, sum_ok, rs_ok, xn_ok = (sem(n) for n in ("x_free", "sum_ok", "rs_ok", "xn_ok"))
        turned, low_out, high_out, ms_ok = (sem(n) for n in ("turned", "low_out", "high_out", "ms_ok"))
        with nc.Block() as block:
            @block.sync
            def _(sp):
                with sp.Fori(0, NT // 2) as pair:
                    for u in range(2):
                        t = 2 * pair + u
                        sp.wait_ge(x_free, t + 1)
                        sp.dma_start(xin[u][:], x[bass.ds(t * P, P), :]).then_inc(x_in[u], 16)

            @block.scalar
            def _(act):
                with act.Fori(0, NT // 2) as pair:
                    for u in range(2):
                        t = 2 * pair + u
                        act.wait_ge(x_in[u], 16 * (pair + 1))
                        act.activation(sq[u][:], xin[u][:], ACT.Square, scale=D ** -0.5,
                                       accum_out=ss[u][:]).then_inc(sum_ok, 1)
                        act.wait_ge(turned, 2 * t + 3)
                        for k in range(4):
                            last = act.activation(hT[:, 4 + k, bass.ds(t * P, P)], tp[u][1][:, k, :], ACT.Copy,
                                                  scale=c.g_mix[:, 4 + k:5 + k])
                        last.then_inc(high_out, 1)

            @block.gpsimd
            def _(pool):
                with pool.Fori(0, NT // 2) as pair:
                    for u in range(2):
                        t = 2 * pair + u
                        pool.wait_ge(sum_ok, t + 1)
                        pool.tensor_tensor(ms[u][:], ss[u][:], c.eps[:, 0:1], ALU.add).then_inc(ms_ok, 1)
                        pool.wait_ge(ms_ok, t + 1)
                        pool.tensor_tensor(rs[u][:], ms[u][:], c.half[:, 0:1], ALU.pow).then_inc(rs_ok, 1)

            @block.vector
            def _(dve):
                dve.sem_inc(x_free, 2)
                with dve.Fori(0, NT // 2) as pair:
                    for u in range(2):
                        t = 2 * pair + u
                        dve.wait_ge(rs_ok, t + 1)
                        dve.wait_ge(turned, 2 * t + 1)
                        dve.tensor_scalar(xn[u][:], xin[u][:], rs[u][:, 0:1], None, ALU.mult).then_inc(xn_ok, 1)
                        dve.wait_ge(xn_ok, t + 1)
                        dve.sem_inc(x_free, 1)
                        dve.wait_ge(turned, 2 * t + 2)
                        dve.tensor_tensor(hT[:, 0:4, bass.ds(t * P, P)], tp[u][0][:],
                                          c.g_mix[:, 0:4].unsqueeze(2).to_broadcast([P, 4, P]), ALU.mult).then_inc(low_out, 1)

            @block.tensor
            def _(pe):
                pe.sem_inc(turned, 1)
                pe.sem_inc(low_out, 2)
                pe.sem_inc(high_out, 2)
                with pe.Fori(0, NT // 2) as pair:
                    for u in range(2):
                        t = 2 * pair + u
                        pe.wait_ge(xn_ok, t + 1)
                        pe.wait_ge(low_out, t + 1)
                        pe.wait_ge(high_out, t + 1)
                        for k in range(KC):
                            last = pe.transpose(tp[u][k // 4][:, k % 4, :], xn[u][:, k * P:(k + 1) * P], c.ident[:])
                            if k % 4 == 3:
                                last.then_inc(turned, 1)


def gate_phase(nc, c, hT, w_in, w_a2, b_a, ep, en, decay):
    N = 512
    with ExitStack() as ctx:
        sb, ps, sem = alloc(nc, ctx, "gate")
        wa, wa2, bcol = sb("wa", [P, KC, RANK]), sb("wa2", [RANK, GLA_QK]), sb("bcol", [P, 2])
        low = sb("low", [RANK, 2, N])
        cum, keep = sb("cum", [P, 2, SEQ]), sb("keep", [P, SEQ])
        lowps, zps = ps("lowps", [RANK, 2, N]), ps("zps", [P, 4, N])
        wa_in, low_mm, low_out, z_mm, z_out = (sem(n) for n in ("wa_in", "low_mm", "low_out", "z_mm", "z_out"))
        keep_ok, mag_ok, soft_ok, sums_ok, exps_ok = (sem(n) for n in ("keep_ok", "mag_ok", "soft_ok", "sums_ok", "exps_ok"))
        dve_step, act_step = sem("dve_step"), sem("act_step")
        z, soft = ep, en
        with nc.Block() as block:
            @block.sync
            def _(sp):
                with nc.allow_non_contiguous_dma("16 columns of w_in; a bias as columns"):
                    sp.dma_start(wa[:], w_in[:, CA:CA + RANK].rearrange("(k p) r -> p k r", p=P)).then_inc(wa_in, 16)
                    sp.dma_start(wa2[:], w_a2).then_inc(wa_in, 16)
                    sp.dma_start(bcol[:], b_a.rearrange("(k p) -> p k", p=P)).then_inc(wa_in, 16)

            @block.gpsimd
            def _(pool):
                pool.memset(keep[:], 1.0).then_inc(keep_ok, 1)
                pool.wait_ge(keep_ok, 1)
                pool.memset(keep[:].rearrange("p (n s) -> p n s", s=CHUNK)[:, :, 0:1], 0.0).then_inc(keep_ok, 1)

            @block.tensor
            def _(pe):
                def gate_input(g):
                    pe.wait_ge(low_out, g + 1)
                    for pair in range(2):
                        last = pe.matmul(zps[:, 2 * (g % 2) + pair, :], wa2[:, pair * P:(pair + 1) * P], low[:, g % 2, :],
                                         start=True, stop=True)
                    last.then_inc(z_mm, 1)

                pe.wait_ge(wa_in, 48)
                for g in range(SEQ // N):
                    if g >= 2:
                        pe.wait_ge(low_out, g - 1)
                    for k in range(KC):
                        last = pe.matmul(lowps[:, g % 2, :], wa[:, k, :], hT[:, k, g * N:(g + 1) * N],
                                         start=(k == 0), stop=(k == KC - 1))
                    last.then_inc(low_mm, 1)
                    if g >= 1:
                        if g >= 3:
                            pe.wait_ge(z_out, g - 2)
                        gate_input(g - 1)
                pe.wait_ge(z_out, 2)
                gate_input(SEQ // N - 1)

            @block.scalar
            def _(act):
                for g in range(SEQ // N):
                    act.wait_ge(low_mm, g + 1)
                    if g >= 2:
                        act.wait_ge(z_mm, g - 1)
                    act.activation(low[:, g % 2, :], lowps[:, g % 2, :], ACT.Copy).then_inc(low_out, 1)
                act.wait_ge(mag_ok, 1)
                act.activation(soft[:], soft[:], ACT.Exp).then_inc(act_step, 1)
                act.wait_ge(act_step, 1)
                act.activation(soft[:], soft[:], ACT.Ln, bias=1.0).then_inc(soft_ok, 1)
                for pair in range(2):
                    act.wait_ge(sums_ok, pair + 1)
                    act.activation(ep[:, pair, :], cum[:, pair, :], ACT.Exp, scale=1.0 / 16.0).then_inc(exps_ok, 1)
                    act.activation(en[:, pair, :], cum[:, pair, :], ACT.Exp, scale=-1.0 / 16.0)

            @block.vector
            def _(dve):
                o = Order(dve, dve_step)
                dve.wait_ge(wa_in, 48)
                for g in range(SEQ // N):
                    dve.wait_ge(z_mm, g + 1)
                    for pair in range(2):
                        last = dve.tensor_scalar(z[:, pair, g * N:(g + 1) * N], zps[:, 2 * (g % 2) + pair, :],
                                                 bcol[:, pair:pair + 1], None, ALU.add)
                    last.then_inc(z_out, 1)
                dve.wait_ge(z_out, SEQ // N)
                o(dve.tensor_scalar(cum[:], z[:], 0.0, None, ALU.min))
                o(dve.tensor_tensor(z[:], cum[:], z[:], ALU.subtract))
                dve.tensor_tensor(soft[:], z[:], cum[:], ALU.add).then_inc(mag_ok, 1)
                dve.wait_ge(soft_ok, 1)
                o(dve.tensor_tensor(z[:], cum[:], soft[:], ALU.subtract))
                dve.wait_ge(keep_ok, 2)
                for pair in range(2):
                    dve.tensor_tensor_scan(cum[:, pair, :], keep[:], z[:, pair, :], 0.0, ALU.mult,
                                           ALU.add).then_inc(sums_ok, 1)
                dve.wait_ge(exps_ok, 2)
                ends = ep[:].rearrange("p a (t n s) -> p a t n s", n=2, s=CHUNK)
                for half in range(2):
                    for chunk in range(2):
                        dve.tensor_copy(decay[chunk * 64:chunk * 64 + 64, half::2, :],
                                        ends[half * 64:half * 64 + 64, :, :, chunk, CHUNK - 1])


def gla_phase(nc, c, hT, w_in, w_a2, b_a, gain, mixed):
    with ExitStack() as outer:
        sb, ps, sem = alloc(nc, outer, "gla")
        ep, en = sb("ep", [P, 2, SEQ]), sb("en", [P, 2, SEQ])
        decay = sb("decay", [P, HEADS, NT])
        gate_phase(nc, c, hT, w_in, w_a2, b_a, ep, en, decay)
        wqk, wvr, gb = sb("w_qk", [P, KC, 2 * GLA_QK]), sb("w_vr", [P, KC, 2 * GLA_V]), sb("gb", [P, DV])
        hs = sb("hs", [P, KC, P])
        qe = [sb(f"qe{u}", [P, 2, P]) for u in range(2)]
        ke = [sb(f"ke{u}", [P, 2, P]) for u in range(2)]
        ks = [sb(f"ks{u}", [P, 2, P]) for u in range(2)]
        q2 = [sb(f"q2{u}", [P, HEADS, P]) for u in range(2)]
        k2 = [sb(f"k2{u}", [P, HEADS, P]) for u in range(2)]
        at = [sb(f"at{u}", [P, 2, 2, P]) for u in range(2)]
        v = [sb(f"v{u}", [P, GLA_V]) for u in range(2)]
        gs = [sb(f"gs{u}", [P, GLA_V]) for u in range(2)]
        st = [sb(f"st{u}", [P, HEADS, DV]) for u in range(2)]
        fin = [sb(f"fin{u}", [P, GLA_V]) for u in range(2)]
        sq, tmp = sb("sq", [P, GLA_V]), sb("tmp", [P, HEADS, DV])
        seen = sb("seen", [P, P], I32)
        ss = [sb(f"ss{u}", [P, HEADS]) for u in range(2)]
        ms = [sb(f"ms{u}", [P, HEADS]) for u in range(2)]
        rs = [sb(f"rs{u}", [P, HEADS]) for u in range(2)]
        qkps, vps, rps = ps("qkps", [P, 4, P]), ps("vps", [P, GLA_V]), ps("rps", [P, GLA_V])
        aps, ktps = ps("aps", [P, 2, 512]), ps("ktps", [P, HEADS, GLA_DK])
        kvps, ops = ps("kvps", [P, HEADS, DV]), ps("ops", [P, HEADS, DV])

        w_in_ok, set_ok, pool_set = sem("w_in_ok"), sem("set_ok"), sem("pool_set")
        staged, pool_go = sem("staged"), sem("pool_go")
        vr_mm, qk_mm = sem("vr_mm"), sem("qk_mm")
        v_out, r_out, gated = sem("v_out"), sem("r_out"), sem("gated")
        qk_out, split_q, split_k = sem("qk_out"), sem("split_q"), sem("split_k")
        scores, turned, masked = sem("scores"), sem("turned"), sem("masked")
        kv_mm, mid_ok, carried = sem("kv_mm"), sem("mid_ok"), sem("carried")
        o_mm, sq_ok, sum_ok, eps_ok, rs_ok = sem("o_mm"), sem("sq_ok"), sem("sum_ok"), sem("eps_ok"), sem("rs_ok")
        o_out, finished, dve_step, dve_go = sem("o_out"), sem("finished"), sem("dve_step"), sem("dve_go")
        stored = [sem(f"stored{u}") for u in range(2)]

        with nc.Block() as block:
            @block.sync
            def _(sp):
                kin = w_in.rearrange("(k p) n -> p k n", p=P)
                sp.dma_start(wvr[:, :, 0:GLA_V], kin[:, :, CV:CV + GLA_V]).then_inc(w_in_ok, 16)
                sp.dma_start(wvr[:, :, GLA_V:], kin[:, :, CR:CR + GLA_V]).then_inc(w_in_ok, 16)
                sp.dma_start(wqk[:], kin[:, :, CQ:CQ + 2 * GLA_QK]).then_inc(w_in_ok, 16)
                sp.dma_start(gb[:], gain.partition_broadcast(P)).then_inc(w_in_ok, 16)

                def store(t, u):
                    sp.wait_ge(finished, t + 2)
                    sp.dma_start(mixed[bass.ds(t * P, P), 0:GLA_V], fin[u][:]).then_inc(stored[u], 16)

                with sp.Fori(0, NT // 2) as pair:
                    for u in range(2):
                        store(2 * pair + u, u)
                for u in range(2):
                    sp.wait_ge(stored[u], 16 * (NT // 2))

            @block.gpsimd
            def _(pool):
                o = Order(pool, pool_set)
                o(pool.memset(seen[:], 1))
                o(pool.affine_select(out=seen[:], in_=seen[:], compare_op=ALU.is_ge, fill=0, base=0,
                                     pattern=[[1, P]], channel_multiplier=-1))
                o(pool.memset(seen[0:CHUNK, CHUNK:], 0))
                for u in range(2):
                    pool.memset(q2[u][:], 0.0)
                    pool.memset(k2[u][:], 0.0)
                    o(pool.memset(at[u][:], 0.0))
                o(pool.memset(st[0][:], 0.0))
                pool.sem_inc(set_ok, 1)
                pool.sem_inc(gated, 1)
                pool.wait_ge(w_in_ok, 64)

                def stage(t):
                    pool.wait_ge(qk_mm, t)
                    pool.sem_inc(pool_go, 1)
                    pool.tensor_copy(hs[:], hT[:, :, bass.ds(t * P, P)]).then_inc(staged, 1)

                def gate(t, u):
                    pool.wait_ge(r_out, t + 2)
                    pool.tensor_tensor(gs[u][:].rearrange("p (h e) -> p h e", e=DV),
                                       gs[u][:].rearrange("p (h e) -> p h e", e=DV),
                                       gb[:].unsqueeze(1).to_broadcast([P, HEADS, DV]), ALU.mult).then_inc(gated, 1)

                def rsqrt(t, u):
                    pool.wait_ge(sum_ok, t + 1)
                    pool.tensor_tensor(ms[u][:], ss[u][:], c.eps[:], ALU.add).then_inc(eps_ok, 1)
                    pool.wait_ge(eps_ok, t + 1)
                    pool.tensor_tensor(rs[u][:], ms[u][:], c.half[:], ALU.pow).then_inc(rs_ok, 1)

                pool.tensor_copy(hs[:], hT[:, :, 0:P]).then_inc(staged, 1)
                gate(0, 0)
                stage(1)
                with pool.Fori(0, NT // 2 - 1) as pair:
                    for u in range(2):
                        t = 2 * pair + u
                        gate(t + 1, 1 - u)
                        stage(t + 2)
                        rsqrt(t, u)
                gate(NT - 1, 1)
                rsqrt(NT - 2, 0)
                rsqrt(NT - 1, 1)

            @block.scalar
            def _(act):
                act.sem_inc(v_out, 1)
                act.sem_inc(r_out, 1)
                act.wait_ge(set_ok, 1)

                def values(t, u):
                    act.wait_ge(vr_mm, t + 1)
                    act.activation(v[u][:], vps[:], ACT.Copy).then_inc(v_out, 1)
                    act.activation(gs[u][:], rps[:], ACT.Silu).then_inc(r_out, 1)

                def split(t, u):
                    act.wait_ge(qk_out, t + 2)
                    for half in range(2):
                        for chunk in range(2):
                            cols = slice(chunk * CHUNK, (chunk + 1) * CHUNK)
                            last = act.activation(q2[u][chunk * 64:chunk * 64 + 64, half::2, cols],
                                                  qe[u][half * 64:half * 64 + 64, :, cols], ACT.Copy)
                    last.then_inc(split_q, 1)

                def square(t):
                    act.wait_ge(o_mm, t + 1)
                    act.wait_ge(finished, t + 1)
                    act.activation(sq[:], ops[:].rearrange("p h e -> p (h e)"), ACT.Square,
                                   scale=DV ** -0.5).then_inc(sq_ok, 1)

                values(0, 0)
                split(0, 0)
                with act.Fori(0, NT // 2 - 1) as pair:
                    for u in range(2):
                        t = 2 * pair + u
                        act.wait_ge(finished, t + 1)
                        values(t + 1, 1 - u)
                        split(t + 1, 1 - u)
                        square(t)
                act.wait_ge(finished, NT - 1)
                values(NT - 1, 1)
                split(NT - 1, 1)
                square(NT - 2)
                square(NT - 1)

            @block.vector
            def _(dve):
                for s in (masked, split_k, carried, qk_out, o_out, finished):
                    dve.sem_inc(s, 1)
                dve.wait_ge(set_ok, 1)
                o = Order(dve, dve_step)

                def project_out(t, u):
                    dve.wait_ge(qk_mm, t + 1)
                    here = bass.ds(t * P, P)
                    dve.scalar_tensor_tensor(out=qe[u][:], in0=qkps[:, 0:2, :], scalar=GLA_DK ** -0.5,
                                             in1=ep[:, :, here], op0=ALU.mult, op1=ALU.mult)
                    o(dve.tensor_tensor(ke[u][:], qkps[:, 2:4, :], en[:, :, here], ALU.mult))
                    for pair in range(2):
                        ends = ep[:, pair, here].rearrange("p (n s) -> p n s", s=CHUNK)[:, :, CHUNK - 1:CHUNK]
                        last = dve.tensor_tensor(ks[u][:, pair, :].rearrange("p (n s) -> p n s", s=CHUNK),
                                                 ke[u][:, pair, :].rearrange("p (n s) -> p n s", s=CHUNK),
                                                 ends.to_broadcast([P, 2, CHUNK]), ALU.mult)
                    last.then_inc(qk_out, 1)

                def chunk_work(t, u):
                    dve.wait_ge(scores, t + 1)
                    dve.sem_inc(dve_go, 1)
                    dve.copy_predicated(at[u][:].rearrange("p a b q -> p (a b) q"),
                                        seen[:].unsqueeze(1).to_broadcast([P, 4, P]),
                                        aps_view).then_inc(masked, 1)
                    dve.wait_ge(turned, t + 1)
                    dve.tensor_copy(k2[u][0:CHUNK, :, 0:64], ktps[0:CHUNK, :, :])
                    dve.tensor_copy(k2[u][CHUNK:P, :, 64:P], ktps[CHUNK:P, :, :]).then_inc(split_k, 1)

                def decayed(lo, t, u):
                    return dve.tensor_tensor(tmp[lo:lo + 64, :, :], st[u][lo:lo + 64, :, :],
                                             decay_now(t)[lo:lo + 64].to_broadcast([64, HEADS, DV]), ALU.mult)

                def decay_now(t):
                    return decay[:, :, bass.ds(t, 1)]

                def middle(t, u):
                    dve.wait_ge(kv_mm, t + 1)
                    o(decayed(0, t, u))
                    dve.tensor_tensor(st[u][64:P, :, :], tmp[0:64, :, :], kvps[0:64, :, :], ALU.add).then_inc(mid_ok, 1)

                def carry(t, u):
                    dve.wait_ge(mid_ok, t + 1)
                    o(decayed(64, t, u))
                    dve.tensor_tensor(st[1 - u][0:64, :, :], tmp[64:P, :, :], kvps[64:P, :, :], ALU.add).then_inc(carried, 1)
                    dve.wait_ge(carried, t + 2)

                def finish(t, u, pair):
                    dve.wait_ge(sq_ok, t + 1)
                    dve.tensor_reduce(ss[u][:], sq[:].rearrange("p (h e) -> p h e", e=DV), AX, ALU.add).then_inc(sum_ok, 1)
                    dve.wait_ge(rs_ok, t + 1)
                    dve.wait_ge(gated, t + 2)
                    if pair is not None:
                        dve.wait_ge(stored[u], 16 * pair)
                    dve.tensor_tensor(fin[u][:].rearrange("p (h e) -> p h e", e=DV), ops[:],
                                      rs[u][:].unsqueeze(2).to_broadcast([P, HEADS, DV]), ALU.mult).then_inc(o_out, 1)
                    dve.wait_ge(o_out, t + 2)
                    dve.tensor_tensor(fin[u][:], fin[u][:], gs[u][:], ALU.mult).then_inc(finished, 1)

                aps_view = aps[:, :, 0:2 * P].rearrange("p a (b q) -> p a b q", b=2)

                def step(t, u, pair, last=False):
                    chunk_work(t, u)
                    middle(t, u)
                    if not last:
                        project_out(t + 1, 1 - u)
                    carry(t, u)
                    finish(t, u, pair)

                project_out(0, 0)
                step(0, 0, None)
                step(1, 1, None)
                with dve.Fori(1, NT // 2 - 1) as pair:
                    for u in range(2):
                        o.at(1 + 3 * (2 * pair + u))
                        step(2 * pair + u, u, pair)
                o.at(1 + 3 * (NT - 2))
                step(NT - 2, 0, NT // 2 - 1)
                step(NT - 1, 1, NT // 2 - 1, last=True)

            @block.tensor
            def _(pe):
                def values(t):
                    pe.wait_ge(staged, t + 1)
                    pe.wait_ge(v_out, t + 1)
                    pe.wait_ge(r_out, t + 1)
                    for k in range(KC):
                        pe.matmul(vps[:], hs[:, k, :], wvr[:, k, 0:GLA_V], start=(k == 0), stop=(k == KC - 1))
                    for k in range(KC):
                        last = pe.matmul(rps[:], hs[:, k, :], wvr[:, k, GLA_V:], start=(k == 0), stop=(k == KC - 1))
                    last.then_inc(vr_mm, 1)

                def queries(t):
                    pe.wait_ge(qk_out, t + 1)
                    for m in range(4):
                        for k in range(KC):
                            last = pe.matmul(qkps[:, m, :], wqk[:, k, m * P:(m + 1) * P], hs[:, k, :],
                                             start=(k == 0), stop=(k == KC - 1))
                    last.then_inc(qk_mm, 1)

                def score(t, u):
                    pe.wait_ge(qk_out, t + 2)
                    pe.wait_ge(masked, t + 1)
                    for half in range(2):
                        rows = slice(half * 64, half * 64 + 64)
                        for pair in range(2):
                            last = pe.matmul(aps[:, half, pair * P:(pair + 1) * P], ke[u][rows, pair, :],
                                             qe[u][rows, pair, :], start=True, stop=True)
                    last.then_inc(scores, 1)
                    pe.wait_ge(split_k, t + 1)
                    for pair in range(2):
                        last = pe.transpose(ktps[:, 2 * pair:2 * pair + 2, :].rearrange("p h d -> p (h d)"), ks[u][:, pair, :],
                                            c.ident[:])
                    last.then_inc(turned, 1)

                def outer_products(t, u):
                    pe.wait_ge(split_k, t + 2)
                    pe.wait_ge(v_out, t + 2)
                    pe.wait_ge(carried, t + 1)
                    for h in range(HEADS):
                        last = pe.matmul(kvps[:, h, :], k2[u][:, h, :], v[u][:, h * DV:(h + 1) * DV], start=True, stop=True)
                    last.then_inc(kv_mm, 1)

                def outputs(t, u):
                    pe.wait_ge(masked, t + 2)
                    pe.wait_ge(split_q, t + 1)
                    pe.wait_ge(mid_ok, t + 1)
                    pe.wait_ge(o_out, t + 1)
                    for h in range(HEADS):
                        pe.matmul(ops[:, h, :], at[u][:, h % 2, h // 2, :], v[u][:, h * DV:(h + 1) * DV],
                                  start=True, stop=False)
                        last = pe.matmul(ops[:, h, :], q2[u][:, h, :], st[u][:, h, :], start=False, stop=True)
                    last.then_inc(o_mm, 1)

                def step(t, u, last=False):
                    score(t, u)
                    if not last:
                        values(t + 1)
                    outer_products(t, u)
                    if not last:
                        queries(t + 1)
                    outputs(t, u)

                pe.wait_ge(set_ok, 1)
                pe.wait_ge(w_in_ok, 64)
                values(0)
                queries(0)
                with pe.Fori(0, NT // 2 - 1) as pair:
                    for u in range(2):
                        step(2 * pair + u, u)
                step(NT - 2, 0)
                step(NT - 1, 1, last=True)


def diff_phase(nc, c, hT, w_in, gain, lambdas, mixed):
    W = 512
    BANKS = 4

    def chunks(i):
        return (i * P + P + W - 1) // W

    def first(i):
        return sum(chunks(j) for j in range(i))

    def scaled_first(i):
        return sum(chunks(j) for j in range(i) if chunks(j) > 1)

    def steps(i):
        score = [("S", m, k) for m in range(2) for k in range(chunks(i))] if i < NT else []
        turns = chunks(i - 1) if i >= 1 else 0
        n, out, j = len(score), [], 0
        for x in range(n + 1):
            while j < turns and x >= min(n, 3 + -(-j * (n - 3) // turns)):
                out.append(("T", j))
                j += 1
            if x < n:
                out.append(score[x])
        return out

    def width(i, k):
        return min(W, (i + 1) * P - k * W)

    ALL = first(NT)
    assert (2 * ALL) % BANKS == 0 and ALL % 4 == 0
    SCALED = scaled_first(NT)
    MANY = sum(chunks(i) > 1 for i in range(NT))
    jobs = [(w, g) for g in range(4) for w in "qk"] + [("v", g) for g in range(4)]
    QK = 8
    hi_rows = [slice(0, 64), slice(64, 128)]
    lo_rows = [slice(64, 128), slice(0, 64)]

    with ExitStack() as ctx:
        sb, ps, sem = alloc(nc, ctx, "diff")
        wd = sb("wd", [P, KC, 3, P])
        qa = [sb(f"qa{m}", [P, SEQ], F32R) for m in range(2)]
        ka = [sb(f"ka{m}", [P, SEQ], F32R) for m in range(2)]
        qb = [sb(f"qb{m}", [P, SEQ], F32R) for m in range(2)]
        kb = [sb(f"kb{m}", [P, SEQ], F32R) for m in range(2)]
        v = sb("v", [P, NT, DV])
        pr = [[sb(f"pr{u}{m}", [P, SEQ]) for m in range(2)] for u in range(2)]
        aT = sb("aT", [P, 4, 4, P])
        qmul, kmul = sb("qmul", [P, 1]), sb("kmul", [P, 1])
        lam, lsum, lexp, neglam = sb("lam", [P, 4, DQK]), sb("lsum", [P, 2]), sb("lexp", [P, 2]), sb("neglam", [P, 1])
        lprod, ldif = sb("lprod", [P, DQK]), sb("ldif", [P, 1])
        gd, gdb, part = sb("gd", [P, DV]), sb("gdb", [P, DV]), sb("part", [P, 1])
        nmx = [sb(f"nmx{u}", [P, 2, 4]) for u in range(2)]
        ntop = [sb(f"ntop{u}", [P, 2]) for u in range(2)]
        ls = [sb(f"ls{u}", [P, 2, 4]) for u in range(2)]
        e = [sb(f"e{u}", [P, 2, 4]) for u in range(2)]
        le, w1 = sb("le", [P, 2, 4]), sb("w1", [P, 4])
        l = [sb(f"l{u}", [P, 2]) for u in range(2)]
        r = [sb(f"r{u}", [P, 2]) for u in range(2)]
        mixw = [sb(f"mixw{u}", [P, 1]) for u in range(2)]
        sq = [sb(f"sq{u}", [P, DV]) for u in range(2)]
        ss = [sb(f"ss{u}", [P, 1]) for u in range(2)]
        f = [[sb(f"f{u}{n}", [P, 1]) for n in range(4)] for u in range(2)]
        fin = [sb(f"fin{u}", [P, DV]) for u in range(2)]
        sps, tps, ops = ps("sps", [P, BANKS, W]), ps("tps", [P, 2, 4, P]), ps("ops", [P, 2, 512])

        small_in, ramps, lam_ok, lexp_ok, set_dve, set_pool = (sem(n) for n in (
            "small_in", "ramps", "lam_ok", "lexp_ok", "set_dve", "set_pool"))
        w_ok = sem("w_ok")
        proj_mm, hi_out, lo_out, alibi_ok = sem("proj_mm"), sem("hi_out"), sem("lo_out"), sem("alibi_ok")
        top_ok, e_ok, scaled = sem("top_ok"), sem("e_ok"), sem("scaled")
        score_mm, max_ok, exp_ok, joined = sem("score_mm"), sem("max_ok"), sem("exp_ok"), sem("joined")
        turned, a_out, pv_mm = sem("turned"), sem("a_out"), sem("pv_mm")
        sq_ok, scale_ok, finished = sem("sq_ok"), sem("scale_ok"), sem("finished")
        dve_step, pool_step = sem("dve_step"), sem("pool_step")
        stored = [sem(f"stored{u}") for u in range(2)]

        def done(h, per, n):
            return h * per + n + 1

        with nc.Block() as block:
            @block.sync
            def _(sp):
                sp.dma_start(gdb[:], gain.partition_broadcast(P)).then_inc(small_in, 16)
                for n, vec in enumerate(lambdas):
                    sp.dma_start(lam[:, n, :], vec.partition_broadcast(P)).then_inc(small_in, 16)
                kin = w_in.rearrange("(k p) n -> p k n", p=P)

                def weights(h):
                    for n, col in enumerate((CDQ, CDK, CDV)):
                        sp.dma_start(wd[:, :, n, :], kin[:, :, bass.ds(h * P + col, P)]).then_inc(w_ok, 16)

                def store(h, i):
                    sp.wait_ge(finished, done(h, NT, i + 1))
                    sp.dma_start(mixed[i * P:(i + 1) * P, bass.ds(h * DV + GLA_V, DV)], fin[i % 2][:]).then_inc(stored[i % 2], 16)

                weights(0)
                with sp.Fori(0, HEADS - 1) as h:
                    sp.wait_ge(proj_mm, done(h, len(jobs), len(jobs)))
                    weights(h + 1)
                    for i in range(NT):
                        store(h, i)
                for i in range(NT):
                    store(HEADS - 1, i)
                for u in range(2):
                    sp.wait_ge(stored[u], 16 * HEADS * NT // 2)

            @block.gpsimd
            def _(pool):
                o = Order(pool, pool_step)
                pool.sem_inc(alibi_ok, 1)
                pool.sem_inc(scale_ok, 1)
                o(pool.memset(part[:], 1.0 / DV))
                two = slice(64, 66)
                ramps_of = [(pr[m][0][two, :], qb[m][two, :], -1, 0) for m in range(2)]
                ramps_of += [(pr[m][1][two, :], kb[m][two, :], 1, 1) for m in range(2)]
                for x, _, sign, _ in ramps_of:
                    o(pool.iota(x, [[sign, SEQ]], base=0, channel_multiplier=0, allow_small_or_imprecise_dtypes=True))
                pool.memset(qmul[two, :], 1.0)
                o(pool.memset(kmul[two, :], 1.0))
                rows = [(x, SEQ, row, 1.0) for x, _, _, row in ramps_of]
                for x, n, row, fill in rows + [(qmul[two, :], 1, 1, 0.25), (kmul[two, :], 1, 0, 0.25)]:
                    o(pool.affine_select(out=x, in_=x, compare_op=ALU.not_equal, fill=fill, base=-row,
                                         pattern=[[0, n]], channel_multiplier=1))
                for x, y, _, _ in ramps_of:
                    o(pool.tensor_copy(y, x))
                START = o.n

                def scale(h, i, u):
                    pool.wait_ge(sq_ok, done(h, NT, i + 1))
                    a, b, d, out = f[u]
                    o(pool.tensor_tensor(a[:], ss[u][:], part[:], ALU.mult))
                    o(pool.tensor_tensor(b[:], a[:], c.eps[:, 0:1], ALU.add))
                    o(pool.tensor_tensor(d[:], b[:], c.half[:, 0:1], ALU.pow))
                    pool.tensor_tensor(out[:], d[:], r[u][:, 0:1], ALU.mult).then_inc(scale_ok, 1)

                with pool.Fori(0, HEADS) as h:
                    o.at(START + h * (3 * NT + 4))
                    pool.wait_ge(proj_mm, done(h, len(jobs), 1))
                    pool.wait_ge(scale_ok, done(h, NT, 0))
                    for m in range(2):
                        o(pool.tensor_tensor(qb[m][two, :], qb[m][two, :].bitcast(F32), qmul[two, :].to_broadcast([2, SEQ]), ALU.mult))
                        o(pool.tensor_tensor(kb[m][two, :], kb[m][two, :].bitcast(F32), kmul[two, :].to_broadcast([2, SEQ]), ALU.mult))
                    pool.sem_inc(alibi_ok, 1)
                    for i in range(NT):
                        scale(h, i, i % 2)

            @block.scalar
            def _(act):
                for s in (hi_out, exp_ok, e_ok, scaled, a_out, sq_ok):
                    act.sem_inc(s, 1)
                act.wait_ge(lam_ok, 1)
                act.activation(lexp[:], lsum[:], ACT.Exp).then_inc(lexp_ok, 1)

                def factors(h, i):
                    u, c = i % 2, chunks(i)
                    act.wait_ge(top_ok, done(h, MANY, i - NT + MANY + 1))
                    act.wait_ge(exp_ok, done(h, 2 * ALL, 2 * first(i + 1)))
                    for m in range(2):
                        last = act.activation(e[u][:, m, 0:c], nmx[u][:, m, 0:c], ACT.Exp, scale=-1.0, bias=ntop[u][:, m:m + 1])
                    last.then_inc(e_ok, 1)
                    act.wait_ge(e_ok, done(h, MANY, i - NT + MANY + 1))

                def scale(h, i, k):
                    u, cols = i % 2, slice(k * W, k * W + width(i, k))
                    act.activation(pr[u][0][:, cols], pr[u][0][:, cols], ACT.Copy, scale=e[u][:, 0, k:k + 1]).then_inc(scaled, 1)

                def exps(h, i, m, k):
                    u, s, w = i % 2, 2 * first(i) + m * chunks(i) + k, width(i, k)
                    act.wait_ge(max_ok, done(h, 2 * ALL, s + 1))
                    if m == k == 0:
                        act.wait_ge(turned, done(h, ALL, first(i - 1) if i >= 2 else 0))
                    act.activation(pr[u][m][:, k * W:k * W + w], sps[:, s % BANKS, 0:w], ACT.Exp,
                                   bias=nmx[u][:, m, k:k + 1], accum_out=ls[u][:, m, k:k + 1]).then_inc(exp_ok, 1)

                def copy(h, i, k):
                    g, n = first(i) + k, width(i, k) // P
                    act.wait_ge(turned, done(h, ALL, g + 1))
                    act.wait_ge(pv_mm, done(h, ALL, max(g - 3, 0)))
                    act.activation(aT[:, g % 4, 0:n, :], tps[:, g % 2, 0:n, :], ACT.Copy).then_inc(a_out, 1)

                def square(h, i):
                    u = i % 2
                    act.wait_ge(pv_mm, done(h, ALL, first(i + 1)))
                    act.wait_ge(finished, done(h, NT, max(i - 1, 0)))
                    act.activation(sq[u][:], ops[:, i % 2, 0:DV], ACT.Square, scale=r[u][:, 0:1],
                                   accum_out=ss[u][:]).then_inc(sq_ok, 1)

                with act.Fori(0, HEADS) as h:
                    for j, (what, g) in enumerate(jobs):
                        act.wait_ge(proj_mm, done(h, len(jobs), j + 1))
                        bank, cols = sps[:, j % BANKS, :], slice(g * W, (g + 1) * W)
                        if what == "v":
                            last = act.activation(v[:, 4 * g:4 * g + 4, :].rearrange("p t d -> p (t d)"), bank, ACT.Copy)
                        else:
                            by = DQK ** -0.5 if what == "q" else 1.0
                            for m in range(2):
                                part_of = bank[m * 64:m * 64 + 64, :]
                                a = (qa if what == "q" else ka)[m]
                                act.activation(a[hi_rows[m], cols], part_of, ACT.Copy, scale=by)
                                twin = qb[m][0:DQK, cols] if what == "q" else a[lo_rows[m], cols]
                                last = act.activation(twin, part_of, ACT.Copy, scale=by)
                        last.then_inc(hi_out, 1)
                    for i in range(NT + 1):
                        n = 0
                        many = 1 <= i <= NT and chunks(i - 1) > 1
                        if many:
                            factors(h, i - 1)
                        for what, *where in steps(i):
                            if many and n < chunks(i - 1) and (what == "S" or where[0] == n):
                                scale(h, i - 1, n)
                                n += 1
                            if what == "S":
                                exps(h, i, *where)
                            if many and i == NT and n < chunks(i - 1):
                                scale(h, i - 1, n)
                                n += 1
                            if what == "T":
                                copy(h, i - 1, *where)
                                if i >= 2 and where[0] == 0:
                                    square(h, i - 2)
                    square(h, NT - 1)

            @block.vector
            def _(dve):
                for s in (lo_out, max_ok, top_ok, joined, finished):
                    dve.sem_inc(s, 1)
                o = Order(dve, dve_step)
                dve.wait_ge(small_in, 16 * 5)
                for n in range(2):
                    o(dve.tensor_tensor_reduce(lprod[:], lam[:, 2 * n, :], lam[:, 2 * n + 1, :], 1.0, 0.0, ALU.mult, ALU.add,
                                               lsum[:, n:n + 1]))
                dve.sem_inc(lam_ok, 1)
                dve.wait_ge(lexp_ok, 1)
                o(dve.tensor_tensor(ldif[:], lexp[:, 1:2], lexp[:, 0:1], ALU.subtract))
                o(dve.tensor_scalar(neglam[:], ldif[:], -LAMBDA_INIT, None, ALU.add))
                o(dve.tensor_scalar(gd[:], gdb[:], 1.0 - LAMBDA_INIT, None, ALU.mult))
                START = o.n

                def maximum(h, i, m, k):
                    s = 2 * first(i) + m * chunks(i) + k
                    dve.wait_ge(score_mm, done(h, 2 * ALL, s + 1))
                    dve.tensor_reduce(nmx[i % 2][:, m, k:k + 1], sps[:, s % BANKS, 0:width(i, k)], AX, ALU.max,
                                      negate=True).then_inc(max_ok, 1)

                def row_maxima(h, i):
                    dve.wait_ge(max_ok, done(h, 2 * ALL, 2 * first(i + 1)))
                    dve.tensor_reduce(ntop[i % 2][:], nmx[i % 2][:, :, 0:chunks(i)], AX, ALU.min).then_inc(top_ok, 1)

                def weights(h, i):
                    u, c = i % 2, chunks(i)
                    dve.wait_ge(exp_ok, done(h, 2 * ALL, 2 * first(i + 1)))
                    if c > 1:
                        dve.wait_ge(e_ok, done(h, MANY, i - NT + MANY + 1))
                        o(dve.tensor_tensor(le[:, :, 0:c], ls[u][:, :, 0:c], e[u][:, :, 0:c], ALU.mult))
                        o(dve.tensor_reduce(l[u][:], le[:, :, 0:c], AX, ALU.add))
                    else:
                        o(dve.tensor_copy(l[u][:], ls[u][:, :, 0]))
                    o(dve.reciprocal(r[u][:], l[u][:]))
                    o(dve.scalar_tensor_tensor(out=mixw[u][:], in0=l[u][:, 0:1], scalar=neglam[:, 0:1], in1=r[u][:, 1:2],
                                               op0=ALU.mult, op1=ALU.mult))
                    if c > 1:
                        o(dve.tensor_scalar(w1[:, 0:c], e[u][:, 1, 0:c], mixw[u][:, 0:1], None, ALU.mult))

                def join(h, i, k):
                    u, cols = i % 2, slice(k * W, k * W + width(i, k))
                    if chunks(i) > 1:
                        dve.wait_ge(scaled, done(h, SCALED, scaled_first(i) + k + 1))
                        by = w1[:, k:k + 1]
                    else:
                        by = mixw[u][:, 0:1]
                    dve.scalar_tensor_tensor(out=pr[u][0][:, cols], in0=pr[u][1][:, cols], scalar=by,
                                             in1=pr[u][0][:, cols], op0=ALU.mult, op1=ALU.add).then_inc(joined, 1)

                def finish(h, i):
                    u = i % 2
                    dve.wait_ge(scale_ok, done(h, NT, i + 1))
                    if i >= 2:
                        dve.wait_ge(stored[u], 16 * (h * (NT // 2) + i // 2))
                    dve.scalar_tensor_tensor(out=fin[u][:], in0=ops[:, i % 2, 0:DV], scalar=f[u][3][:, 0:1], in1=gd[:],
                                             op0=ALU.mult, op1=ALU.mult).then_inc(finished, 1)

                def head(h):
                    for j, (what, g) in enumerate(jobs[:QK]):
                        dve.wait_ge(hi_out, done(h, len(jobs), j + 1))
                        cols = slice(g * W, (g + 1) * W)
                        for m in range(2):
                            part_of = sps[m * 64:m * 64 + 64, j % BANKS, :]
                            if what == "q":
                                last = dve.scalar_tensor_tensor(out=qa[m][lo_rows[m], cols], in0=part_of, scalar=DQK ** -0.5,
                                                                in1=qa[m][hi_rows[m], cols].bitcast(F32),
                                                                op0=ALU.mult, op1=ALU.subtract)
                            else:
                                last = dve.tensor_tensor(kb[m][0:DQK, cols], part_of, ka[m][hi_rows[m], cols].bitcast(F32),
                                                         ALU.subtract)
                        last.then_inc(lo_out, 1)
                    for i in range(NT + 1):
                        n = 0
                        for what, *where in steps(i):
                            if what == "S":
                                maximum(h, i, *where)
                            for _ in range(1 if i < NT else 2):
                                if i >= 1 and n < chunks(i - 1) and (what == "S" or n <= where[0] + 1):
                                    if n == 0:
                                        if i >= 3:
                                            finish(h, i - 3)
                                        weights(h, i - 1)
                                    join(h, i - 1, n)
                                    n += 1
                        if i < NT and chunks(i) > 1:
                            row_maxima(h, i)
                    for i in (NT - 2, NT - 1):
                        finish(h, i)

                head(0)
                PER = o.n - START
                with dve.Fori(1, HEADS) as h:
                    for u in range(2):
                        dve.wait_ge(stored[u], 16 * (NT // 2) * h)
                    o.at(START + h * PER)
                    head(h)

            @block.tensor
            def _(pe):
                for s in (proj_mm, score_mm, turned, pv_mm):
                    pe.sem_inc(s, 1)

                def project(h):
                    pe.wait_ge(w_ok, 48 * (h + 1))
                    pe.wait_ge(exp_ok, done(h, 2 * ALL, 0))
                    for j, (what, g) in enumerate(jobs):
                        if j >= BANKS:
                            if j - BANKS < QK:
                                pe.wait_ge(lo_out, done(h, QK, j - BANKS + 1))
                            else:
                                pe.wait_ge(hi_out, done(h, len(jobs), j - BANKS + 1))
                        bank = sps[:, j % BANKS, :]
                        if what == "v":
                            for t in range(4):
                                for k in range(KC):
                                    last = pe.matmul(bank[:, t * DV:(t + 1) * DV], hT[:, k, (4 * g + t) * P:(4 * g + t + 1) * P],
                                                     wd[:, k, 2, :], start=(k == 0), stop=(k == KC - 1))
                        else:
                            for k in range(KC):
                                last = pe.matmul(bank, wd[:, k, "qk".index(what), :], hT[:, k, g * W:(g + 1) * W],
                                                 start=(k == 0), stop=(k == KC - 1))
                        last.then_inc(proj_mm, 1)

                def score(h, i, m, k):
                    s = 2 * first(i) + m * chunks(i) + k
                    w = width(i, k)
                    if s >= BANKS:
                        pe.wait_ge(exp_ok, done(h, 2 * ALL, s - BANKS + 1))
                    bank, queries, keys = sps[:, s % BANKS, 0:w], slice(i * P, (i + 1) * P), slice(k * W, k * W + w)
                    diag = k == chunks(i) - 1
                    if diag:
                        pe.matmul(bank[:, w - P:w], c.identb[:], c.maskb[:], start=True, stop=False, skip_group_check=True)
                    pe.matmul(bank, qa[m][:, queries], ka[m][:, keys], start=not diag, stop=False, skip_group_check=diag)
                    pe.matmul(bank, qb[m][0:66, queries], kb[m][0:66, keys], start=False, stop=True,
                              skip_group_check=diag).then_inc(score_mm, 1)

                def turn(h, i, k):
                    g = first(i) + k
                    pe.wait_ge(joined, done(h, ALL, g + 1))
                    pe.wait_ge(a_out, done(h, ALL, max(g - 1, 0)))
                    for b in range(width(i, k) // P):
                        last = pe.transpose(tps[:, g % 2, b, :], pr[i % 2][0][:, k * W + b * P:k * W + (b + 1) * P], c.ident[:])
                    last.then_inc(turned, 1)

                def weigh(h, i, k):
                    g = first(i) + k
                    pe.wait_ge(a_out, done(h, ALL, g + 1))
                    if k == 0:
                        pe.wait_ge(finished, done(h, NT, max(i - 1, 0)))
                    for b in range(width(i, k) // P):
                        t = 4 * k + b
                        last = pe.matmul(ops[:, i % 2, 0:DV], aT[:, g % 4, b, :], v[:, t, :], start=(t == 0), stop=(t == i))
                    last.then_inc(pv_mm, 1)

                with pe.Fori(0, HEADS) as h:
                    project(h)
                    pe.wait_ge(hi_out, done(h, len(jobs), len(jobs)))
                    pe.wait_ge(lo_out, done(h, QK, QK))
                    pe.wait_ge(alibi_ok, done(h, 1, 1))
                    before = None
                    for i in range(NT + 1):
                        for what, *where in steps(i):
                            if what == "S":
                                score(h, i, *where)
                            else:
                                turn(h, i - 1, *where)
                                if before:
                                    weigh(h, *before)
                                before = (i - 1, *where)
                    weigh(h, *before)


def memory_phase(nc, c, mem, w_cq, w_ckv, w_co, wqk, wvo):
    MT = MEM // P
    PER_HEAD = DH // P
    with ExitStack() as ctx:
        sb, ps, sem = alloc(nc, ctx, "fold")
        xin = [sb(f"xin{t}", [P, D]) for t in range(MT)]
        sq = sb("sq", [P, MT, D])
        ss, ms, rs = (sb(n, [P, MT]) for n in ("ss", "ms", "rs"))
        memT = sb("memT", [P, KC, MEM])
        wch = [sb(f"wch{u}", [P, KC, P]) for u in range(2)]
        kvT = sb("kvT", [P, 2 * KC, MEM])
        wqT = [sb(f"wqT{d}", [P, KC, P]) for d in range(2)]
        vT = sb("vT", [P, PER_HEAD, MEM])
        wo = sb("wo", [P, KC, D])
        tps = ps("tps", [P, 2, 4, P])
        kvps = [ps(f"kvps{u}", [P, 512]) for u in range(2)]
        fps = ps("fps", [P, 4, 512])
        mem_in, wo_in = sem("mem_in"), sem("wo_in")
        w_ok = [sem(f"w_ok{u}") for u in range(2)]
        sum_ok, eps_ok, rs_ok, scaled = sem("sum_ok"), sem("eps_ok"), sem("rs_ok"), sem("scaled")
        turned, t_act, t_dve = sem("turned"), sem("t_act"), sem("t_dve")
        kv_mm, kv_out, fold_mm, f_act, f_dve, v_ok = (sem(n) for n in ("kv_mm", "kv_out", "fold_mm", "f_act", "f_dve", "v_ok"))
        kin, qin = (w.rearrange("(k p) n -> p k n", p=P) for w in (w_ckv, w_cq))
        with nc.Block() as block:
            @block.sync
            def _(sp):
                for t in range(MT):
                    sp.dma_start(xin[t][:], mem[t * P:(t + 1) * P, :]).then_inc(mem_in, 16)
                with sp.Fori(0, KC) as pair:
                    for u in range(2):
                        m = 2 * pair + u
                        sp.wait_ge(kv_mm, m + 1)
                        sp.dma_start(wch[u][:], kin[:, :, bass.ds(m * P, P)]).then_inc(w_ok[u], 16)
                for u in range(2):
                    sp.wait_ge(kv_mm, 2 * KC + u + 1)
                    sp.dma_start(wch[u][:], qin[:, :, u * P:(u + 1) * P]).then_inc(w_ok[u], 16)
                with sp.Fori(1, HEADS) as h:
                    for u in range(2):
                        sp.wait_ge(turned, 2 * (2 * h + u + MT) - 2)
                        sp.dma_start(wch[u][:], qin[:, :, bass.ds((2 * h + u) * P, P)]).then_inc(w_ok[u], 16)
                sp.dma_start(wo[:], w_co.rearrange("(k p) n -> p k n", p=P)).then_inc(wo_in, 16)

            @block.gpsimd
            def _(pool):
                pool.wait_ge(sum_ok, MT)
                pool.tensor_tensor(ms[:], ss[:], c.eps[:, 0:MT], ALU.add).then_inc(eps_ok, 1)
                pool.wait_ge(eps_ok, 1)
                pool.tensor_tensor(rs[:], ms[:], c.half[:, 0:MT], ALU.pow).then_inc(rs_ok, 1)

            @block.scalar
            def _(act):
                for s in (t_act, f_act, kv_out):
                    act.sem_inc(s, 1)
                act.wait_ge(mem_in, 16 * MT)
                for t in range(MT):
                    act.activation(sq[:, t, :], xin[t][:], ACT.Square, scale=D ** -0.5,
                                   accum_out=ss[:, t:t + 1]).then_inc(sum_ok, 1)
                for t in range(MT):
                    act.wait_ge(turned, 2 * t + 2)
                    for k in range(4):
                        last = act.activation(memT[:, 4 + k, t * P:(t + 1) * P], tps[:, 1, k, :], ACT.Copy,
                                              scale=c.g_mem[:, 4 + k:5 + k])
                    last.then_inc(t_act, 1)
                with act.Fori(0, KC) as pair:
                    for u in range(2):
                        m = 2 * pair + u
                        act.wait_ge(kv_mm, m + 3)
                        act.activation(kvT[:, bass.ds(m, 1), :].rearrange("p a n -> p (a n)"), kvps[u][:, 0:MEM],
                                       ACT.Copy).then_inc(kv_out, 1)
                with act.Fori(0, HEADS) as h:
                    for d in range(2):
                        act.wait_ge(turned, 2 * (2 * h + d + MT) + 2)
                        act.activation(wqT[d][:, 4:8, :], tps[:, 1, :, :], ACT.Copy).then_inc(t_act, 1)
                    act.wait_ge(fold_mm, h + 1)
                    for b in (2, 3):
                        last = act.activation(wqk[:, 2 * b:2 * b + 2, bass.ds(h * MEM, MEM)],
                                              fps[:, b, :].rearrange("p (r m) -> p r m", m=MEM), ACT.Copy, scale=DH ** -0.5)
                    last.then_inc(f_act, 1)
                with act.Fori(0, HEADS) as h:
                    act.wait_ge(fold_mm, h + HEADS + 1)
                    act.activation(wvo[:, bass.ds(2 * h + 1, 1), :].rearrange("p a n -> p (a n)"),
                                   fps[:, 2:4, :].rearrange("p b n -> p (b n)"), ACT.Copy).then_inc(f_act, 1)

            @block.vector
            def _(dve):
                dve.sem_inc(t_dve, 1)
                dve.sem_inc(f_dve, 1)
                dve.wait_ge(rs_ok, 1)
                for t in range(MT):
                    dve.tensor_scalar(xin[t][:], xin[t][:], rs[:, t:t + 1], None, ALU.mult).then_inc(scaled, 1)
                for t in range(MT):
                    dve.wait_ge(turned, 2 * t + 1)
                    dve.tensor_tensor(memT[:, 0:4, t * P:(t + 1) * P], tps[:, 0, :, :],
                                      c.g_mem[:, 0:4].unsqueeze(2).to_broadcast([P, 4, P]), ALU.mult).then_inc(t_dve, 1)
                with dve.Fori(0, HEADS) as h:
                    for d in range(2):
                        dve.wait_ge(turned, 2 * (2 * h + d + MT) + 1)
                        dve.tensor_copy(wqT[d][:, 0:4, :], tps[:, 0, :, :]).then_inc(t_dve, 1)
                    dve.wait_ge(fold_mm, h + 1)
                    for b in (0, 1):
                        last = dve.tensor_scalar(wqk[:, 2 * b:2 * b + 2, bass.ds(h * MEM, MEM)],
                                                 fps[:, b, :].rearrange("p (r m) -> p r m", m=MEM), DH ** -0.5, None, ALU.mult)
                    last.then_inc(f_dve, 1)
                dve.wait_ge(kv_out, 2 * KC + 1)
                with dve.Fori(0, HEADS) as h:
                    dve.wait_ge(fold_mm, h + HEADS)
                    dve.tensor_copy(vT[:], kvT[:, bass.ds(KC + 2 * h, 2), :]).then_inc(v_ok, 1)
                    dve.wait_ge(fold_mm, h + HEADS + 1)
                    dve.tensor_copy(wvo[:, bass.ds(2 * h, 1), :].rearrange("p a n -> p (a n)"),
                                    fps[:, 0:2, :].rearrange("p b n -> p (b n)")).then_inc(f_dve, 1)

            @block.tensor
            def _(pe):
                pe.sem_inc(kv_mm, 2)

                def turn(blocks, n):
                    pe.wait_ge(t_act, n + 1)
                    pe.wait_ge(t_dve, n + 1)
                    for k, blk in enumerate(blocks):
                        last = pe.transpose(tps[:, k // 4, k % 4, :], blk, c.ident[:])
                        if k % 4 == 3:
                            last.then_inc(turned, 1)

                for t in range(MT):
                    pe.wait_ge(scaled, t + 1)
                    turn([xin[t][:, k * P:(k + 1) * P] for k in range(KC)], t)
                pe.wait_ge(t_act, MT + 1)
                pe.wait_ge(t_dve, MT + 1)
                with pe.Fori(0, KC) as pair:
                    for u in range(2):
                        m = 2 * pair + u
                        pe.wait_ge(w_ok[u], 16 * (pair + 1))
                        if u == 0:
                            pe.wait_ge(kv_out, m + 1)
                        for k in range(KC):
                            last = pe.matmul(kvps[u][:, 0:MEM], wch[u][:, k, :], memT[:, k, :], start=(k == 0), stop=(k == KC - 1))
                        last.then_inc(kv_mm, 1)
                pe.wait_ge(kv_out, 2 * KC + 1)
                with pe.Fori(0, HEADS) as h:
                    for d in range(2):
                        pe.wait_ge(w_ok[d], 16 * (h + KC + 1))
                        turn([wch[d][:, k, :] for k in range(KC)], 2 * h + d + MT)
                    pe.wait_ge(t_act, 2 * h + MT + 3)
                    pe.wait_ge(t_dve, 2 * h + MT + 3)
                    pe.wait_ge(f_act, h + 1)
                    pe.wait_ge(f_dve, h + 1)
                    for row in range(KC):
                        for d in range(2):
                            last = pe.matmul(fps[:, row // 2, (row % 2) * MEM:(row % 2 + 1) * MEM], wqT[d][:, row, :],
                                             kvT[:, bass.ds(2 * h + d, 1), :].rearrange("p a n -> p (a n)"),
                                             start=(d == 0), stop=(d == 1))
                    last.then_inc(fold_mm, 1)
                pe.wait_ge(wo_in, 16)
                with pe.Fori(0, HEADS) as h:
                    pe.wait_ge(v_ok, h + 1)
                    pe.wait_ge(f_act, h + HEADS + 1)
                    pe.wait_ge(f_dve, h + HEADS + 1)
                    for half in range(2):
                        for mt in range(MT):
                            for d in range(2):
                                last = pe.matmul(fps[:, 2 * mt + half, :], vT[:, d, mt * P:(mt + 1) * P],
                                                 wo[:, bass.ds(2 * h + d, 1), half * 512:(half + 1) * 512].rearrange(
                                                     "p a n -> p (a n)"), start=(d == 0), stop=(d == 1))
                    last.then_inc(fold_mm, 1)


def cross_phase(nc, c, x, mixed, w_out, wqk, wvo, w_rg, w_re, g_ffn, x3, h4, logits):
    H = 512
    NR = GROUPS + EXPERTS
    with ExitStack() as ctx:
        sb, ps, sem = alloc(nc, ctx, "cross")
        wo, wr = sb("wo", [P, KC, D]), sb("wr", [P, KC, NR])
        mixin = [sb(f"mixin{u}", [P, D]) for u in range(2)]
        xin = [sb(f"xin{u}", [P, D]) for u in range(2)]
        x2 = [sb(f"x2{u}", [P, D]) for u in range(2)]
        x3t = [sb(f"x3t{u}", [P, D]) for u in range(2)]
        xn4 = sb("xn4", [P, D])
        xp4 = [sb(f"xp4{u}", [P, 2, D], F32R) for u in range(2)]
        gb = sb("gb", [P, D])
        oT, hT3, pT, hT4 = (sb(n, [P, KC, P]) for n in ("oT", "hT3", "pT", "hT4"))
        xn3, pr, sq = sb("xn3", [P, D]), sb("pr", [P, HEADS, MEM]), sb("sq", [P, D])
        top, ntop, l, rl = (sb(n, [P, HEADS]) for n in ("top", "ntop", "l", "rl"))
        ss3, ms3, rs3, ss4, ms4, rs4 = (sb(n, [P, 1]) for n in ("ss3", "ms3", "rs3", "ss4", "ms4", "rs4"))
        tA, tB, acc, sc = (ps(n, [P, 2, H]) for n in ("tA", "tB", "acc", "sc"))
        w_ok = sem("w_ok")
        in_ok = [sem(f"in_ok{u}") for u in range(2)]
        names = ("o_turned oT_dve oT_act s_mm max_ok exp_ok p_ok out_mm x2_ok ss3_ok ms3_ok rs3_ok xn3_ok p_turned pT_dve "
                 "pT_act h4_turned hT4_dve hT4_act co_mm x3_ok ss4_ok ms4_ok rs4_ok xf_ok xh_ok xn4_ok r_mm logits_ok h3_turned "
                 "hT3_dve hT3_act dve_step").split()
        s = {n: sem(n) for n in names}
        x3_out = [sem(f"x3_out{u}") for u in range(2)]
        h4_out = [sem(f"h4_out{u}") for u in range(2)]

        def upto(t):
            return t + 2

        def steps(eng, step):
            step(0, 0, 0, True, False, False)
            step(1, 1, 0, True, True, False)
            with eng.Fori(1, NT // 2) as pair:
                for u in range(2):
                    step(2 * pair + u, u, pair, True, True, True)
            step(NT, 0, NT // 2, False, True, True)
            step(NT + 1, 1, NT // 2, False, False, True)

        def lows(tile):
            return tile[:, 0, :].rearrange("p (k n) -> p k n", n=P)

        with nc.Block() as block:
            @block.sync
            def _(sp):
                sp.dma_start(gb[:], g_ffn.partition_broadcast(P)).then_inc(w_ok, 16)
                sp.dma_start(wo[:], w_out.rearrange("(k p) n -> p k n", p=P)).then_inc(w_ok, 16)
                with nc.allow_non_contiguous_dma("routers' weights: 4 and 16 columns"):
                    sp.dma_start(wr[:, :, 0:GROUPS], w_rg.rearrange("(k p) n -> p k n", p=P)).then_inc(w_ok, 16)
                    sp.dma_start(wr[:, :, GROUPS:], w_re.rearrange("(k p) n -> p k n", p=P)).then_inc(w_ok, 16)

                def load(t, u):
                    rows = bass.ds(t * P, P)
                    sp.dma_start(mixin[u][:], mixed[rows, :]).then_inc(in_ok[u], 16)
                    sp.dma_start(xin[u][:], x[rows, :]).then_inc(in_ok[u], 16)

                def stores(t, u):
                    rows = bass.ds(t * P, P)
                    sp.wait_ge(s["x3_ok"], upto(t))
                    sp.dma_start(x3[rows, :], x3t[u][:]).then_inc(x3_out[u], 16)
                    sp.wait_ge(s["xn4_ok"], upto(t))
                    sp.dma_start(h4[rows, :], xp4[u][:].rearrange("p a n -> p (a n)").bitcast(F32)).then_inc(h4_out[u], 16)

                for out in x3_out + h4_out:
                    sp.sem_inc(out, 16)
                load(0, 0)
                load(1, 1)
                with sp.Fori(0, NT // 2 - 1) as pair:
                    for u in range(2):
                        t = 2 * pair + u
                        sp.wait_ge(s["x2_ok"], upto(t))
                        sp.wait_ge(s["o_turned"], upto(t))
                        load(t + 2, u)
                        stores(t, u)
                stores(NT - 2, 0)
                stores(NT - 1, 1)
                for u in range(2):
                    sp.wait_ge(x3_out[u], 16 * (NT // 2 + 1))
                    sp.wait_ge(h4_out[u], 16 * (NT // 2 + 1))

            @block.gpsimd
            def _(pool):
                for n in ("ms3_ok", "rs3_ok", "ms4_ok", "rs4_ok"):
                    pool.sem_inc(s[n], 1)

                def rsqrt(t, k, ss, ms, rs):
                    pool.wait_ge(s[f"ss{k}_ok"], upto(t))
                    pool.tensor_tensor(ms[:], ss[:], c.eps[:, 0:1], ALU.add).then_inc(s[f"ms{k}_ok"], 1)
                    pool.wait_ge(s[f"ms{k}_ok"], upto(t))
                    pool.tensor_tensor(rs[:], ms[:], c.half[:, 0:1], ALU.pow).then_inc(s[f"rs{k}_ok"], 1)

                def step(t, u, pair, a, b, d):
                    if a:
                        rsqrt(t, 3, ss3, ms3, rs3)
                    if b:
                        rsqrt(t - 1, 4, ss4, ms4, rs4)

                steps(pool, step)

            @block.scalar
            def _(act):
                for n in ("oT_act", "exp_ok", "xh_ok", "ss3_ok", "pT_act", "hT4_act", "ss4_ok", "hT3_act"):
                    act.sem_inc(s[n], 1)

                def high(t, name, turned, used, dst, src, gain=None):
                    act.wait_ge(s[turned], upto(t))
                    act.wait_ge(s[used], upto(t - 1))
                    if gain is None:
                        act.activation(dst[:, 4:8, :].rearrange("p k n -> p (k n)"), src[:, 1, :],
                                       ACT.Copy).then_inc(s[name], 1)
                    else:
                        for k in range(4):
                            last = act.activation(dst[:, 4 + k, :], src[:, 1, k * P:(k + 1) * P], ACT.Copy,
                                                  scale=gain[:, 4 + k:5 + k])
                        last.then_inc(s[name], 1)

                def step(t, u, pair, a, b, d):
                    if a:
                        high(t, "oT_act", "o_turned", "out_mm", oT, tA)
                    if b:
                        act.wait_ge(s["max_ok"], upto(t - 1))
                        act.wait_ge(s["p_turned"], upto(t - 2))
                        for h in range(HEADS):
                            last = act.activation(pr[:, h, :], sc[:, h // 2, (h % 2) * MEM:(h % 2 + 1) * MEM], ACT.Exp,
                                                  bias=ntop[:, h:h + 1], accum_out=l[:, h:h + 1])
                        last.then_inc(s["exp_ok"], 1)
                    if a:
                        act.wait_ge(s["x2_ok"], upto(t))
                        act.activation(sq[:], x2[u][:], ACT.Square, scale=D ** -0.5, accum_out=ss3[:]).then_inc(s["ss3_ok"], 1)
                    if b:
                        high(t - 1, "pT_act", "p_turned", "co_mm", pT, tB)
                    if d:
                        high(t - 2, "hT4_act", "h4_turned", "r_mm", hT4, tA)
                    if b:
                        act.wait_ge(s["x3_ok"], upto(t - 1))
                        act.activation(sq[:], x3t[1 - u][:], ACT.Square, scale=D ** -0.5,
                                       accum_out=ss4[:]).then_inc(s["ss4_ok"], 1)
                    if a:
                        high(t, "hT3_act", "h3_turned", "s_mm", hT3, tB, c.g_cross)
                    if b:
                        act.wait_ge(s["xf_ok"], upto(t - 1))
                        act.activation(xp4[1 - u][:, 0, :], xn4[:], ACT.Copy).then_inc(s["xh_ok"], 1)

                steps(act, step)

            @block.vector
            def _(dve):
                for n in ("oT_dve", "max_ok", "p_ok", "x2_ok", "xn3_ok", "pT_dve", "hT4_dve", "x3_ok", "xn4_ok", "logits_ok",
                          "hT3_dve", "xf_ok"):
                    dve.sem_inc(s[n], 1)
                o = Order(dve, s["dve_step"])
                dve.wait_ge(w_ok, 64)

                def low(t, name, turned, used, dst, src, gain=None):
                    dve.wait_ge(s[turned], upto(t))
                    dve.wait_ge(s[used], upto(t - 1))
                    if gain is None:
                        last = dve.tensor_copy(dst[:, 0:4, :], lows(src))
                    else:
                        last = dve.tensor_tensor(dst[:, 0:4, :], lows(src), gain[:, 0:4].unsqueeze(2).to_broadcast([P, 4, P]),
                                                 ALU.mult)
                    last.then_inc(s[name], 1)

                def step(t, u, pair, a, b, d):
                    o.at(2 * (t - 1) if b else 0)
                    if a:
                        low(t, "oT_dve", "o_turned", "out_mm", oT, tA)
                    if b:
                        dve.wait_ge(s["s_mm"], upto(t - 1))
                        o(dve.tensor_reduce(top[:], sc[:].rearrange("p a (b m) -> p (a b) m", m=MEM), AX, ALU.max))
                        dve.tensor_scalar(ntop[:], top[:], -1.0, None, ALU.mult).then_inc(s["max_ok"], 1)
                        dve.wait_ge(s["exp_ok"], upto(t - 1))
                        o(dve.reciprocal(rl[:], l[:]))
                        dve.tensor_tensor(pr[:], pr[:], rl[:].unsqueeze(2).to_broadcast([P, HEADS, MEM]),
                                          ALU.mult).then_inc(s["p_ok"], 1)
                    if a:
                        dve.wait_ge(in_ok[u], 32 * (pair + 1))
                        dve.wait_ge(s["out_mm"], upto(t))
                        dve.tensor_tensor(x2[u][:], acc[:].rearrange("p a n -> p (a n)"), xin[u][:],
                                          ALU.add).then_inc(s["x2_ok"], 1)
                    if b:
                        low(t - 1, "pT_dve", "p_turned", "co_mm", pT, tB)
                    if d:
                        low(t - 2, "hT4_dve", "h4_turned", "r_mm", hT4, tA)
                    if a:
                        dve.wait_ge(s["rs3_ok"], upto(t))
                        dve.wait_ge(s["h3_turned"], upto(t - 1))
                        dve.tensor_scalar(xn3[:], x2[u][:], rs3[:, 0:1], None, ALU.mult).then_inc(s["xn3_ok"], 1)
                    if b:
                        dve.wait_ge(s["co_mm"], upto(t - 1))
                        dve.wait_ge(x3_out[1 - u], 16 * (pair + u))
                        dve.tensor_tensor(x3t[1 - u][:], sc[:].rearrange("p a n -> p (a n)"), x2[1 - u][:],
                                          ALU.add).then_inc(s["x3_ok"], 1)
                    if d:
                        dve.wait_ge(s["r_mm"], upto(t - 2))
                        dve.tensor_copy(logits[:, bass.ds(t - 2, 1), :].rearrange("p a n -> p (a n)"),
                                        tA[:, 0, 0:NR]).then_inc(s["logits_ok"], 1)
                    if a:
                        low(t, "hT3_dve", "h3_turned", "s_mm", hT3, tB, c.g_cross)
                    if b:
                        dve.wait_ge(s["rs4_ok"], upto(t - 1))
                        dve.wait_ge(h4_out[1 - u], 16 * (pair + u))
                        if d:
                            dve.wait_ge(s["h4_turned"], upto(t - 3))
                        dve.scalar_tensor_tensor(out=xn4[:], in0=x3t[1 - u][:], scalar=rs4[:, 0:1], in1=gb[:],
                                                 op0=ALU.mult, op1=ALU.mult).then_inc(s["xf_ok"], 1)
                        dve.wait_ge(s["xh_ok"], upto(t - 1))
                        dve.tensor_tensor(xp4[1 - u][:, 1, :], xn4[:], xp4[1 - u][:, 0, :].bitcast(F32),
                                          ALU.subtract).then_inc(s["xn4_ok"], 1)

                steps(dve, step)

            @block.tensor
            def _(pe):
                for n in ("o_turned", "s_mm", "out_mm", "p_turned", "h4_turned", "co_mm", "r_mm", "h3_turned"):
                    pe.sem_inc(s[n], 1)
                pe.wait_ge(w_ok, 64)

                def turn(name, dst, blocks):
                    for k, blk in enumerate(blocks):
                        last = pe.transpose(dst[:, k // 4, (k % 4) * P:(k % 4 + 1) * P], blk, c.ident[:])
                    last.then_inc(s[name], 1)

                def cut(tile):
                    return [tile[:, k * P:(k + 1) * P] for k in range(KC)]

                def product(name, dst, left, right):
                    for half in range(2):
                        for k in range(KC):
                            last = pe.matmul(dst[:, half, :], left[:, k, :], right[:, k, half * H:(half + 1) * H],
                                             start=(k == 0), stop=(k == KC - 1))
                    last.then_inc(s[name], 1)

                def step(t, u, pair, a, b, d):
                    if a:
                        pe.wait_ge(in_ok[u], 32 * (pair + 1))
                        pe.wait_ge(s["logits_ok"], upto(t - 3) if d else 1)
                        pe.wait_ge(s["oT_act"], upto(t - 1))
                        pe.wait_ge(s["oT_dve"], upto(t - 1))
                        turn("o_turned", tA, cut(mixin[u]))
                    if b:
                        pe.wait_ge(s["hT3_dve"], upto(t - 1))
                        pe.wait_ge(s["hT3_act"], upto(t - 1))
                        pe.wait_ge(s["x3_ok"], upto(t - 2))
                        product("s_mm", sc, hT3, wqk)
                    if a:
                        pe.wait_ge(s["oT_dve"], upto(t))
                        pe.wait_ge(s["oT_act"], upto(t))
                        pe.wait_ge(s["x2_ok"], upto(t - 1))
                        product("out_mm", acc, oT, wo)
                    if b:
                        pe.wait_ge(s["p_ok"], upto(t - 1))
                        pe.wait_ge(s["hT3_dve"], upto(t - 1))
                        pe.wait_ge(s["hT3_act"], upto(t - 1))
                        turn("p_turned", tB, cut(pr[:].rearrange("p h m -> p (h m)")))
                    if d:
                        pe.wait_ge(s["xn4_ok"], upto(t - 2))
                        if a:
                            pe.wait_ge(s["oT_dve"], upto(t))
                            pe.wait_ge(s["oT_act"], upto(t))
                        for k in range(KC):
                            for part in range(2):
                                last = pe.matmul(tA[:, k // 4, (k % 4) * P:(k % 4 + 1) * P],
                                                 xp4[u][:, part, k * P:(k + 1) * P], c.identr[:],
                                                 start=(part == 0), stop=(part == 1))
                        last.then_inc(s["h4_turned"], 1)
                    if b:
                        pe.wait_ge(s["pT_dve"], upto(t - 1))
                        pe.wait_ge(s["pT_act"], upto(t - 1))
                        pe.wait_ge(s["exp_ok"], upto(t - 1))
                        product("co_mm", sc, pT, wvo)
                    if d:
                        pe.wait_ge(s["hT4_dve"], upto(t - 2))
                        pe.wait_ge(s["hT4_act"], upto(t - 2))
                        for k in range(KC):
                            last = pe.matmul(tA[:, 0, 0:NR], hT4[:, k, :], wr[:, k, :], start=(k == 0), stop=(k == KC - 1))
                        last.then_inc(s["r_mm"], 1)
                    if a:
                        pe.wait_ge(s["xn3_ok"], upto(t))
                        if b:
                            pe.wait_ge(s["pT_dve"], upto(t - 1))
                            pe.wait_ge(s["pT_act"], upto(t - 1))
                        turn("h3_turned", tB, cut(xn3))

                steps(pe, step)


EXPERT, CHANGED, BEFORE, LOADS = range(4)
TOTAL = 4 * NBLK


def route_phase(nc, c, b_rg, b_re, logits, dest, gate, rows, table):
    NR = GROUPS + EXPERTS
    ROUND = 8
    with ExitStack() as ctx:
        sb, ps, sem = alloc(nc, ctx, "route")
        bias = sb("bias", [P, NR])
        lg = sb("lg", [P, NT, NR])
        rank = sb("rank", [P, PER_GROUP])
        thr, blk_id, row_id, keep, one = (sb("thr", [P, NT]), sb("blk_id", [P, NBLK]), sb("row_id", [P, P]),
                                          sb("keep", [P, EXPERTS, NT]), sb("one", [P, P]))
        before, token = sb("before", [P, P]), sb("token", [P, NT])
        t1 = [sb(f"t1_{n}", [P, NT]) for n in range(3)]
        t4 = [sb(f"t4_{n}", [P, NT, 4]) for n in range(4)]
        og, oe = sb("og", [P, NT, GROUPS]), sb("oe", [P, 2, NT, PER_GROUP])
        pg, e2, half_gate = sb("pg", [P, NT]), sb("e2", [P, NT]), sb("half_gate", [P, NT])
        t16 = sb("t16", [P, NT, GROUPS, PER_GROUP])
        pick = sb("pick", [P, 2, NT, EXPERTS])
        both = sb("both", [P, NT, EXPERTS])
        tot, cum, offs = (sb(n, [P, EXPERTS, NT]) for n in ("tot", "cum", "offs"))
        counts, nblk, endb, startr = (sb(n, [P, EXPERTS]) for n in ("counts", "nblk", "endb", "startr"))
        wide = sb("wide", [P, NBLK, EXPERTS])
        eb, ch, tm1 = sb("eb", [P, NBLK]), sb("ch", [P, NBLK]), sb("tm1", [P, 1])
        bt = [sb(f"bt{n}", [P, NBLK]) for n in range(4)]
        place, part, destf = sb("place", [P, NT, EXPERTS]), sb("part", [P, NT, EXPERTS]), sb("destf", [P, NT, 2])
        hi_i, lo_i = sb("hi_i", [P, NT, 2], I32), sb("lo_i", [P, NT, 2], I32)
        hi, lo = sb("hi", [P, NT, 2]), sb("lo", [P, NT, 2])
        low_hot = [sb(f"low_hot{u}", [P, ROUND, P]) for u in range(2)]
        high_hot = sb("high_hot", [P, 2 * NT, NBLK])
        cps, rps = ps("cps", [P, 2, NT * EXPERTS]), ps("rps", [P, NBLK])
        bias_in, set_ok, ask_exp, exp_ok, count_ok, count_mm, hot_ok, hot_used, rows_mm, step_dve, step_pool = (
            sem(n) for n in ("bias_in", "set_ok", "ask_exp", "exp_ok", "count_ok", "count_mm", "hot_ok", "hot_used",
                             "rows_mm", "step_dve", "step_pool"))
        with nc.Block() as block:
            @block.sync
            def _(sp):
                sp.dma_start(bias[:, 0:GROUPS], b_rg.partition_broadcast(P)).then_inc(bias_in, 16)
                sp.dma_start(bias[:, GROUPS:], b_re.partition_broadcast(P)).then_inc(bias_in, 16)

            @block.gpsimd
            def _(pool):
                o = Order(pool, step_pool)
                real = dict(allow_small_or_imprecise_dtypes=True)
                o(pool.iota(rank[:], [[-1, PER_GROUP]], base=PER_GROUP, channel_multiplier=0, **real))
                o(pool.iota(thr[:], [[P, NT]], base=0, channel_multiplier=0, **real))
                o(pool.iota(blk_id[:], [[1, NBLK]], base=0, channel_multiplier=0, **real))
                o(pool.iota(row_id[:], [[1, P]], base=0, channel_multiplier=0, **real))
                o(pool.iota(token[:], [[P, NT]], base=0, channel_multiplier=1, **real))
                o(pool.memset(keep[:], 1.0))
                o(pool.memset(keep[:, :, 0:1], 0.0))
                o(pool.memset(one[:], 1.0))
                o(pool.affine_select(out=before[:], in_=one[:], compare_op=ALU.is_gt, fill=0.0, base=0,
                                     pattern=[[1, P]], channel_multiplier=-1))
                pool.sem_inc(set_ok, 1)

            @block.scalar
            def _(act):
                act.wait_ge(ask_exp, 1)
                act.activation(t4[1][:], t4[0][:], ACT.Exp).then_inc(exp_ok, 1)
                act.wait_ge(ask_exp, 2)
                act.activation(e2[:], t1[2][:], ACT.Exp).then_inc(exp_ok, 1)

            @block.tensor
            def _(pe):
                pe.wait_ge(count_ok, 1)
                flat = both[:].rearrange("p t e -> p (t e)")
                pe.matmul(cps[:, 0, :], before[:], flat, start=True, stop=True)
                pe.matmul(cps[:, 1, :], one[:], flat, start=True, stop=True).then_inc(count_mm, 1)
                for n in range(2 * NT):
                    if n % ROUND == 0:
                        pe.wait_ge(hot_ok, n // ROUND + 1)
                    last = pe.matmul(rps[:], low_hot[n // ROUND % 2][:, n % ROUND, :], high_hot[:, n, :],
                                     start=(n == 0), stop=(n == 2 * NT - 1))
                    if n % ROUND == ROUND - 1:
                        last.then_inc(hot_used, 1)

            @block.vector
            def _(dve):
                o = Order(dve, step_dve)

                def over(x, n):
                    return x.unsqueeze(2).to_broadcast([P, x.shape[1], n])

                def rows_of(x, n):
                    return x.unsqueeze(1).to_broadcast([P, n, x.shape[1]])

                def first_of(out, d, tmp, top):
                    o(dve.tensor_scalar(tmp[:], d[:], 0.0, None, ALU.is_ge))
                    o(dve.tensor_tensor(tmp[:], tmp[:], rows_of(rank[:], NT), ALU.mult))
                    o(dve.tensor_reduce(top[:], tmp[:], AX, ALU.max))
                    o(dve.tensor_tensor(out, tmp[:], over(top[:], 4), ALU.is_equal))

                dve.wait_ge(bias_in, 32)
                dve.wait_ge(set_ok, 1)
                o(dve.tensor_tensor(lg[:], logits[:], rows_of(bias[:], NT), ALU.add))
                o(dve.tensor_reduce(t1[0][:], lg[:, :, 0:GROUPS], AX, ALU.max))
                dve.tensor_tensor(t4[0][:], lg[:, :, 0:GROUPS], over(t1[0][:], GROUPS), ALU.subtract).then_inc(ask_exp, 1)
                dve.wait_ge(ask_exp, 1)
                first_of(og[:], t4[0], t4[2], t1[1])
                dve.wait_ge(exp_ok, 1)
                o(dve.tensor_reduce(t1[0][:], t4[1][:], AX, ALU.add))
                o(dve.reciprocal(pg[:], t1[0][:]))
                for g in range(GROUPS):
                    last = dve.tensor_tensor(t16[:, :, g, :], lg[:, :, GROUPS + g * PER_GROUP:GROUPS + (g + 1) * PER_GROUP],
                                             og[:, :, g:g + 1].to_broadcast([P, NT, PER_GROUP]), ALU.mult)
                o(last)
                o(dve.tensor_reduce(t4[3][:], t16[:].rearrange("p t g j -> p t j g"), AX, ALU.add))
                o(dve.tensor_reduce(t1[0][:], t4[3][:], AX, ALU.max))
                o(dve.tensor_tensor(t4[3][:], t4[3][:], over(t1[0][:], 4), ALU.subtract))
                first_of(oe[:, 0, :, :], t4[3], t4[2], t1[1])
                o(dve.scalar_tensor_tensor(out=t4[3][:], in0=oe[:, 0, :, :], scalar=NEG, in1=t4[3][:], op0=ALU.mult, op1=ALU.add))
                dve.tensor_reduce(t1[2][:], t4[3][:], AX, ALU.max).then_inc(ask_exp, 1)
                dve.wait_ge(ask_exp, 2)
                o(dve.tensor_tensor(t4[3][:], t4[3][:], over(t1[2][:], 4), ALU.subtract))
                first_of(oe[:, 1, :, :], t4[3], t4[2], t1[1])
                dve.wait_ge(exp_ok, 2)
                o(dve.tensor_scalar(t1[0][:], e2[:], 1.0, None, ALU.add))
                o(dve.reciprocal(half_gate[:], t1[0][:]))
                o(dve.tensor_tensor(half_gate[:], half_gate[:], pg[:], ALU.mult))
                dve.tensor_copy(gate[:, :, 0], half_gate[:])
                dve.tensor_tensor(gate[:, :, 1], half_gate[:], e2[:], ALU.mult)
                for k in range(2):
                    for g in range(GROUPS):
                        last = dve.tensor_tensor(pick[:, k, :, g * PER_GROUP:(g + 1) * PER_GROUP], oe[:, k, :, :],
                                                 og[:, :, g:g + 1].to_broadcast([P, NT, PER_GROUP]), ALU.mult)
                o(last)
                dve.tensor_tensor(both[:], pick[:, 0, :, :], pick[:, 1, :, :], ALU.add).then_inc(count_ok, 1)
                dve.wait_ge(count_mm, 1)
                o(dve.tensor_copy(tot[:], cps[:, 1, :].rearrange("p (t e) -> p e t", e=EXPERTS)))
                o(dve.tensor_tensor_scan(cum[:].rearrange("p e t -> p (e t)"), keep[:].rearrange("p e t -> p (e t)"),
                                         tot[:].rearrange("p e t -> p (e t)"), 0.0, ALU.mult, ALU.add))
                dve.tensor_copy(counts[:], cum[:, :, NT - 1])
                o(dve.tensor_tensor(offs[:], cum[:], tot[:], ALU.subtract))
                o(dve.tensor_tensor(tot[:], over(counts[:], NT), rows_of(thr[:], EXPERTS), ALU.is_gt))
                o(dve.tensor_reduce(nblk[:], tot[:], AX, ALU.add))
                o(dve.tensor_tensor_scan(endb[:], one[:, 0:EXPERTS], nblk[:], 0.0, ALU.mult, ALU.add))
                o(dve.tensor_tensor(startr[:], endb[:], nblk[:], ALU.subtract))
                o(dve.tensor_scalar(startr[:], startr[:], float(P), None, ALU.mult))
                o(dve.tensor_tensor(offs[:], offs[:], over(startr[:], NT), ALU.add))
                o(dve.tensor_tensor(place[:], cps[:, 0, :].rearrange("p (t e) -> p t e", e=EXPERTS),
                                    offs[:].rearrange("p e t -> p t e"), ALU.add))
                for k in range(2):
                    o(dve.tensor_tensor(part[:], place[:], pick[:, k, :, :], ALU.mult))
                    o(dve.tensor_reduce(destf[:, :, k:k + 1].rearrange("p t a -> p (t a)"), part[:], AX, ALU.add))
                o(dve.tensor_copy(dest[:], destf[:]))
                o(dve.tensor_scalar(hi_i[:], dest[:], 7, None, ALU.arith_shift_right))
                o(dve.tensor_scalar(lo_i[:], dest[:], P - 1, None, ALU.bitwise_and))
                o(dve.tensor_copy(hi[:], hi_i[:]))
                o(dve.tensor_copy(lo[:], lo_i[:]))
                hi_f, lo_f = (x[:].rearrange("p t k -> p (t k)") for x in (hi, lo))
                o(dve.tensor_tensor(high_hot[:], rows_of(blk_id[:], 2 * NT), over(hi_f, NBLK), ALU.is_equal))
                for k in range(2):
                    last = dve.tensor_tensor(high_hot[:].rearrange("p (t k) b -> p t k b", k=2)[:, :, k, :],
                                             high_hot[:].rearrange("p (t k) b -> p t k b", k=2)[:, :, k, :],
                                             over(token[:], NBLK), ALU.mult)
                o(last)
                for n in range(2 * NT // ROUND):
                    if n >= 2:
                        dve.wait_ge(hot_used, n - 1)
                    dve.tensor_tensor(low_hot[n % 2][:], rows_of(row_id[:], ROUND),
                                      over(lo_f[:, n * ROUND:(n + 1) * ROUND], P), ALU.is_equal).then_inc(hot_ok, 1)
                o(dve.tensor_scalar(tm1[:], endb[:, EXPERTS - 1:EXPERTS], -1.0, None, ALU.add))
                o(dve.tensor_scalar(bt[0][:], blk_id[:], tm1[:, 0:1], None, ALU.min))
                o(dve.tensor_tensor(wide[:], rows_of(endb[:], NBLK), over(bt[0][:], EXPERTS), ALU.is_le))
                o(dve.tensor_reduce(eb[:], wide[:], AX, ALU.add))
                o(dve.memset(ch[:, 0:1], 1.0))
                o(dve.tensor_tensor(ch[:, 1:], eb[:, 1:], eb[:, 0:NBLK - 1], ALU.not_equal))
                o(dve.memset(bt[1][:], 1.0))
                o(dve.tensor_tensor_scan(bt[2][:], bt[1][:], ch[:], 0.0, ALU.mult, ALU.add))
                o(dve.tensor_tensor(bt[0][:], ch[:], blk_id[:], ALU.mult))
                o(dve.memset(bt[1][:], 0.0))
                o(dve.memset(bt[3][:, 0:1], -1.0))
                o(dve.tensor_tensor_scan(bt[3][:, 1:], bt[0][:, 0:NBLK - 1], bt[1][:, 0:NBLK - 1], -1.0, ALU.max, ALU.add))
                o(dve.tensor_scalar(bt[3][:], bt[3][:], 1.0, None, ALU.add))
                for what, src in ((EXPERT, eb), (CHANGED, ch), (BEFORE, bt[3]), (LOADS, bt[2])):
                    dve.tensor_copy(table[:, what * NBLK:(what + 1) * NBLK], src[:])
                dve.tensor_copy(table[:, TOTAL:TOTAL + 1], endb[:, EXPERTS - 1:EXPERTS])
                dve.wait_ge(hot_used, 2 * NT // ROUND)
                dve.tensor_copy(rows[:], rps[:])


def expert_phase(nc, c, h4, w_gate, w_up, w_down, rows, table, ys):
    ND = DE // P
    GU, DN = 2 * DE, D
    DOWN = KC * GU
    ALL = DOWN + ND * DN
    with ExitStack() as ctx:
        sb, ps, sem = alloc(nc, ctx, "exp")
        raw = sb("raw", [P, ALL])
        wh, wl = sb("wh", [P, ALL], F32R), sb("wl", [P, ALL], F32R)
        xg, idx = sb("xg", [P, 2 * D], F32R), sb("idx", [P, 1], I32)
        xT = sb("xT", [P, 2, KC, P], F32R)
        sg, hid = sb("sg", [P, DE]), sb("hid", [P, DE])
        hs, hT = sb("hs", [P, 2, DE], F32R), sb("hT", [P, 2, ND, P], F32R)
        y = sb("y", [P, D])
        xps, hps = ps("xps", [P, 2, 512], F32R), ps("hps", [P, 2, DE], F32R)
        gups, yps = ps("gups", [P, 2, DE]), ps("yps", [P, 2, 512])
        names = ("x_turned x_low x_high gu_mm silu_ok hid_ok hi_ok hs_ok h_turned hT_ok hT_act down_mm y_low y_high "
                 "gu_hi gu_ok dn_hi dn_ok").split()
        s = {n: sem(n) for n in names}
        gu_dma, dn_dma, gu_raw, dn_raw, idx_ok, pool_go, x_in, y_out, passed = (sem(n) for n in (
            "gu_dma", "dn_dma", "gu_raw", "dn_raw", "idx_ok", "pool_go", "x_in", "y_out", "passed"))

        def upto(b, per=1):
            return b * per + per + 1

        def entry(eng, b, what, most):
            return eng.value_load(table[0:1, bass.ds(b + what * NBLK, 1)], min_val=0, max_val=most)

        def steps(eng, step):
            step(0, True, False)
            with eng.Fori(1, NBLK - 1) as b:
                step(b, False, False)
            step(NBLK - 1, False, True)

        with nc.Block() as block:
            @block.sync
            def _(sp):
                def load_gate_up(e):
                    gu = raw[:, 0:DOWN].rearrange("p (k m n) -> p k m n", m=2, n=DE)
                    for m, src in ((0, w_gate), (1, w_up)):
                        sp.dma_start(gu[:, :, m, :], src[bass.ds(e, 1), :, :].rearrange("a (k p) n -> p (a k) n", p=P)
                                     ).then_inc(gu_dma, 16)

                def load_down(e):
                    sp.dma_start(raw[:, DOWN:].rearrange("p (k n) -> p k n", n=D),
                                 w_down[bass.ds(e, 1), :, :].rearrange("a (k p) n -> p (a k) n", p=P)).then_inc(dn_dma, 16)

                def step(b, first, last):
                    e = entry(sp, b, EXPERT, EXPERTS - 1)
                    before = entry(sp, b, BEFORE, NBLK)
                    loads = entry(sp, b, LOADS, EXPERTS)
                    with sp.If(entry(sp, b, CHANGED, 1) >= 1):
                        sp.wait_ge(s["gu_ok"], before * KC + 1)
                        load_gate_up(e)
                        sp.wait_ge(gu_dma, loads * 32)
                        sp.sem_inc(gu_raw, 1)
                        sp.wait_ge(s["dn_ok"], before * ND + 1)
                        load_down(e)
                        sp.wait_ge(dn_dma, loads * 16)
                        sp.sem_inc(dn_raw, 1)
                    with sp.Else():
                        sp.sem_inc(gu_raw, 1)
                        sp.sem_inc(dn_raw, 1)

                steps(sp, step)

            @block.gpsimd
            def _(pool):
                def step(b, first, last):
                    if not first:
                        pool.wait_ge(s["x_turned"], upto(b - 1, 2))
                        pool.sem_inc(pool_go, 1)
                    pool.tensor_copy(idx[:], rows[:, bass.ds(b, 1)]).then_inc(idx_ok, 1)
                    pool.wait_ge(idx_ok, b + 1)
                    pool.sem_inc(pool_go, 1)
                    pool.indirect_dma_start(out=xg[:].bitcast(F32), out_offset=None, in_=h4[:, :],
                                            in_offset=bass.IndirectOffsetOnAxis(ap=idx[:, 0:1], axis=0)).then_inc(x_in, 16)

                steps(pool, step)

            @block.scalar
            def _(act):
                for n in ("x_high", "silu_ok", "hi_ok", "hT_act", "y_high", "gu_hi", "dn_hi"):
                    act.sem_inc(s[n], 1)
                act.sem_inc(y_out, 16)

                def rows_in(b, part):
                    act.wait_ge(s["x_turned"], upto(b, 2) - 1 + part)
                    act.activation(xT[:, part, 4:8, :].rearrange("p k n -> p (k n)"), xps[:, 1, :].bitcast(F32),
                                   ACT.Copy).then_inc(s["x_high"], 1)

                def round_weights(b, arrived, name, done, start, chunks, size):
                    with act.If(entry(act, b, CHANGED, 1) >= 1):
                        act.wait_ge(arrived, b + 1)
                        act.wait_ge(s[done], upto(b - 1, chunks))
                        for k in range(chunks):
                            cols = slice(start + k * size, start + (k + 1) * size)
                            act.activation(wh[:, cols], raw[:, cols], ACT.Copy).then_inc(s[name], 1)
                    with act.Else():
                        act.sem_inc(s[name], chunks)

                def step(b, first, last):
                    if first:
                        rows_in(0, 0)
                        rows_in(0, 1)
                        round_weights(0, gu_raw, "gu_hi", "gu_ok", 0, KC, GU)
                    act.wait_ge(s["gu_mm"], upto(b))
                    act.activation(sg[:], gups[:, 0, :], ACT.Silu).then_inc(s["silu_ok"], 1)
                    if not last:
                        rows_in(b + 1, 0)
                    act.wait_ge(s["hid_ok"], upto(b))
                    act.activation(hs[:, 0, :], hid[:], ACT.Copy).then_inc(s["hi_ok"], 1)
                    if not last:
                        rows_in(b + 1, 1)
                        round_weights(b + 1, gu_raw, "gu_hi", "gu_ok", 0, KC, GU)
                    if not first:
                        result(b - 1)
                    round_weights(b, dn_raw, "dn_hi", "dn_ok", DOWN, ND, DN)
                    act.wait_ge(s["h_turned"], upto(b))
                    act.activation(hT[:, 1, :, :].rearrange("p k n -> p (k n)"), hps[:, 1, :].bitcast(F32),
                                   ACT.Copy).then_inc(s["hT_act"], 1)
                    if last:
                        result(b)

                def result(b):
                    act.wait_ge(s["down_mm"], upto(b))
                    act.wait_ge(y_out, 16 * (b + 1))
                    act.activation(y[:, 512:], yps[:, 1, :], ACT.Copy).then_inc(s["y_high"], 1)
                    act.wait_ge(s["y_high"], upto(b))
                    act.wait_ge(s["y_low"], upto(b))
                    act.dma_start(ys[bass.ds(b * P, P), :], y[:]).then_inc(y_out, 16)

                steps(act, step)
                act.wait_ge(y_out, 16 * (NBLK + 1))

            @block.vector
            def _(dve):
                for n in ("x_low", "hid_ok", "hs_ok", "hT_ok", "y_low", "gu_ok", "dn_ok"):
                    dve.sem_inc(s[n], 1)

                def rows_in(b, part):
                    dve.wait_ge(s["x_turned"], upto(b, 2) - 1 + part)
                    dve.tensor_copy(xT[:, part, 0:4, :].rearrange("p k n -> p (k n)"),
                                    xps[:, 0, :].bitcast(F32)).then_inc(s["x_low"], 1)

                def rest_of_weights(b, name, hi, start, chunks, size):
                    with dve.If(entry(dve, b, CHANGED, 1) >= 1):
                        for k in range(chunks):
                            cols = slice(start + k * size, start + (k + 1) * size)
                            dve.wait_ge(s[hi], b * chunks + k + 2)
                            dve.tensor_tensor(wl[:, cols], raw[:, cols], wh[:, cols].bitcast(F32),
                                              ALU.subtract).then_inc(s[name], 1)
                    with dve.Else():
                        dve.sem_inc(s[name], chunks)

                def result(b):
                    dve.wait_ge(s["down_mm"], upto(b))
                    dve.wait_ge(y_out, 16 * (b + 1))
                    dve.tensor_copy(y[:, 0:512], yps[:, 0, :]).then_inc(s["y_low"], 1)

                def step(b, first, last):
                    if first:
                        rows_in(0, 0)
                        rows_in(0, 1)
                        rest_of_weights(0, "gu_ok", "gu_hi", 0, KC, GU)
                    dve.wait_ge(s["silu_ok"], upto(b))
                    dve.tensor_tensor(hid[:], sg[:], gups[:, 1, :], ALU.mult).then_inc(s["hid_ok"], 1)
                    if not last:
                        rows_in(b + 1, 0)
                    dve.wait_ge(s["hi_ok"], upto(b))
                    dve.tensor_tensor(hs[:, 1, :], hid[:], hs[:, 0, :].bitcast(F32), ALU.subtract).then_inc(s["hs_ok"], 1)
                    if not last:
                        rows_in(b + 1, 1)
                        rest_of_weights(b + 1, "gu_ok", "gu_hi", 0, KC, GU)
                    if not first:
                        result(b - 1)
                    rest_of_weights(b, "dn_ok", "dn_hi", DOWN, ND, DN)
                    dve.wait_ge(s["h_turned"], upto(b))
                    dve.tensor_copy(hT[:, 0, :, :].rearrange("p k n -> p (k n)"), hps[:, 0, :].bitcast(F32)).then_inc(s["hT_ok"], 1)
                    if last:
                        result(b)

                steps(dve, step)

            @block.tensor
            def _(pe):
                for n in ("x_turned", "gu_mm", "h_turned", "down_mm"):
                    pe.sem_inc(s[n], 1)
                blocks = pe.value_load(table[0:1, TOTAL:TOTAL + 1], min_val=0, max_val=NBLK)

                def rows_turned(b, part):
                    if part == 0:
                        pe.wait_ge(x_in, 16 * (b + 1))
                    for n in ("x_low", "x_high"):
                        pe.wait_ge(s[n], upto(b, 2) - 2 + part)
                    for k in range(KC):
                        last = pe.transpose(xps[:, k // 4, (k % 4) * P:(k % 4 + 1) * P],
                                            xg[:, part * D + k * P:part * D + (k + 1) * P], c.identr[:])
                    last.then_inc(s["x_turned"], 1)

                def triple(dst, left, k, cols, first, last):
                    pe.matmul(dst, left[:, 0, k, :], wh[:, cols], start=first, stop=False)
                    pe.matmul(dst, left[:, 0, k, :], wl[:, cols], start=False, stop=False)
                    return pe.matmul(dst, left[:, 1, k, :], wh[:, cols], start=False, stop=last)

                def gate_up(b):
                    for n in ("x_low", "x_high"):
                        pe.wait_ge(s[n], upto(b, 2))
                    pe.wait_ge(s["hid_ok"], upto(b - 1))
                    with pe.If(blocks > b):
                        for k in range(KC):
                            pe.wait_ge(s["gu_ok"], b * KC + k + 2)
                            for m in range(2):
                                cols = slice(k * GU + m * DE, k * GU + (m + 1) * DE)
                                last = triple(gups[:, m, :], xT, k, cols, k == 0, k == KC - 1)
                        last.then_inc(s["gu_mm"], 1)
                    with pe.Else():
                        pe.sem_inc(s["gu_mm"], 1)

                def hidden_turned(b):
                    pe.wait_ge(s["hs_ok"], upto(b))
                    pe.wait_ge(s["hi_ok"], upto(b))
                    pe.wait_ge(s["hT_ok"], upto(b - 1))
                    pe.wait_ge(s["hT_act"], upto(b - 1))
                    for part in range(2):
                        for k in range(ND):
                            last = pe.transpose(hps[:, part, k * P:(k + 1) * P], hs[:, part, k * P:(k + 1) * P], c.identr[:])
                    last.then_inc(s["h_turned"], 1)

                def down(b, half):
                    if half == 0:
                        pe.wait_ge(s["hT_ok"], upto(b))
                        pe.wait_ge(s["hT_act"], upto(b))
                        pe.wait_ge(s["y_low"], upto(b - 1))
                        pe.wait_ge(s["y_high"], upto(b - 1))
                    with pe.If(blocks > b):
                        for k in range(ND):
                            if half == 0:
                                pe.wait_ge(s["dn_ok"], b * ND + k + 2)
                            cols = slice(DOWN + k * DN + half * 512, DOWN + k * DN + half * 512 + 512)
                            last = triple(yps[:, half, :], hT, k, cols, k == 0, k == ND - 1)
                        if half == 1:
                            last.then_inc(s["down_mm"], 1)
                    with pe.Else():
                        if half == 1:
                            pe.sem_inc(s["down_mm"], 1)
                        else:
                            pe.sem_inc(passed, 1)

                def step(b, first, last):
                    if first:
                        rows_turned(0, 0)
                        rows_turned(0, 1)
                    gate_up(b)
                    if not last:
                        rows_turned(b + 1, 0)
                    if not first:
                        down(b - 1, 0)
                    if not last:
                        rows_turned(b + 1, 1)
                    if not first:
                        down(b - 1, 1)
                    hidden_turned(b)
                    if last:
                        down(b, 0)
                        down(b, 1)

                steps(pe, step)


def combine_phase(nc, c, x3, ys, dest, gate, gain, out):
    DEPTH = 4
    with ExitStack() as ctx:
        sb, ps, sem = alloc(nc, ctx, "comb")
        R = range(DEPTH)
        idx = [sb(f"idx{u}", [P, 2], I32) for u in R]
        xin, y0, y1, res = ([sb(f"{n}{u}", [P, D]) for u in R] for n in ("xin", "y0", "y1", "res"))
        gb, sq = sb("gb", [P, D]), sb("sq", [P, D])
        ss, ms, rs = ([sb(f"{n}{u}", [P, 1]) for u in R] for n in ("ss", "ms", "rs"))
        g_in, idx_ok, pool_go, sum_ok, ss_ok, ms_ok, rs_ok, done, part = (sem(n) for n in (
            "g_in", "idx_ok", "pool_go", "sum_ok", "ss_ok", "ms_ok", "rs_ok", "done", "part"))
        x_in, y0_in, y1_in, stored = ([sem(f"{n}{u}") for u in R] for n in ("x_in", "y0_in", "y1_in", "stored"))
        with nc.Block() as block:
            @block.sync
            def _(sp):
                sp.dma_start(gb[:], gain.partition_broadcast(P)).then_inc(g_in, 16)
                with sp.Fori(0, NT // DEPTH) as four:
                    for u in R:
                        t = DEPTH * four + u
                        sp.wait_ge(done, t + 1)
                        sp.dma_start(xin[u][:], x3[bass.ds(t * P, P), :]).then_inc(x_in[u], 16)

            @block.gpsimd
            def _(pool):
                def gather(t, u):
                    pool.wait_ge(done, t + 1)
                    pool.sem_inc(pool_go, 1)
                    pool.tensor_copy(idx[u][:], dest[:, bass.ds(t, 1), :].rearrange("p a k -> p (a k)")).then_inc(idx_ok, 1)
                    pool.wait_ge(idx_ok, t + 1)
                    pool.sem_inc(pool_go, 1)
                    for k, (dst, arrived) in enumerate(((y0, y0_in), (y1, y1_in))):
                        pool.indirect_dma_start(out=dst[u][:], out_offset=None, in_=ys[:, :],
                                                in_offset=bass.IndirectOffsetOnAxis(ap=idx[u][:, k:k + 1], axis=0)
                                                ).then_inc(arrived[u], 16)

                def rsqrt(t, u):
                    pool.wait_ge(ss_ok, t + 1)
                    pool.tensor_tensor(ms[u][:], ss[u][:], c.eps[:, 0:1], ALU.add).then_inc(ms_ok, 1)
                    pool.wait_ge(ms_ok, t + 1)
                    pool.tensor_tensor(rs[u][:], ms[u][:], c.half[:, 0:1], ALU.pow).then_inc(rs_ok, 1)

                for u in R:
                    gather(u, u)
                with pool.Fori(0, NT // DEPTH - 1) as four:
                    for u in R:
                        rsqrt(DEPTH * four + u, u)
                        gather(DEPTH * four + u + DEPTH, u)
                for u in R:
                    rsqrt(NT - DEPTH + u, u)

            @block.scalar
            def _(act):
                for s in stored:
                    act.sem_inc(s, 16)
                with act.Fori(0, NT // DEPTH) as four:
                    for u in R:
                        t = DEPTH * four + u
                        act.wait_ge(sum_ok, t + 1)
                        act.wait_ge(done, t + DEPTH)
                        act.activation(sq[:], res[u][:], ACT.Square, scale=D ** -0.5, accum_out=ss[u][:]).then_inc(ss_ok, 1)
                        act.wait_ge(done, t + DEPTH + 1)
                        act.dma_start(out[bass.ds(t * P, P), :], res[u][:]).then_inc(stored[u], 16)
                for s in stored:
                    act.wait_ge(s, 16 * (NT // DEPTH + 1))

            @block.vector
            def _(dve):
                dve.sem_inc(done, DEPTH)
                dve.wait_ge(g_in, 16)
                with dve.Fori(0, NT // DEPTH) as four:
                    for u in R:
                        t = DEPTH * four + u
                        dve.wait_ge(x_in[u], 16 * (four + 1))
                        dve.wait_ge(y0_in[u], 16 * (four + 1))
                        dve.scalar_tensor_tensor(out=y0[u][:], in0=y0[u][:], scalar=gate[:, bass.ds(t, 1), 0], in1=xin[u][:],
                                                 op0=ALU.mult, op1=ALU.add).then_inc(part, 1)
                        dve.wait_ge(part, t + 1)
                        dve.wait_ge(y1_in[u], 16 * (four + 1))
                        dve.wait_ge(stored[u], 16 * (four + 1))
                        dve.scalar_tensor_tensor(out=res[u][:], in0=y1[u][:], scalar=gate[:, bass.ds(t, 1), 1], in1=y0[u][:],
                                                 op0=ALU.mult, op1=ALU.add).then_inc(sum_ok, 1)
                        dve.wait_ge(rs_ok, t + 1)
                        dve.scalar_tensor_tensor(out=res[u][:], in0=res[u][:], scalar=rs[u][:, 0:1], in1=gb[:],
                                                 op0=ALU.mult, op1=ALU.mult).then_inc(done, 1)


def trunk(nc, x, mem, norm_mix_g, w_in, w_gla_a2, b_gla_a, gla_norm_g, diff_norm_g, lambda_q1, lambda_k1,
          lambda_q2, lambda_k2, w_out, norm_cross_g, norm_mem_g, w_cq, w_ckv, w_co, norm_ffn_g, w_router_grp,
          b_router_grp, w_router_exp, b_router_exp, w_e_gate, w_e_up, w_e_down, norm_final_g, out):
    x = x.rearrange("b s d -> (b s) d")
    mem = mem.rearrange("b s d -> (b s) d")
    out = out.rearrange("b s d -> (b s) d")
    w_in = w_in[0]
    mixed = nc.dram_tensor("mixed", (SEQ, D), F32).ap()
    x3 = nc.dram_tensor("x3", (SEQ, D), F32).ap()
    h4 = nc.dram_tensor("h4", (SEQ, 2 * D), F32).ap()
    ys = nc.dram_tensor("ys", (NBLK * P, D), F32).ap()
    with ExitStack() as ctx:
        sb, ps, sem = alloc(nc, ctx, "all")

        class c:
            ident = sb("ident", [P, P])
            identr = sb("identr", [P, P], F32R)
            identb = sb("identb", [P, P], BF16)
            maskb = sb("maskb", [P, P], BF16)
            half = sb("half", [P, HEADS])
            eps = sb("eps", [P, HEADS])
            g_mix = sb("g_mix", [P, KC])
            g_cross = sb("g_cross", [P, KC])
            g_mem = sb("g_mem", [P, KC])
        c.gains = [(c.g_mix[:], norm_mix_g[0].rearrange("(k p) -> p k", p=P)),
                   (c.g_cross[:], norm_cross_g[0].rearrange("(k p) -> p k", p=P)),
                   (c.g_mem[:], norm_mem_g[0].rearrange("(k p) -> p k", p=P))]
        constants(nc, c)
        with ExitStack() as mix:
            hT = mix.enter_context(nc.sbuf_tensor("hT", [P, KC, SEQ], F32))
            norm_phase(nc, c, x, hT)
            gla_phase(nc, c, hT, w_in, w_gla_a2[0], b_gla_a[0], gla_norm_g[0], mixed)
            diff_phase(nc, c, hT, w_in, diff_norm_g[0], (lambda_q1[0], lambda_k1[0], lambda_q2[0], lambda_k2[0]), mixed)
        with ExitStack() as cross:
            logits = cross.enter_context(nc.sbuf_tensor("logits", [P, NT, GROUPS + EXPERTS], F32))
            with ExitStack() as fold:
                wqk = fold.enter_context(nc.sbuf_tensor("wqk", [P, KC, D], F32))
                wvo = fold.enter_context(nc.sbuf_tensor("wvo", [P, KC, D], F32))
                memory_phase(nc, c, mem, w_cq[0], w_ckv[0], w_co[0], wqk, wvo)
                cross_phase(nc, c, x, mixed, w_out[0], wqk, wvo, w_router_grp[0], w_router_exp[0],
                            norm_ffn_g[0], x3, h4, logits)
            dest = cross.enter_context(nc.sbuf_tensor("dest", [P, NT, 2], I32))
            gate = cross.enter_context(nc.sbuf_tensor("gate", [P, NT, 2], F32))
            rows = cross.enter_context(nc.sbuf_tensor("rows", [P, NBLK], I32))
            table = cross.enter_context(nc.sbuf_tensor("table", [P, TOTAL + 1], I32))
            route_phase(nc, c, b_router_grp[0], b_router_exp[0], logits, dest, gate, rows, table)
            expert_phase(nc, c, h4, w_e_gate[0], w_e_up[0], w_e_down[0], rows, table, ys)
            combine_phase(nc, c, x3, ys, dest, gate, norm_final_g, out)


_INS = ["x", "mem", "norm_mix_g", "w_in", "w_gla_a2", "b_gla_a", "gla_norm_g", "diff_norm_g", "lambda_q1",
        "lambda_k1", "lambda_q2", "lambda_k2", "w_out", "norm_cross_g", "norm_mem_g", "w_cq", "w_ckv", "w_co",
        "norm_ffn_g", "w_router_grp", "b_router_grp", "w_router_exp", "b_router_exp", "w_e_gate", "w_e_up",
        "w_e_down", "norm_final_g"]


def kernel(**inputs):
    import numpy as _np
    import concourse.bacc as _bacc
    from concourse.bass_utils import run_bass_kernel_spmd as _run

    nc = _bacc.Bacc("TRN2", target_bir_lowering=False, num_devices=1)
    arrays, args = {}, []
    for name in _INS:
        a = _np.ascontiguousarray(inputs[name])
        arrays[f"in_{name}"] = a
        args.append(nc.dram_tensor(f"in_{name}", a.shape, mybir.dt.from_np(a.dtype), kind="ExternalInput").ap())
    out = nc.dram_tensor("out", (1, SEQ, D), F32, kind="ExternalOutput").ap()
    trunk(nc, *args, out)
    r = _run(nc, [arrays], core_ids=[0])
    return r.results[0]["out"]
```

```python
from contextlib import ExitStack

import concourse.bass as bass
from concourse import mybir

F32 = mybir.dt.float32
F32R = mybir.dt.float32r
BF16 = mybir.dt.bfloat16
I32 = mybir.dt.int32
U8 = mybir.dt.uint8
ALU = mybir.AluOpType
ACT = mybir.ActivationFunctionType
AX = mybir.AxisListType.X

P = 128
D = 1024
KC = D // P
SEQ = 2048
NT = SEQ // P
HEADS = 4
GLA_DK, DV, CHUNK, RANK = 64, 128, 64, 16
GLA_QK, GLA_V = HEADS * GLA_DK, HEADS * DV
DQK = 64
MEM = 256
DH = D // HEADS
GROUPS, PER_GROUP = 4, 4
EXPERTS = GROUPS * PER_GROUP
DE = 512
NBLK = (2 * SEQ + EXPERTS * (P - 1)) // P
EPS = 1e-6
LAMBDA_INIT = 0.2
NEG = -1e30
CQ, CK = 0, GLA_QK
CV = 2 * GLA_QK
CA = CV + GLA_V
CR = CA + RANK
CDQ = CR + GLA_V
CDK = CDQ + HEADS * 2 * DQK
CDV = CDK + HEADS * 2 * DQK


def alloc(nc, ctx, phase):
    sems = []

    def sb(name, shape, dt=F32):
        return ctx.enter_context(nc.sbuf_tensor(f"{phase}_{name}", shape, dt))

    def ps(name, shape, dt=F32):
        return ctx.enter_context(nc.psum_tensor(f"{phase}_{name}", shape, dt))

    def sem(name):
        sems.append(nc.alloc_semaphore(name=f"{phase}_{name}"))
        return sems[-1]

    def clear():
        if sems:
            nc.clear_and_free_semaphores(sems)
            nc.all_engine_barrier()

    ctx.callback(clear)
    return sb, ps, sem


class Order:

    def __init__(self, eng, sem):
        self.eng, self.sem, self.base, self.n = eng, sem, 0, 0

    def at(self, base):
        self.base, self.n = base, 0

    def __call__(self, ins):
        self.n += 1
        ins.then_inc(self.sem, 1)
        self.eng.wait_ge(self.sem, self.base + self.n)


def constants(nc, c):
    with ExitStack() as ctx:
        _, _, sem = alloc(nc, ctx, "const")
        made, loaded = sem("const_made"), sem("gains_loaded")
        with nc.Block() as block:
            @block.gpsimd
            def _(pool):
                o = Order(pool, made)
                o(pool.memset(c.ident[:], 0.0))
                o(pool.affine_select(out=c.ident[:], in_=c.ident[:], compare_op=ALU.not_equal, fill=1.0,
                                     base=0, pattern=[[-1, P]], channel_multiplier=1))
                o(pool.tensor_copy(c.identb[:], c.ident[:]))
                o(pool.tensor_copy(c.identr[:], c.ident[:]))
                o(pool.memset(c.maskb[:], 0.0))
                o(pool.affine_select(out=c.maskb[:], in_=c.maskb[:], compare_op=ALU.is_ge, fill=NEG,
                                     base=0, pattern=[[-1, P]], channel_multiplier=1))
                o(pool.memset(c.half[:], -0.5))
                o(pool.memset(c.eps[:], EPS))

            @block.sync
            def _(sp):
                n = 0
                for tile, gain in c.gains:
                    with nc.allow_non_contiguous_dma("small column loads"):
                        sp.dma_start(tile, gain).then_inc(loaded, 16)
                    n += 1
                sp.wait_ge(loaded, 16 * n)


def norm_phase(nc, c, x, hT):
    B = 4
    with ExitStack() as ctx:
        sb, ps, sem = alloc(nc, ctx, "norm")
        xin = [sb(f"xin{u}", [P, D]) for u in range(B)]
        xn = [sb(f"xn{u}", [P, D]) for u in range(2)]
        sq = sb("sq", [P, B, D], BF16)
        ss, ms, rs = (sb(n, [P, B]) for n in ("ss", "ms", "rs"))
        tp = [[ps(f"tp{u}{k}", [P, 4, P]) for k in range(2)] for u in range(2)]
        x_in = [sem(f"x_in{u}") for u in range(B)]
        x_free, sum_ok, rs_ok, xn_ok = (sem(n) for n in ("x_free", "sum_ok", "rs_ok", "xn_ok"))
        turned, low_out, high_out, ms_ok = (sem(n) for n in ("turned", "low_out", "high_out", "ms_ok"))

        def steps(eng, step):
            with eng.Fori(0, NT // B - 1) as quad:
                for u in range(B):
                    step(B * quad + u, u, quad, True)
            for u in range(B):
                step(NT - B + u, u, NT // B - 1, u < B - 1)

        with nc.Block() as block:
            @block.sync
            def _(sp):
                with sp.Fori(0, NT // B) as quad:
                    for u in range(B):
                        t = B * quad + u
                        sp.wait_ge(x_free, t + 1)
                        sp.dma_start(xin[u][:], x[bass.ds(t * P, P), :]).then_inc(x_in[u], 16)

            @block.scalar
            def _(act):
                def square(t, u, quad):
                    act.wait_ge(x_in[u], 16 * (quad + 1))
                    act.activation(sq[:, u, :], xin[u][:], ACT.Square, scale=D ** -0.5,
                                   accum_out=ss[:, u:u + 1]).then_inc(sum_ok, 1)

                def step(t, u, quad, more):
                    if more:
                        square(t + 1, (u + 1) % B, quad + (u + 1) // B)
                    act.wait_ge(turned, 2 * t + 3)
                    for k in range(4):
                        last = act.activation(hT[:, 4 + k, bass.ds(t * P, P)], tp[u % 2][1][:, k, :], ACT.Copy,
                                              scale=c.g_mix[:, 4 + k:5 + k])
                    last.then_inc(high_out, 1)

                square(0, 0, 0)
                steps(act, step)

            @block.gpsimd
            def _(pool):
                with pool.Fori(0, NT // B) as quad:
                    for u in range(B):
                        t = B * quad + u
                        col = slice(u, u + 1)
                        pool.wait_ge(sum_ok, t + 1)
                        pool.tensor_tensor(ms[:, col], ss[:, col], c.eps[:, 0:1], ALU.add).then_inc(ms_ok, 1)
                        pool.wait_ge(ms_ok, t + 1)
                        pool.tensor_tensor(rs[:, col], ms[:, col], c.half[:, 0:1], ALU.pow).then_inc(rs_ok, 1)

            @block.vector
            def _(dve):
                def scale(t, u):
                    dve.wait_ge(rs_ok, t + 1)
                    dve.tensor_scalar(xn[u % 2][:], xin[u][:], rs[:, u:u + 1], None, ALU.mult).then_inc(xn_ok, 1)

                def step(t, u, quad, more):
                    if more:
                        dve.wait_ge(turned, 2 * t + 1)
                        scale(t + 1, (u + 1) % B)
                    dve.wait_ge(turned, 2 * t + 2)
                    dve.tensor_tensor(hT[:, 0:4, bass.ds(t * P, P)], tp[u % 2][0][:],
                                      c.g_mix[:, 0:4].unsqueeze(2).to_broadcast([P, 4, P]), ALU.mult).then_inc(low_out, 1)
                    if more:
                        dve.wait_ge(xn_ok, t + 2)
                        dve.sem_inc(x_free, 1)

                dve.sem_inc(x_free, B)
                scale(0, 0)
                dve.wait_ge(xn_ok, 1)
                dve.sem_inc(x_free, 1)
                steps(dve, step)

            @block.tensor
            def _(pe):
                pe.sem_inc(turned, 1)
                pe.sem_inc(low_out, 2)
                pe.sem_inc(high_out, 2)
                with pe.Fori(0, NT // 2) as pair:
                    for u in range(2):
                        t = 2 * pair + u
                        pe.wait_ge(xn_ok, t + 1)
                        pe.wait_ge(low_out, t + 1)
                        pe.wait_ge(high_out, t + 1)
                        for k in range(KC):
                            last = pe.transpose(tp[u][k // 4][:, k % 4, :], xn[u][:, k * P:(k + 1) * P], c.ident[:])
                            if k % 4 == 3:
                                last.then_inc(turned, 1)




def gate_phase(nc, c, hT, w_in, w_a2, b_a, ep, en, decay, preload):
    N = 512
    with ExitStack() as ctx:
        sb, ps, sem = alloc(nc, ctx, "gate")
        wa, wa2, bcol = sb("wa", [P, KC, RANK]), sb("wa2", [RANK, GLA_QK]), sb("bcol", [P, 2])
        low = sb("low", [RANK, 2, N])
        cum, keep = sb("cum", [P, 2, SEQ]), sb("keep", [P, SEQ])
        lowps, zps = ps("lowps", [RANK, 2, N]), ps("zps", [P, 4, N])
        wa_in, low_mm, low_out, z_mm, z_out = (sem(n) for n in ("wa_in", "low_mm", "low_out", "z_mm", "z_out"))
        keep_ok, mag_ok, soft_ok, sums_ok, exps_ok = (sem(n) for n in ("keep_ok", "mag_ok", "soft_ok", "sums_ok", "exps_ok"))
        dve_step, act_step = sem("dve_step"), sem("act_step")
        z, soft = ep, en
        with nc.Block() as block:
            @block.sync
            def _(sp):
                with nc.allow_non_contiguous_dma("16 columns of w_in; a bias as columns"):
                    sp.dma_start(wa[:], w_in[:, CA:CA + RANK].rearrange("(k p) r -> p k r", p=P)).then_inc(wa_in, 16)
                    sp.dma_start(wa2[:], w_a2).then_inc(wa_in, 16)
                    sp.dma_start(bcol[:], b_a.rearrange("(k p) -> p k", p=P)).then_inc(wa_in, 16)
                preload(sp)

            @block.gpsimd
            def _(pool):
                pool.memset(keep[:], 1.0).then_inc(keep_ok, 1)
                pool.wait_ge(keep_ok, 1)
                pool.memset(keep[:].rearrange("p (n s) -> p n s", s=CHUNK)[:, :, 0:1], 0.0).then_inc(keep_ok, 1)

            @block.tensor
            def _(pe):
                def gate_input(g):
                    pe.wait_ge(low_out, g + 1)
                    for pair in range(2):
                        last = pe.matmul(zps[:, 2 * (g % 2) + pair, :], wa2[:, pair * P:(pair + 1) * P], low[:, g % 2, :],
                                         start=True, stop=True)
                    last.then_inc(z_mm, 1)

                pe.wait_ge(wa_in, 48)
                for g in range(SEQ // N):
                    if g >= 2:
                        pe.wait_ge(low_out, g - 1)
                    for k in range(KC):
                        last = pe.matmul(lowps[:, g % 2, :], wa[:, k, :], hT[:, k, g * N:(g + 1) * N],
                                         start=(k == 0), stop=(k == KC - 1))
                    last.then_inc(low_mm, 1)
                    if g >= 1:
                        if g >= 3:
                            pe.wait_ge(z_out, g - 2)
                        gate_input(g - 1)
                pe.wait_ge(z_out, 2)
                gate_input(SEQ // N - 1)

            @block.scalar
            def _(act):
                for g in range(SEQ // N):
                    act.wait_ge(low_mm, g + 1)
                    if g >= 2:
                        act.wait_ge(z_mm, g - 1)
                    act.activation(low[:, g % 2, :], lowps[:, g % 2, :], ACT.Copy).then_inc(low_out, 1)
                act.wait_ge(mag_ok, 1)
                act.activation(soft[:], soft[:], ACT.Exp).then_inc(act_step, 1)
                act.wait_ge(act_step, 1)
                act.activation(soft[:], soft[:], ACT.Ln, bias=1.0).then_inc(soft_ok, 1)
                for pair in range(2):
                    act.wait_ge(sums_ok, pair + 1)
                    act.activation(ep[:, pair, :], cum[:, pair, :], ACT.Exp, scale=1.0 / 16.0).then_inc(exps_ok, 1)
                    act.activation(en[:, pair, :], cum[:, pair, :], ACT.Exp, scale=-1.0 / 16.0)

            @block.vector
            def _(dve):
                o = Order(dve, dve_step)
                dve.wait_ge(wa_in, 48)
                for g in range(SEQ // N):
                    dve.wait_ge(z_mm, g + 1)
                    for pair in range(2):
                        last = dve.tensor_scalar(z[:, pair, g * N:(g + 1) * N], zps[:, 2 * (g % 2) + pair, :],
                                                 bcol[:, pair:pair + 1], None, ALU.add)
                    last.then_inc(z_out, 1)
                dve.wait_ge(z_out, SEQ // N)
                o(dve.tensor_scalar(cum[:], z[:], 0.0, None, ALU.min))
                o(dve.tensor_tensor(z[:], cum[:], z[:], ALU.subtract))
                dve.tensor_tensor(soft[:], z[:], cum[:], ALU.add).then_inc(mag_ok, 1)
                dve.wait_ge(soft_ok, 1)
                o(dve.tensor_tensor(z[:], cum[:], soft[:], ALU.subtract))
                dve.wait_ge(keep_ok, 2)
                for pair in range(2):
                    dve.tensor_tensor_scan(cum[:, pair, :], keep[:], z[:, pair, :], 0.0, ALU.mult,
                                           ALU.add).then_inc(sums_ok, 1)
                dve.wait_ge(exps_ok, 2)
                ends = ep[:].rearrange("p a (t n s) -> p a t n s", n=2, s=CHUNK)
                for half in range(2):
                    for chunk in range(2):
                        dve.tensor_copy(decay[chunk * 64:chunk * 64 + 64, half::2, :],
                                        ends[half * 64:half * 64 + 64, :, :, chunk, CHUNK - 1])


def gla_phase(nc, c, hT, w_in, w_a2, b_a, gain, mixed):
    with ExitStack() as outer:
        sb, ps, sem = alloc(nc, outer, "gla")
        ep, en = sb("ep", [P, 2, SEQ]), sb("en", [P, 2, SEQ])
        decay = sb("decay", [P, HEADS, NT])
        wqk, wvr, gb = sb("w_qk", [P, KC, 2 * GLA_QK]), sb("w_vr", [P, KC, 2 * GLA_V]), sb("gb", [P, DV])
        w_in_ok = sem("w_in_ok")

        def load_weights(sp):
            kin = w_in.rearrange("(k p) n -> p k n", p=P)
            sp.dma_start(wvr[:, :, 0:GLA_V], kin[:, :, CV:CV + GLA_V]).then_inc(w_in_ok, 16)
            sp.dma_start(wvr[:, :, GLA_V:], kin[:, :, CR:CR + GLA_V]).then_inc(w_in_ok, 16)
            sp.dma_start(wqk[:], kin[:, :, CQ:CQ + 2 * GLA_QK]).then_inc(w_in_ok, 16)
            sp.dma_start(gb[:], gain.partition_broadcast(P)).then_inc(w_in_ok, 16)

        gate_phase(nc, c, hT, w_in, w_a2, b_a, ep, en, decay, load_weights)
        hs = sb("hs", [P, KC, P])
        qe = [sb(f"qe{u}", [P, 2, P]) for u in range(2)]
        ke = [sb(f"ke{u}", [P, 2, P]) for u in range(2)]
        ks = [sb(f"ks{u}", [P, 2, P]) for u in range(2)]
        q2 = [sb(f"q2{u}", [P, HEADS, P]) for u in range(2)]
        k2 = [sb(f"k2{u}", [P, HEADS, P]) for u in range(2)]
        at = [sb(f"at{u}", [P, 2, 2, P]) for u in range(2)]
        v = [sb(f"v{u}", [P, GLA_V]) for u in range(2)]
        gs = [sb(f"gs{u}", [P, GLA_V]) for u in range(2)]
        st = [sb(f"st{u}", [P, HEADS, DV]) for u in range(2)]
        fin = [sb(f"fin{u}", [P, GLA_V]) for u in range(2)]
        sq, tmp = sb("sq", [P, GLA_V]), sb("tmp", [P, HEADS, DV])
        seen = sb("seen", [P, P], I32)
        ss = [sb(f"ss{u}", [P, HEADS]) for u in range(2)]
        ms = [sb(f"ms{u}", [P, HEADS]) for u in range(2)]
        rs = [sb(f"rs{u}", [P, HEADS]) for u in range(2)]
        qkps, vps, rps = ps("qkps", [P, 4, P]), ps("vps", [P, GLA_V]), ps("rps", [P, GLA_V])
        aps, ktps = ps("aps", [P, 2, 512]), ps("ktps", [P, HEADS, GLA_DK])
        kvps, ops = ps("kvps", [P, HEADS, DV]), ps("ops", [P, HEADS, DV])

        set_ok, pool_set = sem("set_ok"), sem("pool_set")
        staged, pool_go = sem("staged"), sem("pool_go")
        vr_mm, qk_mm = sem("vr_mm"), sem("qk_mm")
        v_out, r_out, gated = sem("v_out"), sem("r_out"), sem("gated")
        qk_out, split_q, split_k = sem("qk_out"), sem("split_q"), sem("split_k")
        scores, turned, masked = sem("scores"), sem("turned"), sem("masked")
        kv_mm, mid_ok, carried = sem("kv_mm"), sem("mid_ok"), sem("carried")
        o_mm, sq_ok, sum_ok, eps_ok, rs_ok = sem("o_mm"), sem("sq_ok"), sem("sum_ok"), sem("eps_ok"), sem("rs_ok")
        o_out, finished, dve_step, dve_go = sem("o_out"), sem("finished"), sem("dve_step"), sem("dve_go")
        stored = [sem(f"stored{u}") for u in range(2)]

        with nc.Block() as block:
            @block.sync
            def _(sp):
                def store(t, u):
                    sp.wait_ge(finished, t + 2)
                    sp.dma_start(mixed[bass.ds(t * P, P), 0:GLA_V], fin[u][:]).then_inc(stored[u], 16)

                with sp.Fori(0, NT // 2) as pair:
                    for u in range(2):
                        store(2 * pair + u, u)
                for u in range(2):
                    sp.wait_ge(stored[u], 16 * (NT // 2))

            @block.gpsimd
            def _(pool):
                o = Order(pool, pool_set)
                o(pool.memset(seen[:], 1))
                o(pool.affine_select(out=seen[:], in_=seen[:], compare_op=ALU.is_ge, fill=0, base=0,
                                     pattern=[[1, P]], channel_multiplier=-1))
                o(pool.memset(seen[0:CHUNK, CHUNK:], 0))
                for u in range(2):
                    pool.memset(q2[u][:], 0.0)
                    pool.memset(k2[u][:], 0.0)
                    o(pool.memset(at[u][:], 0.0))
                o(pool.memset(st[0][:], 0.0))
                pool.sem_inc(set_ok, 1)
                pool.sem_inc(gated, 1)
                pool.wait_ge(w_in_ok, 64)

                def stage(t):
                    pool.wait_ge(qk_mm, t)
                    pool.sem_inc(pool_go, 1)
                    pool.tensor_copy(hs[:], hT[:, :, bass.ds(t * P, P)]).then_inc(staged, 1)

                def gate(t, u):
                    pool.wait_ge(r_out, t + 2)
                    pool.tensor_tensor(gs[u][:].rearrange("p (h e) -> p h e", e=DV),
                                       gs[u][:].rearrange("p (h e) -> p h e", e=DV),
                                       gb[:].unsqueeze(1).to_broadcast([P, HEADS, DV]), ALU.mult).then_inc(gated, 1)

                def rsqrt(t, u):
                    pool.wait_ge(sum_ok, t + 1)
                    pool.tensor_tensor(ms[u][:], ss[u][:], c.eps[:], ALU.add).then_inc(eps_ok, 1)
                    pool.wait_ge(eps_ok, t + 1)
                    pool.tensor_tensor(rs[u][:], ms[u][:], c.half[:], ALU.pow).then_inc(rs_ok, 1)

                pool.tensor_copy(hs[:], hT[:, :, 0:P]).then_inc(staged, 1)
                gate(0, 0)
                stage(1)
                with pool.Fori(0, NT // 2 - 1) as pair:
                    for u in range(2):
                        t = 2 * pair + u
                        gate(t + 1, 1 - u)
                        stage(t + 2)
                        rsqrt(t, u)
                gate(NT - 1, 1)
                rsqrt(NT - 2, 0)
                rsqrt(NT - 1, 1)

            @block.scalar
            def _(act):
                act.sem_inc(v_out, 1)
                act.sem_inc(r_out, 1)
                act.wait_ge(set_ok, 1)

                def values(t, u):
                    act.wait_ge(vr_mm, t + 1)
                    act.activation(v[u][:], vps[:], ACT.Copy).then_inc(v_out, 1)
                    act.activation(gs[u][:], rps[:], ACT.Silu).then_inc(r_out, 1)

                def split(t, u):
                    act.wait_ge(qk_out, t + 2)
                    for half in range(2):
                        for chunk in range(2):
                            cols = slice(chunk * CHUNK, (chunk + 1) * CHUNK)
                            last = act.activation(q2[u][chunk * 64:chunk * 64 + 64, half::2, cols],
                                                  qe[u][half * 64:half * 64 + 64, :, cols], ACT.Copy)
                    last.then_inc(split_q, 1)

                def square(t):
                    act.wait_ge(o_mm, t + 1)
                    act.wait_ge(finished, t + 1)
                    act.activation(sq[:], ops[:].rearrange("p h e -> p (h e)"), ACT.Square,
                                   scale=DV ** -0.5).then_inc(sq_ok, 1)

                values(0, 0)
                split(0, 0)
                with act.Fori(0, NT // 2 - 1) as pair:
                    for u in range(2):
                        t = 2 * pair + u
                        act.wait_ge(finished, t + 1)
                        values(t + 1, 1 - u)
                        split(t + 1, 1 - u)
                        square(t)
                act.wait_ge(finished, NT - 1)
                values(NT - 1, 1)
                split(NT - 1, 1)
                square(NT - 2)
                square(NT - 1)

            @block.vector
            def _(dve):
                for s in (masked, split_k, carried, qk_out, o_out, finished):
                    dve.sem_inc(s, 1)
                dve.wait_ge(set_ok, 1)
                o = Order(dve, dve_step)

                def project_out(t, u):
                    dve.wait_ge(qk_mm, t + 1)
                    here = bass.ds(t * P, P)
                    dve.scalar_tensor_tensor(out=qe[u][:], in0=qkps[:, 0:2, :], scalar=GLA_DK ** -0.5,
                                             in1=ep[:, :, here], op0=ALU.mult, op1=ALU.mult)
                    o(dve.tensor_tensor(ke[u][:], qkps[:, 2:4, :], en[:, :, here], ALU.mult))
                    for pair in range(2):
                        ends = ep[:, pair, here].rearrange("p (n s) -> p n s", s=CHUNK)[:, :, CHUNK - 1:CHUNK]
                        last = dve.tensor_tensor(ks[u][:, pair, :].rearrange("p (n s) -> p n s", s=CHUNK),
                                                 ke[u][:, pair, :].rearrange("p (n s) -> p n s", s=CHUNK),
                                                 ends.to_broadcast([P, 2, CHUNK]), ALU.mult)
                    last.then_inc(qk_out, 1)

                def chunk_work(t, u):
                    dve.wait_ge(scores, t + 1)
                    dve.sem_inc(dve_go, 1)
                    dve.copy_predicated(at[u][:].rearrange("p a b q -> p (a b) q"),
                                        seen[:].unsqueeze(1).to_broadcast([P, 4, P]),
                                        aps_view).then_inc(masked, 1)
                    dve.wait_ge(turned, t + 1)
                    dve.tensor_copy(k2[u][0:CHUNK, :, 0:64], ktps[0:CHUNK, :, :])
                    dve.tensor_copy(k2[u][CHUNK:P, :, 64:P], ktps[CHUNK:P, :, :]).then_inc(split_k, 1)

                def decayed(lo, t, u):
                    return dve.tensor_tensor(tmp[lo:lo + 64, :, :], st[u][lo:lo + 64, :, :],
                                             decay_now(t)[lo:lo + 64].to_broadcast([64, HEADS, DV]), ALU.mult)

                def decay_now(t):
                    return decay[:, :, bass.ds(t, 1)]

                def middle(t, u):
                    dve.wait_ge(kv_mm, t + 1)
                    o(decayed(0, t, u))
                    dve.tensor_tensor(st[u][64:P, :, :], tmp[0:64, :, :], kvps[0:64, :, :], ALU.add).then_inc(mid_ok, 1)

                def carry(t, u):
                    dve.wait_ge(mid_ok, t + 1)
                    o(decayed(64, t, u))
                    dve.tensor_tensor(st[1 - u][0:64, :, :], tmp[64:P, :, :], kvps[64:P, :, :], ALU.add).then_inc(carried, 1)
                    dve.wait_ge(carried, t + 2)

                def finish(t, u, pair):
                    dve.wait_ge(sq_ok, t + 1)
                    dve.tensor_reduce(ss[u][:], sq[:].rearrange("p (h e) -> p h e", e=DV), AX, ALU.add).then_inc(sum_ok, 1)
                    dve.wait_ge(rs_ok, t + 1)
                    dve.wait_ge(gated, t + 2)
                    if pair is not None:
                        dve.wait_ge(stored[u], 16 * pair)
                    dve.tensor_tensor(fin[u][:].rearrange("p (h e) -> p h e", e=DV), ops[:],
                                      rs[u][:].unsqueeze(2).to_broadcast([P, HEADS, DV]), ALU.mult).then_inc(o_out, 1)
                    dve.wait_ge(o_out, t + 2)
                    dve.tensor_tensor(fin[u][:], fin[u][:], gs[u][:], ALU.mult).then_inc(finished, 1)

                aps_view = aps[:, :, 0:2 * P].rearrange("p a (b q) -> p a b q", b=2)

                def step(t, u, pair, last=False):
                    chunk_work(t, u)
                    middle(t, u)
                    if not last:
                        project_out(t + 1, 1 - u)
                    carry(t, u)
                    finish(t, u, pair)

                project_out(0, 0)
                step(0, 0, None)
                step(1, 1, None)
                with dve.Fori(1, NT // 2 - 1) as pair:
                    for u in range(2):
                        o.at(1 + 3 * (2 * pair + u))
                        step(2 * pair + u, u, pair)
                o.at(1 + 3 * (NT - 2))
                step(NT - 2, 0, NT // 2 - 1)
                step(NT - 1, 1, NT // 2 - 1, last=True)

            @block.tensor
            def _(pe):
                def values(t):
                    pe.wait_ge(staged, t + 1)
                    pe.wait_ge(v_out, t + 1)
                    pe.wait_ge(r_out, t + 1)
                    for k in range(KC):
                        pe.matmul(vps[:], hs[:, k, :], wvr[:, k, 0:GLA_V], start=(k == 0), stop=(k == KC - 1))
                    for k in range(KC):
                        last = pe.matmul(rps[:], hs[:, k, :], wvr[:, k, GLA_V:], start=(k == 0), stop=(k == KC - 1))
                    last.then_inc(vr_mm, 1)

                def queries(t):
                    pe.wait_ge(qk_out, t + 1)
                    for m in range(4):
                        for k in range(KC):
                            last = pe.matmul(qkps[:, m, :], wqk[:, k, m * P:(m + 1) * P], hs[:, k, :],
                                             start=(k == 0), stop=(k == KC - 1))
                    last.then_inc(qk_mm, 1)

                def score(t, u):
                    pe.wait_ge(qk_out, t + 2)
                    pe.wait_ge(masked, t + 1)
                    for half in range(2):
                        rows = slice(half * 64, half * 64 + 64)
                        for pair in range(2):
                            last = pe.matmul(aps[:, half, pair * P:(pair + 1) * P], ke[u][rows, pair, :],
                                             qe[u][rows, pair, :], start=True, stop=True)
                    last.then_inc(scores, 1)
                    pe.wait_ge(split_k, t + 1)
                    for pair in range(2):
                        last = pe.transpose(ktps[:, 2 * pair:2 * pair + 2, :].rearrange("p h d -> p (h d)"), ks[u][:, pair, :],
                                            c.ident[:])
                    last.then_inc(turned, 1)

                def outer_products(t, u):
                    pe.wait_ge(split_k, t + 2)
                    pe.wait_ge(v_out, t + 2)
                    pe.wait_ge(carried, t + 1)
                    for h in range(HEADS):
                        last = pe.matmul(kvps[:, h, :], k2[u][:, h, :], v[u][:, h * DV:(h + 1) * DV], start=True, stop=True)
                    last.then_inc(kv_mm, 1)

                def outputs(t, u):
                    pe.wait_ge(masked, t + 2)
                    pe.wait_ge(split_q, t + 1)
                    pe.wait_ge(mid_ok, t + 1)
                    pe.wait_ge(o_out, t + 1)
                    for h in range(HEADS):
                        pe.matmul(ops[:, h, :], at[u][:, h % 2, h // 2, :], v[u][:, h * DV:(h + 1) * DV],
                                  start=True, stop=False)
                        last = pe.matmul(ops[:, h, :], q2[u][:, h, :], st[u][:, h, :], start=False, stop=True)
                    last.then_inc(o_mm, 1)

                def step(t, u, last=False):
                    score(t, u)
                    if not last:
                        values(t + 1)
                    outer_products(t, u)
                    if not last:
                        queries(t + 1)
                    outputs(t, u)

                pe.wait_ge(set_ok, 1)
                pe.wait_ge(w_in_ok, 64)
                values(0)
                queries(0)
                with pe.Fori(0, NT // 2 - 1) as pair:
                    for u in range(2):
                        step(2 * pair + u, u)
                step(NT - 2, 0)
                step(NT - 1, 1, last=True)


def diff_phase(nc, c, hT, w_in, gain, lambdas, mixed):
    W = 512
    BANKS = 4

    def chunks(i):
        return (i * P + P + W - 1) // W

    def first(i):
        return sum(chunks(j) for j in range(i))

    def scaled_first(i):
        return sum(chunks(j) for j in range(i) if chunks(j) > 1)

    def steps(i):
        score = [("S", m, k) for m in range(2) for k in range(chunks(i))] if i < NT else []
        turns = chunks(i - 1) if i >= 1 else 0
        n, out, j = len(score), [], 0
        for x in range(n + 1):
            while j < turns and x >= min(n, 3 + -(-j * (n - 3) // turns)):
                out.append(("T", j))
                j += 1
            if x < n:
                out.append(score[x])
        return out

    def width(i, k):
        return min(W, (i + 1) * P - k * W)

    ALL = first(NT)
    assert (2 * ALL) % BANKS == 0 and ALL % 4 == 0
    SCALED = scaled_first(NT)
    MANY = sum(chunks(i) > 1 for i in range(NT))
    jobs = [(w, g) for g in range(4) for w in "qk"] + [("v", g) for g in range(4)]
    QK = 8
    hi_rows = [slice(0, 64), slice(64, 128)]
    lo_rows = [slice(64, 128), slice(0, 64)]

    with ExitStack() as ctx:
        sb, ps, sem = alloc(nc, ctx, "diff")
        wd = sb("wd", [P, KC, 3, P])
        qa = [sb(f"qa{m}", [P, SEQ], F32R) for m in range(2)]
        ka = [sb(f"ka{m}", [P, SEQ], F32R) for m in range(2)]
        qb = [sb(f"qb{m}", [P, SEQ], F32R) for m in range(2)]
        kb = [sb(f"kb{m}", [P, SEQ], F32R) for m in range(2)]
        v = sb("v", [P, NT, DV])
        pr = [[sb(f"pr{u}{m}", [P, SEQ]) for m in range(2)] for u in range(2)]
        aT = sb("aT", [P, 4, 4, P])
        qmul, kmul = sb("qmul", [P, 1]), sb("kmul", [P, 1])
        lam, lsum, lexp, neglam = sb("lam", [P, 4, DQK]), sb("lsum", [P, 2]), sb("lexp", [P, 2]), sb("neglam", [P, 1])
        lprod, ldif = sb("lprod", [P, DQK]), sb("ldif", [P, 1])
        gd, gdb, part = sb("gd", [P, DV]), sb("gdb", [P, DV]), sb("part", [P, 1])
        nmx = [sb(f"nmx{u}", [P, 2, 4]) for u in range(2)]
        ntop = [sb(f"ntop{u}", [P, 2]) for u in range(2)]
        ls = [sb(f"ls{u}", [P, 2, 4]) for u in range(2)]
        e = [sb(f"e{u}", [P, 2, 4]) for u in range(2)]
        le, w1 = sb("le", [P, 2, 4]), sb("w1", [P, 4])
        l = [sb(f"l{u}", [P, 2]) for u in range(2)]
        r = [sb(f"r{u}", [P, 2]) for u in range(2)]
        mixw = [sb(f"mixw{u}", [P, 1]) for u in range(2)]
        sq = [sb(f"sq{u}", [P, DV]) for u in range(2)]
        ss = [sb(f"ss{u}", [P, 1]) for u in range(2)]
        f = [[sb(f"f{u}{n}", [P, 1]) for n in range(4)] for u in range(2)]
        fin = [sb(f"fin{u}", [P, DV]) for u in range(2)]
        sps, tps, ops = ps("sps", [P, BANKS, W]), ps("tps", [P, 2, 4, P]), ps("ops", [P, 2, 512])

        small_in, ramps, lam_ok, lexp_ok, set_dve, set_pool = (sem(n) for n in (
            "small_in", "ramps", "lam_ok", "lexp_ok", "set_dve", "set_pool"))
        w_ok = sem("w_ok")
        proj_mm, hi_out, lo_out, alibi_ok = sem("proj_mm"), sem("hi_out"), sem("lo_out"), sem("alibi_ok")
        top_ok, e_ok, scaled = sem("top_ok"), sem("e_ok"), sem("scaled")
        score_mm, max_ok, exp_ok, joined = sem("score_mm"), sem("max_ok"), sem("exp_ok"), sem("joined")
        turned, a_out, pv_mm = sem("turned"), sem("a_out"), sem("pv_mm")
        sq_ok, scale_ok, finished = sem("sq_ok"), sem("scale_ok"), sem("finished")
        dve_step, pool_step = sem("dve_step"), sem("pool_step")
        stored = [sem(f"stored{u}") for u in range(2)]

        def done(h, per, n):
            return h * per + n + 1

        with nc.Block() as block:
            @block.sync
            def _(sp):
                sp.dma_start(gdb[:], gain.partition_broadcast(P)).then_inc(small_in, 16)
                for n, vec in enumerate(lambdas):
                    sp.dma_start(lam[:, n, :], vec.partition_broadcast(P)).then_inc(small_in, 16)
                kin = w_in.rearrange("(k p) n -> p k n", p=P)

                def weights(h):
                    for n, col in enumerate((CDQ, CDK, CDV)):
                        sp.dma_start(wd[:, :, n, :], kin[:, :, bass.ds(h * P + col, P)]).then_inc(w_ok, 16)

                def store(h, i):
                    sp.wait_ge(finished, done(h, NT, i + 1))
                    sp.dma_start(mixed[i * P:(i + 1) * P, bass.ds(h * DV + GLA_V, DV)], fin[i % 2][:]).then_inc(stored[i % 2], 16)

                weights(0)
                with sp.Fori(0, HEADS - 1) as h:
                    sp.wait_ge(proj_mm, done(h, len(jobs), len(jobs)))
                    weights(h + 1)
                    for i in range(NT):
                        store(h, i)
                for i in range(NT):
                    store(HEADS - 1, i)
                for u in range(2):
                    sp.wait_ge(stored[u], 16 * HEADS * NT // 2)

            @block.gpsimd
            def _(pool):
                o = Order(pool, pool_step)
                pool.sem_inc(alibi_ok, 1)
                pool.sem_inc(scale_ok, 1)
                o(pool.memset(part[:], 1.0 / DV))
                two = slice(64, 66)
                ramps_of = [(pr[m][0][two, :], qb[m][two, :], -1, 0) for m in range(2)]
                ramps_of += [(pr[m][1][two, :], kb[m][two, :], 1, 1) for m in range(2)]
                for x, _, sign, _ in ramps_of:
                    o(pool.iota(x, [[sign, SEQ]], base=0, channel_multiplier=0, allow_small_or_imprecise_dtypes=True))
                pool.memset(qmul[two, :], 1.0)
                o(pool.memset(kmul[two, :], 1.0))
                rows = [(x, SEQ, row, 1.0) for x, _, _, row in ramps_of]
                for x, n, row, fill in rows + [(qmul[two, :], 1, 1, 0.25), (kmul[two, :], 1, 0, 0.25)]:
                    o(pool.affine_select(out=x, in_=x, compare_op=ALU.not_equal, fill=fill, base=-row,
                                         pattern=[[0, n]], channel_multiplier=1))
                for x, y, _, _ in ramps_of:
                    o(pool.tensor_copy(y, x))
                START = o.n

                def scale(h, i, u):
                    pool.wait_ge(sq_ok, done(h, NT, i + 1))
                    a, b, d, out = f[u]
                    o(pool.tensor_tensor(a[:], ss[u][:], part[:], ALU.mult))
                    o(pool.tensor_tensor(b[:], a[:], c.eps[:, 0:1], ALU.add))
                    o(pool.tensor_tensor(d[:], b[:], c.half[:, 0:1], ALU.pow))
                    pool.tensor_tensor(out[:], d[:], r[u][:, 0:1], ALU.mult).then_inc(scale_ok, 1)

                with pool.Fori(0, HEADS) as h:
                    o.at(START + h * (3 * NT + 4))
                    pool.wait_ge(proj_mm, done(h, len(jobs), 1))
                    pool.wait_ge(scale_ok, done(h, NT, 0))
                    for m in range(2):
                        o(pool.tensor_tensor(qb[m][two, :], qb[m][two, :].bitcast(F32), qmul[two, :].to_broadcast([2, SEQ]), ALU.mult))
                        o(pool.tensor_tensor(kb[m][two, :], kb[m][two, :].bitcast(F32), kmul[two, :].to_broadcast([2, SEQ]), ALU.mult))
                    pool.sem_inc(alibi_ok, 1)
                    for i in range(NT):
                        scale(h, i, i % 2)

            @block.scalar
            def _(act):
                for s in (hi_out, exp_ok, e_ok, scaled, a_out, sq_ok):
                    act.sem_inc(s, 1)
                act.wait_ge(lam_ok, 1)
                act.activation(lexp[:], lsum[:], ACT.Exp).then_inc(lexp_ok, 1)

                def factors(h, i):
                    u, c = i % 2, chunks(i)
                    act.wait_ge(top_ok, done(h, MANY, i - NT + MANY + 1))
                    act.wait_ge(exp_ok, done(h, 2 * ALL, 2 * first(i + 1)))
                    for m in range(2):
                        last = act.activation(e[u][:, m, 0:c], nmx[u][:, m, 0:c], ACT.Exp, scale=-1.0, bias=ntop[u][:, m:m + 1])
                    last.then_inc(e_ok, 1)
                    act.wait_ge(e_ok, done(h, MANY, i - NT + MANY + 1))

                def scale(h, i, k):
                    u, cols = i % 2, slice(k * W, k * W + width(i, k))
                    act.activation(pr[u][0][:, cols], pr[u][0][:, cols], ACT.Copy, scale=e[u][:, 0, k:k + 1]).then_inc(scaled, 1)

                def exps(h, i, m, k):
                    u, s, w = i % 2, 2 * first(i) + m * chunks(i) + k, width(i, k)
                    act.wait_ge(max_ok, done(h, 2 * ALL, s + 1))
                    if m == k == 0:
                        act.wait_ge(turned, done(h, ALL, first(i - 1) if i >= 2 else 0))
                    act.activation(pr[u][m][:, k * W:k * W + w], sps[:, s % BANKS, 0:w], ACT.Exp,
                                   bias=nmx[u][:, m, k:k + 1], accum_out=ls[u][:, m, k:k + 1]).then_inc(exp_ok, 1)

                def copy(h, i, k):
                    g, n = first(i) + k, width(i, k) // P
                    act.wait_ge(turned, done(h, ALL, g + 1))
                    act.wait_ge(pv_mm, done(h, ALL, max(g - 3, 0)))
                    act.activation(aT[:, g % 4, 0:n, :], tps[:, g % 2, 0:n, :], ACT.Copy).then_inc(a_out, 1)

                def square(h, i):
                    u = i % 2
                    act.wait_ge(pv_mm, done(h, ALL, first(i + 1)))
                    act.wait_ge(finished, done(h, NT, max(i - 1, 0)))
                    act.activation(sq[u][:], ops[:, i % 2, 0:DV], ACT.Square, scale=r[u][:, 0:1],
                                   accum_out=ss[u][:]).then_inc(sq_ok, 1)

                with act.Fori(0, HEADS) as h:
                    for j, (what, g) in enumerate(jobs):
                        act.wait_ge(proj_mm, done(h, len(jobs), j + 1))
                        bank, cols = sps[:, j % BANKS, :], slice(g * W, (g + 1) * W)
                        if what == "v":
                            last = act.activation(v[:, 4 * g:4 * g + 4, :].rearrange("p t d -> p (t d)"), bank, ACT.Copy)
                        else:
                            by = DQK ** -0.5 if what == "q" else 1.0
                            for m in range(2):
                                part_of = bank[m * 64:m * 64 + 64, :]
                                a = (qa if what == "q" else ka)[m]
                                act.activation(a[hi_rows[m], cols], part_of, ACT.Copy, scale=by)
                                twin = qb[m][0:DQK, cols] if what == "q" else a[lo_rows[m], cols]
                                last = act.activation(twin, part_of, ACT.Copy, scale=by)
                        last.then_inc(hi_out, 1)
                    for i in range(NT + 1):
                        n = 0
                        many = 1 <= i <= NT and chunks(i - 1) > 1
                        if many:
                            factors(h, i - 1)
                        for what, *where in steps(i):
                            if many and n < chunks(i - 1) and (what == "S" or where[0] == n):
                                scale(h, i - 1, n)
                                n += 1
                            if what == "S":
                                exps(h, i, *where)
                            if many and i == NT and n < chunks(i - 1):
                                scale(h, i - 1, n)
                                n += 1
                            if what == "T":
                                copy(h, i - 1, *where)
                                if i >= 2 and where[0] == 0:
                                    square(h, i - 2)
                    square(h, NT - 1)

            @block.vector
            def _(dve):
                for s in (lo_out, max_ok, top_ok, joined, finished):
                    dve.sem_inc(s, 1)
                o = Order(dve, dve_step)
                dve.wait_ge(small_in, 16 * 5)
                for n in range(2):
                    o(dve.tensor_tensor_reduce(lprod[:], lam[:, 2 * n, :], lam[:, 2 * n + 1, :], 1.0, 0.0, ALU.mult, ALU.add,
                                               lsum[:, n:n + 1]))
                dve.sem_inc(lam_ok, 1)
                dve.wait_ge(lexp_ok, 1)
                o(dve.tensor_tensor(ldif[:], lexp[:, 1:2], lexp[:, 0:1], ALU.subtract))
                o(dve.tensor_scalar(neglam[:], ldif[:], -LAMBDA_INIT, None, ALU.add))
                o(dve.tensor_scalar(gd[:], gdb[:], 1.0 - LAMBDA_INIT, None, ALU.mult))
                START = o.n

                def maximum(h, i, m, k):
                    s = 2 * first(i) + m * chunks(i) + k
                    dve.wait_ge(score_mm, done(h, 2 * ALL, s + 1))
                    dve.tensor_reduce(nmx[i % 2][:, m, k:k + 1], sps[:, s % BANKS, 0:width(i, k)], AX, ALU.max,
                                      negate=True).then_inc(max_ok, 1)

                def row_maxima(h, i):
                    dve.wait_ge(max_ok, done(h, 2 * ALL, 2 * first(i + 1)))
                    dve.tensor_reduce(ntop[i % 2][:], nmx[i % 2][:, :, 0:chunks(i)], AX, ALU.min).then_inc(top_ok, 1)

                def weights(h, i):
                    u, c = i % 2, chunks(i)
                    dve.wait_ge(exp_ok, done(h, 2 * ALL, 2 * first(i + 1)))
                    if c > 1:
                        dve.wait_ge(e_ok, done(h, MANY, i - NT + MANY + 1))
                        o(dve.tensor_tensor(le[:, :, 0:c], ls[u][:, :, 0:c], e[u][:, :, 0:c], ALU.mult))
                        o(dve.tensor_reduce(l[u][:], le[:, :, 0:c], AX, ALU.add))
                    else:
                        o(dve.tensor_copy(l[u][:], ls[u][:, :, 0]))
                    o(dve.reciprocal(r[u][:], l[u][:]))
                    o(dve.scalar_tensor_tensor(out=mixw[u][:], in0=l[u][:, 0:1], scalar=neglam[:, 0:1], in1=r[u][:, 1:2],
                                               op0=ALU.mult, op1=ALU.mult))
                    if c > 1:
                        o(dve.tensor_scalar(w1[:, 0:c], e[u][:, 1, 0:c], mixw[u][:, 0:1], None, ALU.mult))

                def join(h, i, k):
                    u, cols = i % 2, slice(k * W, k * W + width(i, k))
                    if chunks(i) > 1:
                        dve.wait_ge(scaled, done(h, SCALED, scaled_first(i) + k + 1))
                        by = w1[:, k:k + 1]
                    else:
                        by = mixw[u][:, 0:1]
                    dve.scalar_tensor_tensor(out=pr[u][0][:, cols], in0=pr[u][1][:, cols], scalar=by,
                                             in1=pr[u][0][:, cols], op0=ALU.mult, op1=ALU.add).then_inc(joined, 1)

                def finish(h, i):
                    u = i % 2
                    dve.wait_ge(scale_ok, done(h, NT, i + 1))
                    if i >= 2:
                        dve.wait_ge(stored[u], 16 * (h * (NT // 2) + i // 2))
                    dve.scalar_tensor_tensor(out=fin[u][:], in0=ops[:, i % 2, 0:DV], scalar=f[u][3][:, 0:1], in1=gd[:],
                                             op0=ALU.mult, op1=ALU.mult).then_inc(finished, 1)

                def head(h):
                    for j, (what, g) in enumerate(jobs[:QK]):
                        dve.wait_ge(hi_out, done(h, len(jobs), j + 1))
                        cols = slice(g * W, (g + 1) * W)
                        for m in range(2):
                            part_of = sps[m * 64:m * 64 + 64, j % BANKS, :]
                            if what == "q":
                                last = dve.scalar_tensor_tensor(out=qa[m][lo_rows[m], cols], in0=part_of, scalar=DQK ** -0.5,
                                                                in1=qa[m][hi_rows[m], cols].bitcast(F32),
                                                                op0=ALU.mult, op1=ALU.subtract)
                            else:
                                last = dve.tensor_tensor(kb[m][0:DQK, cols], part_of, ka[m][hi_rows[m], cols].bitcast(F32),
                                                         ALU.subtract)
                        last.then_inc(lo_out, 1)
                    for i in range(NT + 1):
                        n = 0
                        for what, *where in steps(i):
                            if what == "S":
                                maximum(h, i, *where)
                            for _ in range(1 if i < NT else 2):
                                if i >= 1 and n < chunks(i - 1) and (what == "S" or n <= where[0] + 1):
                                    if n == 0:
                                        if i >= 3:
                                            finish(h, i - 3)
                                        weights(h, i - 1)
                                    join(h, i - 1, n)
                                    n += 1
                        if i < NT and chunks(i) > 1:
                            row_maxima(h, i)
                    for i in (NT - 2, NT - 1):
                        finish(h, i)

                head(0)
                PER = o.n - START
                with dve.Fori(1, HEADS) as h:
                    for u in range(2):
                        dve.wait_ge(stored[u], 16 * (NT // 2) * h)
                    o.at(START + h * PER)
                    head(h)

            @block.tensor
            def _(pe):
                for s in (proj_mm, score_mm, turned, pv_mm):
                    pe.sem_inc(s, 1)

                def project(h):
                    pe.wait_ge(w_ok, 48 * (h + 1))
                    pe.wait_ge(exp_ok, done(h, 2 * ALL, 0))
                    for j, (what, g) in enumerate(jobs):
                        if j >= BANKS:
                            if j - BANKS < QK:
                                pe.wait_ge(lo_out, done(h, QK, j - BANKS + 1))
                            else:
                                pe.wait_ge(hi_out, done(h, len(jobs), j - BANKS + 1))
                        bank = sps[:, j % BANKS, :]
                        if what == "v":
                            for t in range(4):
                                for k in range(KC):
                                    last = pe.matmul(bank[:, t * DV:(t + 1) * DV], hT[:, k, (4 * g + t) * P:(4 * g + t + 1) * P],
                                                     wd[:, k, 2, :], start=(k == 0), stop=(k == KC - 1))
                        else:
                            for k in range(KC):
                                last = pe.matmul(bank, wd[:, k, "qk".index(what), :], hT[:, k, g * W:(g + 1) * W],
                                                 start=(k == 0), stop=(k == KC - 1))
                        last.then_inc(proj_mm, 1)

                def score(h, i, m, k):
                    s = 2 * first(i) + m * chunks(i) + k
                    w = width(i, k)
                    if s >= BANKS:
                        pe.wait_ge(exp_ok, done(h, 2 * ALL, s - BANKS + 1))
                    bank, queries, keys = sps[:, s % BANKS, 0:w], slice(i * P, (i + 1) * P), slice(k * W, k * W + w)
                    diag = k == chunks(i) - 1
                    if diag:
                        pe.matmul(bank[:, w - P:w], c.identb[:], c.maskb[:], start=True, stop=False, skip_group_check=True)
                    pe.matmul(bank, qa[m][:, queries], ka[m][:, keys], start=not diag, stop=False, skip_group_check=diag)
                    pe.matmul(bank, qb[m][0:66, queries], kb[m][0:66, keys], start=False, stop=True,
                              skip_group_check=diag).then_inc(score_mm, 1)

                def turn(h, i, k):
                    g = first(i) + k
                    pe.wait_ge(joined, done(h, ALL, g + 1))
                    pe.wait_ge(a_out, done(h, ALL, max(g - 1, 0)))
                    for b in range(width(i, k) // P):
                        last = pe.transpose(tps[:, g % 2, b, :], pr[i % 2][0][:, k * W + b * P:k * W + (b + 1) * P], c.ident[:])
                    last.then_inc(turned, 1)

                def weigh(h, i, k):
                    g = first(i) + k
                    pe.wait_ge(a_out, done(h, ALL, g + 1))
                    if k == 0:
                        pe.wait_ge(finished, done(h, NT, max(i - 1, 0)))
                    for b in range(width(i, k) // P):
                        t = 4 * k + b
                        last = pe.matmul(ops[:, i % 2, 0:DV], aT[:, g % 4, b, :], v[:, t, :], start=(t == 0), stop=(t == i))
                    last.then_inc(pv_mm, 1)

                with pe.Fori(0, HEADS) as h:
                    project(h)
                    pe.wait_ge(hi_out, done(h, len(jobs), len(jobs)))
                    pe.wait_ge(lo_out, done(h, QK, QK))
                    pe.wait_ge(alibi_ok, done(h, 1, 1))
                    before = None
                    for i in range(NT + 1):
                        for what, *where in steps(i):
                            if what == "S":
                                score(h, i, *where)
                            else:
                                turn(h, i - 1, *where)
                                if before:
                                    weigh(h, *before)
                                before = (i - 1, *where)
                    weigh(h, *before)


def out_phase(nc, c, x, mixed, w_out, x2):
    H = 512
    with ExitStack() as ctx:
        sb, ps, sem = alloc(nc, ctx, "out")
        win = sb("win", [P, KC, D])
        w = sb("w", [P, 2, KC, D], F32R)
        mixin = [sb(f"mixin{u}", [P, D]) for u in range(2)]
        xin = [sb(f"xin{u}", [P, D]) for u in range(2)]
        x2t = [sb(f"x2t{u}", [P, D]) for u in range(2)]
        oT = [sb(f"oT{u}", [P, 2, KC, P], F32R) for u in range(2)]
        tps = ps("tps", [P, 2, H])
        acc = [ps(f"acc{u}", [P, 2, H]) for u in range(2)]
        w_in = [sem(f"w_in{k}") for k in range(KC)]
        w_hi, w_lo = sem("w_hi"), sem("w_lo")
        mix_in, x_in, stored = ([sem(f"{n}{u}") for u in range(2)] for n in ("mix_in", "x_in", "stored"))
        turned, hi_ok, lo_ok, mm_ok, x2_ok = (sem(n) for n in ("turned", "hi_ok", "lo_ok", "mm_ok", "x2_ok"))

        with nc.Block() as block:
            @block.sync
            def _(sp):
                def load(t, u):
                    rows = bass.ds(t * P, P)
                    sp.dma_start(mixin[u][:], mixed[rows, :]).then_inc(mix_in[u], 16)
                    sp.dma_start(xin[u][:], x[rows, :]).then_inc(x_in[u], 16)

                def store(t, u):
                    sp.wait_ge(x2_ok, t + 3)
                    sp.dma_start(x2[bass.ds(t * P, P), :], x2t[u][:]).then_inc(stored[u], 16)

                for u in range(2):
                    sp.sem_inc(stored[u], 16)
                load(0, 0)
                for k in range(KC):
                    sp.dma_start(win[:, k, :], w_out[k * P:(k + 1) * P, :]).then_inc(w_in[k], 16)
                load(1, 1)
                with sp.Fori(0, NT // 2 - 1) as pair:
                    for u in range(2):
                        t = 2 * pair + u
                        sp.wait_ge(turned, t + 1)
                        sp.dma_start(mixin[u][:], mixed[bass.ds((t + 2) * P, P), :]).then_inc(mix_in[u], 16)
                        store(t, u)
                        sp.dma_start(xin[u][:], x[bass.ds((t + 2) * P, P), :]).then_inc(x_in[u], 16)
                store(NT - 2, 0)
                store(NT - 1, 1)
                for u in range(2):
                    sp.wait_ge(stored[u], 16 * (NT // 2 + 1))

            @block.scalar
            def _(act):
                for k in range(KC):
                    act.wait_ge(w_in[k], 16)
                    act.activation(w[:, 0, k, :], win[:, k, :], ACT.Copy).then_inc(w_hi, 1)
                with act.Fori(0, NT // 2) as pair:
                    for u in range(2):
                        t = 2 * pair + u
                        act.wait_ge(turned, t + 1)
                        act.wait_ge(mm_ok, t + 1)
                        for b in range(2):
                            act.activation(oT[u][:, 0, 4 * b:4 * b + 4, :].rearrange("p k n -> p (k n)"), tps[:, b, :],
                                           ACT.Copy).then_inc(hi_ok, 1)

            @block.vector
            def _(dve):
                def lows(t, u):
                    for b in range(2):
                        dve.wait_ge(hi_ok, 2 * t + b + 1)
                        last = dve.tensor_tensor(oT[u][:, 1, 4 * b:4 * b + 4, :].rearrange("p k n -> p (k n)"), tps[:, b, :],
                                                 oT[u][:, 0, 4 * b:4 * b + 4, :].rearrange("p k n -> p (k n)").bitcast(F32),
                                                 ALU.subtract)
                    last.then_inc(lo_ok, 1)

                def add(t, u, pair):
                    dve.wait_ge(mm_ok, t + 3)
                    dve.wait_ge(x_in[u], 16 * (pair + 1))
                    dve.wait_ge(stored[u], 16 * (pair + 1))
                    dve.tensor_tensor(x2t[u][:], acc[u][:].rearrange("p a n -> p (a n)"), xin[u][:], ALU.add).then_inc(x2_ok, 1)

                dve.sem_inc(lo_ok, 1)
                dve.sem_inc(x2_ok, 2)
                for k in range(KC):
                    dve.wait_ge(w_hi, k + 1)
                    dve.tensor_tensor(w[:, 1, k, :], win[:, k, :], w[:, 0, k, :].bitcast(F32), ALU.subtract).then_inc(w_lo, 1)
                lows(0, 0)
                with dve.Fori(0, NT // 2 - 1) as pair:
                    for u in range(2):
                        lows(2 * pair + u + 1, 1 - u)
                        add(2 * pair + u, u, pair)
                lows(NT - 1, 1)
                add(NT - 2, 0, NT // 2 - 1)
                add(NT - 1, 1, NT // 2 - 1)

            @block.tensor
            def _(pe):
                def turn(t, u, pair):
                    pe.wait_ge(mix_in[u], 16 * (pair + 1))
                    pe.wait_ge(lo_ok, t + 1)
                    for k in range(KC):
                        last = pe.transpose(tps[:, k // 4, (k % 4) * P:(k % 4 + 1) * P], mixin[u][:, k * P:(k + 1) * P], c.ident[:])
                    last.then_inc(turned, 1)

                def multiply(t, u):
                    pe.wait_ge(lo_ok, t + 2)
                    pe.wait_ge(x2_ok, t + 1)
                    for half in range(2):
                        last = split_product(pe, acc[u][:, half, :], oT[u], w, slice(half * H, (half + 1) * H))
                    last.then_inc(mm_ok, 1)

                pe.sem_inc(mm_ok, 2)
                turn(0, 0, 0)
                pe.wait_ge(w_lo, KC)
                with pe.Fori(0, NT // 2 - 1) as pair:
                    for u in range(2):
                        turn(2 * pair + u + 1, 1 - u, pair + u)
                        multiply(2 * pair + u, u)
                turn(NT - 1, 1, NT // 2 - 1)
                multiply(NT - 2, 0)
                multiply(NT - 1, 1)


def split_product(pe, dst, left, right, cols):
    passes = [(k, a, b) for k in range(KC) for a, b in ((0, 0), (0, 1), (1, 0))]
    for n, (k, a, b) in enumerate(passes):
        last = pe.matmul(dst, left[:, a, k, :], right[:, b, k, cols], start=(n == 0), stop=(n == len(passes) - 1))
    return last


def memory_phase(nc, c, mem, w_cq, w_ckv, w_co, wqk, wvo):
    MT = MEM // P
    PER_HEAD = DH // P
    with ExitStack() as ctx:
        sb, ps, sem = alloc(nc, ctx, "fold")
        xin = [sb(f"xin{t}", [P, D]) for t in range(MT)]
        sq = sb("sq", [P, MT, D], BF16)
        gcol = sb("gcol", [P, KC])
        ss, ms, rs = (sb(n, [P, MT]) for n in ("ss", "ms", "rs"))
        memT = sb("memT", [P, KC, MEM])
        wch = [sb(f"wch{u}", [P, KC, P]) for u in range(2)]
        kvT = sb("kvT", [P, 2 * KC, MEM])
        wqT = [sb(f"wqT{d}", [P, KC, P]) for d in range(2)]
        vT = sb("vT", [P, PER_HEAD, MEM])
        wo = [sb(f"wo{u}", [P, PER_HEAD, D]) for u in range(2)]
        tps = ps("tps", [P, 2, 4, P])
        kvps = [ps(f"kvps{u}", [P, 512]) for u in range(2)]
        fps = ps("fps", [P, 4, 512])
        mem_in, wo_in, gcol_ok = sem("mem_in"), [sem(f"wo_in{u}") for u in range(2)], sem("gcol_ok")
        w_ok = [sem(f"w_ok{u}") for u in range(2)]
        sum_ok, eps_ok, rs_ok, scaled = sem("sum_ok"), sem("eps_ok"), sem("rs_ok"), sem("scaled")
        turned, t_act, t_dve = sem("turned"), sem("t_act"), sem("t_dve")
        kv_mm, kv_out, fold_mm, f_act, f_dve, v_ok = (sem(n) for n in ("kv_mm", "kv_out", "fold_mm", "f_act", "f_dve", "v_ok"))
        kin, qin = (w.rearrange("(k p) n -> p k n", p=P) for w in (w_ckv, w_cq))
        with nc.Block() as block:
            @block.sync
            def _(sp):
                for t in range(MT):
                    sp.dma_start(xin[t][:], mem[t * P:(t + 1) * P, :]).then_inc(mem_in, 16)
                oin = w_co.rearrange("(h k p) n -> h p k n", p=P, k=PER_HEAD)
                for u in range(2):
                    sp.dma_start(wo[u][:], oin[u]).then_inc(wo_in[u], 16)
                with sp.Fori(0, KC) as pair:
                    for u in range(2):
                        m = 2 * pair + u
                        sp.wait_ge(kv_mm, m + 1)
                        sp.dma_start(wch[u][:], kin[:, :, bass.ds(m * P, P)]).then_inc(w_ok[u], 16)
                for u in range(2):
                    sp.wait_ge(kv_mm, 2 * KC + u + 1)
                    sp.dma_start(wch[u][:], qin[:, :, u * P:(u + 1) * P]).then_inc(w_ok[u], 16)
                with sp.Fori(1, HEADS) as h:
                    for u in range(2):
                        sp.wait_ge(turned, 2 * (2 * h + u + MT) - 2)
                        sp.dma_start(wch[u][:], qin[:, :, bass.ds((2 * h + u) * P, P)]).then_inc(w_ok[u], 16)
                for h in range(2, HEADS):
                    sp.wait_ge(fold_mm, h + HEADS - 1)
                    sp.dma_start(wo[h % 2][:], oin[h]).then_inc(wo_in[h % 2], 16)

            @block.gpsimd
            def _(pool):
                pool.wait_ge(sum_ok, MT)
                pool.tensor_tensor(ms[:], ss[:], c.eps[:, 0:MT], ALU.add).then_inc(eps_ok, 1)
                pool.wait_ge(eps_ok, 1)
                pool.tensor_tensor(rs[:], ms[:], c.half[:, 0:MT], ALU.pow).then_inc(rs_ok, 1)

            @block.scalar
            def _(act):
                for s in (t_act, f_act, kv_out):
                    act.sem_inc(s, 1)
                act.wait_ge(mem_in, 16 * MT)
                act.wait_ge(gcol_ok, 1)
                for t in range(MT):
                    act.activation(sq[:, t, :], xin[t][:], ACT.Square, scale=D ** -0.5,
                                   accum_out=ss[:, t:t + 1]).then_inc(sum_ok, 1)
                for t in range(MT):
                    act.wait_ge(turned, 2 * t + 2)
                    for k in range(4):
                        last = act.activation(memT[:, 4 + k, t * P:(t + 1) * P], tps[:, 1, k, :], ACT.Copy,
                                              scale=c.g_mem[:, 4 + k:5 + k])
                    last.then_inc(t_act, 1)
                with act.Fori(0, KC) as pair:
                    for u in range(2):
                        m = 2 * pair + u
                        act.wait_ge(kv_mm, m + 3)
                        act.activation(kvT[:, bass.ds(m, 1), :].rearrange("p a n -> p (a n)"), kvps[u][:, 0:MEM],
                                       ACT.Copy).then_inc(kv_out, 1)
                with act.Fori(0, HEADS) as h:
                    for d in range(2):
                        act.wait_ge(turned, 2 * (2 * h + d + MT) + 2)
                        act.activation(wqT[d][:, 4:8, :], tps[:, 1, :, :], ACT.Copy).then_inc(t_act, 1)
                    act.wait_ge(fold_mm, h + 1)
                    for row in range(KC):
                        last = act.activation(wqk[:, 0, row, bass.ds(h * MEM, MEM)],
                                              fps[:, row // 2, (row % 2) * MEM:(row % 2 + 1) * MEM], ACT.Copy,
                                              scale=gcol[:, row:row + 1])
                        if row % 4 == 3:
                            last.then_inc(f_act, 1)
                with act.Fori(0, HEADS) as h:
                    act.wait_ge(fold_mm, h + HEADS + 1)
                    for mt in range(MT):
                        act.activation(wvo[:, 0, bass.ds(2 * h + mt, 1), :].rearrange("p a n -> p (a n)"),
                                       fps[:, 2 * mt:2 * mt + 2, :].rearrange("p b n -> p (b n)"), ACT.Copy).then_inc(f_act, 1)

            @block.vector
            def _(dve):
                dve.sem_inc(t_dve, 1)
                dve.sem_inc(f_dve, 1)
                dve.tensor_scalar(gcol[:], c.g_cross[:], DH ** -0.5, None, ALU.mult).then_inc(gcol_ok, 1)
                dve.wait_ge(gcol_ok, 1)
                dve.wait_ge(rs_ok, 1)
                for t in range(MT):
                    dve.tensor_scalar(xin[t][:], xin[t][:], rs[:, t:t + 1], None, ALU.mult).then_inc(scaled, 1)
                for t in range(MT):
                    dve.wait_ge(turned, 2 * t + 1)
                    dve.tensor_tensor(memT[:, 0:4, t * P:(t + 1) * P], tps[:, 0, :, :],
                                      c.g_mem[:, 0:4].unsqueeze(2).to_broadcast([P, 4, P]), ALU.mult).then_inc(t_dve, 1)
                with dve.Fori(0, HEADS) as h:
                    for d in range(2):
                        dve.wait_ge(turned, 2 * (2 * h + d + MT) + 1)
                        dve.tensor_copy(wqT[d][:, 0:4, :], tps[:, 0, :, :]).then_inc(t_dve, 1)
                    for row in range(KC):
                        if row % 4 == 0:
                            dve.wait_ge(f_act, 2 * h + 2 + row // 4)
                        cols = bass.ds(h * MEM, MEM)
                        last = dve.scalar_tensor_tensor(out=wqk[:, 1, row, cols],
                                                        in0=fps[:, row // 2, (row % 2) * MEM:(row % 2 + 1) * MEM],
                                                        scalar=gcol[:, row:row + 1], in1=wqk[:, 0, row, cols].bitcast(F32),
                                                        op0=ALU.mult, op1=ALU.subtract)
                    last.then_inc(f_dve, 1)
                dve.wait_ge(kv_out, 2 * KC + 1)
                with dve.Fori(0, HEADS) as h:
                    dve.wait_ge(fold_mm, h + HEADS)
                    dve.tensor_copy(vT[:], kvT[:, bass.ds(KC + 2 * h, 2), :]).then_inc(v_ok, 1)
                    for mt in range(MT):
                        dve.wait_ge(f_act, 2 * (h + HEADS) + 2 + mt)
                        row = bass.ds(2 * h + mt, 1)
                        last = dve.tensor_tensor(wvo[:, 1, row, :].rearrange("p a n -> p (a n)"),
                                                 fps[:, 2 * mt:2 * mt + 2, :].rearrange("p b n -> p (b n)"),
                                                 wvo[:, 0, row, :].rearrange("p a n -> p (a n)").bitcast(F32), ALU.subtract)
                    last.then_inc(f_dve, 1)

            @block.tensor
            def _(pe):
                pe.sem_inc(kv_mm, 2)

                def turn(blocks, n):
                    pe.wait_ge(t_act, n + 1)
                    pe.wait_ge(t_dve, n + 1)
                    for k, blk in enumerate(blocks):
                        last = pe.transpose(tps[:, k // 4, k % 4, :], blk, c.ident[:])
                        if k % 4 == 3:
                            last.then_inc(turned, 1)

                for t in range(MT):
                    pe.wait_ge(scaled, t + 1)
                    turn([xin[t][:, k * P:(k + 1) * P] for k in range(KC)], t)
                pe.wait_ge(t_act, MT + 1)
                pe.wait_ge(t_dve, MT + 1)
                with pe.Fori(0, KC) as pair:
                    for u in range(2):
                        m = 2 * pair + u
                        pe.wait_ge(w_ok[u], 16 * (pair + 1))
                        if u == 0:
                            pe.wait_ge(kv_out, m + 1)
                        for k in range(KC):
                            last = pe.matmul(kvps[u][:, 0:MEM], wch[u][:, k, :], memT[:, k, :], start=(k == 0), stop=(k == KC - 1))
                        last.then_inc(kv_mm, 1)
                pe.wait_ge(kv_out, 2 * KC + 1)
                with pe.Fori(0, HEADS) as h:
                    for d in range(2):
                        pe.wait_ge(w_ok[d], 16 * (h + KC + 1))
                        turn([wch[d][:, k, :] for k in range(KC)], 2 * h + d + MT)
                    pe.wait_ge(t_act, 2 * h + MT + 3)
                    pe.wait_ge(t_dve, 2 * h + MT + 3)
                    pe.wait_ge(f_dve, h + 1)
                    for row in range(KC):
                        for d in range(2):
                            last = pe.matmul(fps[:, row // 2, (row % 2) * MEM:(row % 2 + 1) * MEM], wqT[d][:, row, :],
                                             kvT[:, bass.ds(2 * h + d, 1), :].rearrange("p a n -> p (a n)"),
                                             start=(d == 0), stop=(d == 1))
                    last.then_inc(fold_mm, 1)
                with pe.Fori(0, HEADS // 2) as pair:
                    for u in range(2):
                        h = 2 * pair + u
                        pe.wait_ge(wo_in[u], 16 * (pair + 1))
                        pe.wait_ge(v_ok, h + 1)
                        pe.wait_ge(f_dve, h + HEADS + 1)
                        for half in range(2):
                            for mt in range(MT):
                                for d in range(2):
                                    last = pe.matmul(fps[:, 2 * mt + half, :], vT[:, d, mt * P:(mt + 1) * P],
                                                     wo[u][:, d, half * 512:(half + 1) * 512], start=(d == 0), stop=(d == 1))
                        last.then_inc(fold_mm, 1)


def cross_phase(nc, c, x2d, wqk, wvo, w_rg, w_re, g_ffn, x3, h4, logits):
    H = 512
    NR = GROUPS + EXPERTS
    with ExitStack() as ctx:
        sb, ps, sem = alloc(nc, ctx, "cross")
        wr = sb("wr", [P, KC, NR])
        xa, xr = sb("xa", [P, D]), sb("xr", [P, D])
        x3t = [sb(f"x3t{u}", [P, D]) for u in range(2)]
        xn4 = sb("xn4", [P, D])
        xp4 = [sb(f"xp4{u}", [P, 2, D], F32R) for u in range(2)]
        gb = sb("gb", [P, D])
        hT3, pT = (sb(n, [P, 2, KC, P], F32R) for n in ("hT3", "pT"))
        hT4 = sb("hT4", [P, KC, P])
        xn3, pr, sq = sb("xn3", [P, D]), sb("pr", [P, HEADS, MEM]), sb("sq", [P, 2, D], BF16)
        top, ntop, l, rl = (sb(n, [P, HEADS]) for n in ("top", "ntop", "l", "rl"))
        ss3, ms3, rs3, ss4, ms4, rs4 = (sb(n, [P, 1]) for n in ("ss3", "ms3", "rs3", "ss4", "ms4", "rs4"))
        tA, tB, sc, acc = (ps(n, [P, 2, H]) for n in ("tA", "tB", "sc", "acc"))
        w_ok = sem("w_ok")
        xa_in, xr_in = sem("xa_in"), sem("xr_in")
        names = ("s_mm max_ok exp_ok p_ok ss3_ok ms3_ok rs3_ok xn3_ok p_turned pT_dve "
                 "pT_act h4_turned hT4_dve hT4_act co_mm x3_ok ss4_ok ms4_ok rs4_ok xf_ok xh_ok xn4_ok r_mm logits_ok h3_turned "
                 "hT3_dve hT3_act dve_step").split()
        s = {n: sem(n) for n in names}
        x3_out = [sem(f"x3_out{u}") for u in range(2)]
        h4_out = [sem(f"h4_out{u}") for u in range(2)]

        def upto(t):
            return t + 2

        def steps(eng, step):
            step(-1, 1, -1, True, False, False, False)
            step(0, 0, 0, True, True, False, False)
            step(1, 1, 0, True, True, True, False)
            with eng.Fori(1, NT // 2 - 1) as pair:
                for u in range(2):
                    step(2 * pair + u, u, pair, True, True, True, True)
            step(NT - 2, 0, NT // 2 - 1, True, True, True, True)
            step(NT - 1, 1, NT // 2 - 1, False, True, True, True)
            step(NT, 0, NT // 2, False, False, True, True)
            step(NT + 1, 1, NT // 2, False, False, False, True)

        def lows(tile):
            return tile[:, 0, :].rearrange("p (k n) -> p k n", n=P)

        with nc.Block() as block:
            @block.sync
            def _(sp):
                def load(tile, t, done):
                    sp.dma_start(tile[:], x2d[bass.ds(t * P, P), :]).then_inc(done, 16)

                def step(t, u, pair, n, a, b, d):
                    if n and a:
                        sp.wait_ge(s["xn3_ok"], upto(t))
                        load(xa, t + 1, xa_in)
                    if d:
                        sp.wait_ge(s["xn4_ok"], upto(t - 2))
                        sp.dma_start(h4[bass.ds((t - 2) * P, P), :],
                                     xp4[u][:].rearrange("p a n -> p (a n)").bitcast(F32)).then_inc(h4_out[u], 16)
                    if b:
                        sp.wait_ge(s["x3_ok"], upto(t - 1))
                        sp.dma_start(x3[bass.ds((t - 1) * P, P), :], x3t[1 - u][:]).then_inc(x3_out[1 - u], 16)
                    if a and b:
                        load(xr, t, xr_in)

                for out in x3_out + h4_out:
                    sp.sem_inc(out, 16)
                load(xa, 0, xa_in)
                load(xr, 0, xr_in)
                sp.dma_start(gb[:], g_ffn.partition_broadcast(P)).then_inc(w_ok, 16)
                with nc.allow_non_contiguous_dma("routers' weights: 4 and 16 columns"):
                    sp.dma_start(wr[:, :, 0:GROUPS], w_rg.rearrange("(k p) n -> p k n", p=P)).then_inc(w_ok, 16)
                    sp.dma_start(wr[:, :, GROUPS:], w_re.rearrange("(k p) n -> p k n", p=P)).then_inc(w_ok, 16)
                steps(sp, step)
                for u in range(2):
                    sp.wait_ge(x3_out[u], 16 * (NT // 2 + 1))
                    sp.wait_ge(h4_out[u], 16 * (NT // 2 + 1))

            @block.gpsimd
            def _(pool):
                for n in ("ms3_ok", "rs3_ok", "ms4_ok", "rs4_ok"):
                    pool.sem_inc(s[n], 1)

                def rsqrt(t, k, ss, ms, rs):
                    pool.wait_ge(s[f"ss{k}_ok"], upto(t))
                    pool.tensor_tensor(ms[:], ss[:], c.eps[:, 0:1], ALU.add).then_inc(s[f"ms{k}_ok"], 1)
                    pool.wait_ge(s[f"ms{k}_ok"], upto(t))
                    pool.tensor_tensor(rs[:], ms[:], c.half[:, 0:1], ALU.pow).then_inc(s[f"rs{k}_ok"], 1)

                def step(t, u, pair, n, a, b, d):
                    if d:
                        rsqrt(t - 2, 4, ss4, ms4, rs4)
                    if n:
                        rsqrt(t + 1, 3, ss3, ms3, rs3)

                steps(pool, step)

            @block.scalar
            def _(act):
                for n in ("exp_ok", "xh_ok", "ss3_ok", "pT_act", "hT4_act", "ss4_ok", "hT3_act"):
                    act.sem_inc(s[n], 1)

                def highs(t, name, turned, used, dst, src):
                    act.wait_ge(s[turned], upto(t))
                    act.wait_ge(s[used], upto(t - 1))
                    for b in range(2):
                        act.activation(dst[:, 0, 4 * b:4 * b + 4, :].rearrange("p k n -> p (k n)"), src[:, b, :],
                                       ACT.Copy).then_inc(s[name], 1)

                def high(t, name, turned, used, dst, src):
                    act.wait_ge(s[turned], upto(t))
                    act.wait_ge(s[used], upto(t - 1))
                    act.activation(dst[:, 4:8, :].rearrange("p k n -> p (k n)"), src[:, 1, :], ACT.Copy).then_inc(s[name], 1)

                def step(t, u, pair, n, a, b, d):
                    if b:
                        highs(t - 1, "pT_act", "p_turned", "co_mm", pT, tB)
                    if d:
                        act.wait_ge(s["x3_ok"], upto(t - 2))
                        act.activation(sq[:, 1, :], x3t[u][:], ACT.Square, scale=D ** -0.5, accum_out=ss4[:]).then_inc(s["ss4_ok"], 1)
                    if n:
                        act.wait_ge(xa_in, 16 * (t + 2))
                        act.wait_ge(s["rs3_ok"], upto(t))
                        act.activation(sq[:, 0, :], xa[:], ACT.Square, scale=D ** -0.5, accum_out=ss3[:]).then_inc(s["ss3_ok"], 1)
                    if d:
                        act.wait_ge(s["xf_ok"], upto(t - 2))
                        act.activation(xp4[u][:, 0, :], xn4[:], ACT.Copy).then_inc(s["xh_ok"], 1)
                    if n:
                        highs(t + 1, "hT3_act", "h3_turned", "s_mm", hT3, tB)
                    if a:
                        act.wait_ge(s["max_ok"], upto(t))
                        act.wait_ge(s["p_turned"], upto(t - 1))
                        for h in range(HEADS):
                            last = act.activation(pr[:, h, :], sc[:, h // 2, (h % 2) * MEM:(h % 2 + 1) * MEM], ACT.Exp,
                                                  bias=ntop[:, h:h + 1], accum_out=l[:, h:h + 1])
                        last.then_inc(s["exp_ok"], 1)
                    if d:
                        high(t - 2, "hT4_act", "h4_turned", "r_mm", hT4, tA)

                steps(act, step)

            @block.vector
            def _(dve):
                for n in ("max_ok", "p_ok", "xn3_ok", "pT_dve", "hT4_dve", "x3_ok", "xn4_ok", "logits_ok",
                          "hT3_dve", "xf_ok"):
                    dve.sem_inc(s[n], 1)
                o = Order(dve, s["dve_step"])
                dve.wait_ge(w_ok, 48)

                def low(t, name, turned, used, dst, src):
                    dve.wait_ge(s[turned], upto(t))
                    dve.wait_ge(s[used], upto(t - 1))
                    dve.tensor_copy(dst[:, 0:4, :], lows(src)).then_inc(s[name], 1)

                def rest(t, name, hi, dst, src):
                    for b in range(2):
                        dve.wait_ge(s[hi], 2 * t + 2 + b)
                        part = dst[:, :, 4 * b:4 * b + 4, :].rearrange("p a k n -> p a (k n)")
                        last = dve.tensor_tensor(part[:, 1, :], src[:, b, :], part[:, 0, :].bitcast(F32), ALU.subtract)
                    last.then_inc(s[name], 1)

                def step(t, u, pair, n, a, b, d):
                    if b:
                        rest(t - 1, "pT_dve", "pT_act", pT, tB)
                    if d:
                        dve.wait_ge(s["rs4_ok"], upto(t - 2))
                        dve.wait_ge(h4_out[u], 16 * pair)
                        dve.wait_ge(s["h4_turned"], upto(t - 3))
                        dve.scalar_tensor_tensor(out=xn4[:], in0=x3t[u][:], scalar=rs4[:, 0:1], in1=gb[:],
                                                 op0=ALU.mult, op1=ALU.mult).then_inc(s["xf_ok"], 1)
                    if n:
                        dve.wait_ge(s["rs3_ok"], upto(t + 1))
                        dve.wait_ge(s["h3_turned"], upto(t))
                        dve.tensor_scalar(xn3[:], xa[:], rs3[:, 0:1], None, ALU.mult).then_inc(s["xn3_ok"], 1)
                    if d:
                        dve.wait_ge(s["xh_ok"], upto(t - 2))
                        dve.tensor_tensor(xp4[u][:, 1, :], xn4[:], xp4[u][:, 0, :].bitcast(F32),
                                          ALU.subtract).then_inc(s["xn4_ok"], 1)
                    if a:
                        o.at(2 * t)
                        dve.wait_ge(s["s_mm"], upto(t))
                        o(dve.tensor_reduce(top[:], sc[:].rearrange("p a (b m) -> p (a b) m", m=MEM), AX, ALU.max))
                        dve.tensor_scalar(ntop[:], top[:], -1.0, None, ALU.mult).then_inc(s["max_ok"], 1)
                    if n:
                        rest(t + 1, "hT3_dve", "hT3_act", hT3, tB)
                    if a:
                        dve.wait_ge(s["exp_ok"], upto(t))
                        o(dve.reciprocal(rl[:], l[:]))
                        dve.tensor_tensor(pr[:], pr[:], rl[:].unsqueeze(2).to_broadcast([P, HEADS, MEM]),
                                          ALU.mult).then_inc(s["p_ok"], 1)
                    if d:
                        low(t - 2, "hT4_dve", "h4_turned", "r_mm", hT4, tA)
                    if b:
                        dve.wait_ge(s["co_mm"], upto(t - 1))
                        dve.wait_ge(xr_in, 16 * t)
                        dve.wait_ge(x3_out[1 - u], 16 * (pair + u))
                        dve.tensor_tensor(x3t[1 - u][:], acc[:].rearrange("p a n -> p (a n)"), xr[:],
                                          ALU.add).then_inc(s["x3_ok"], 1)
                    if d:
                        dve.wait_ge(s["r_mm"], upto(t - 2))
                        dve.tensor_copy(logits[:, bass.ds(t - 2, 1), :].rearrange("p a n -> p (a n)"),
                                        tA[:, 0, 0:NR]).then_inc(s["logits_ok"], 1)

                steps(dve, step)

            @block.tensor
            def _(pe):
                for n in ("s_mm", "p_turned", "h4_turned", "co_mm", "r_mm", "h3_turned"):
                    pe.sem_inc(s[n], 1)
                pe.wait_ge(w_ok, 48)

                def turn(name, dst, blocks):
                    for k, blk in enumerate(blocks):
                        last = pe.transpose(dst[:, k // 4, (k % 4) * P:(k % 4 + 1) * P], blk, c.ident[:])
                    last.then_inc(s[name], 1)

                def cut(tile):
                    return [tile[:, k * P:(k + 1) * P] for k in range(KC)]

                def product(name, dst, left, right):
                    for half in range(2):
                        last = split_product(pe, dst[:, half, :], left, right, slice(half * H, (half + 1) * H))
                    last.then_inc(s[name], 1)

                def step(t, u, pair, n, a, b, d):
                    if b:
                        pe.wait_ge(s["p_ok"], upto(t - 1))
                        pe.wait_ge(s["hT3_dve"], upto(t) if a else upto(t - 1))
                        turn("p_turned", tB, cut(pr[:].rearrange("p h m -> p (h m)")))
                    if a:
                        pe.wait_ge(s["hT3_dve"], upto(t))
                        pe.wait_ge(s["exp_ok"], upto(t - 1))
                        product("s_mm", sc, hT3, wqk)
                    if n:
                        pe.wait_ge(s["xn3_ok"], upto(t + 1))
                        if b:
                            pe.wait_ge(s["pT_dve"], upto(t - 1))
                        turn("h3_turned", tB, cut(xn3))
                    if d:
                        pe.wait_ge(s["xn4_ok"], upto(t - 2))
                        pe.wait_ge(s["logits_ok"], upto(t - 3))
                        for k in range(KC):
                            for part in range(2):
                                last = pe.matmul(tA[:, k // 4, (k % 4) * P:(k % 4 + 1) * P],
                                                 xp4[u][:, part, k * P:(k + 1) * P], c.identr[:],
                                                 start=(part == 0), stop=(part == 1))
                        last.then_inc(s["h4_turned"], 1)
                    if b:
                        pe.wait_ge(s["pT_dve"], upto(t - 1))
                        pe.wait_ge(s["x3_ok"], upto(t - 2))
                        product("co_mm", acc, pT, wvo)
                    if d:
                        pe.wait_ge(s["hT4_dve"], upto(t - 2))
                        pe.wait_ge(s["hT4_act"], upto(t - 2))
                        for k in range(KC):
                            last = pe.matmul(tA[:, 0, 0:NR], hT4[:, k, :], wr[:, k, :], start=(k == 0), stop=(k == KC - 1))
                        last.then_inc(s["r_mm"], 1)

                steps(pe, step)


EXPERT, CHANGED, BEFORE, LOADS = range(4)
TOTAL = 4 * NBLK


def route_phase(nc, c, b_rg, b_re, logits, dest, gate, rows, table):
    NR = GROUPS + EXPERTS
    ROUND = 8
    with ExitStack() as ctx:
        sb, ps, sem = alloc(nc, ctx, "route")
        bias = sb("bias", [P, NR])
        lg = sb("lg", [P, NT, NR])
        rank = sb("rank", [P, PER_GROUP])
        thr, blk_id, row_id, keep, one = (sb("thr", [P, NT]), sb("blk_id", [P, NBLK]), sb("row_id", [P, P]),
                                          sb("keep", [P, EXPERTS, NT]), sb("one", [P, P]))
        before, token = sb("before", [P, P]), sb("token", [P, NT])
        t1 = [sb(f"t1_{n}", [P, NT]) for n in range(3)]
        t4 = [sb(f"t4_{n}", [P, NT, 4]) for n in range(4)]
        og, oe = sb("og", [P, NT, GROUPS]), sb("oe", [P, 2, NT, PER_GROUP])
        pg, e2, half_gate = sb("pg", [P, NT]), sb("e2", [P, NT]), sb("half_gate", [P, NT])
        t16 = sb("t16", [P, NT, GROUPS, PER_GROUP])
        pick = sb("pick", [P, 2, NT, EXPERTS])
        both = sb("both", [P, NT, EXPERTS])
        tot, cum, offs = (sb(n, [P, EXPERTS, NT]) for n in ("tot", "cum", "offs"))
        counts, nblk, endb, startr = (sb(n, [P, EXPERTS]) for n in ("counts", "nblk", "endb", "startr"))
        wide = sb("wide", [P, NBLK, EXPERTS])
        eb, ch, tm1 = sb("eb", [P, NBLK]), sb("ch", [P, NBLK]), sb("tm1", [P, 1])
        bt = [sb(f"bt{n}", [P, NBLK]) for n in range(4)]
        place, part, destf = sb("place", [P, NT, EXPERTS]), sb("part", [P, NT, EXPERTS]), sb("destf", [P, NT, 2])
        hi_i, lo_i = sb("hi_i", [P, NT, 2], I32), sb("lo_i", [P, NT, 2], I32)
        hi, lo = sb("hi", [P, NT, 2]), sb("lo", [P, NT, 2])
        low_hot = [sb(f"low_hot{u}", [P, ROUND, P]) for u in range(2)]
        high_hot = sb("high_hot", [P, 2 * NT, NBLK])
        cps, rps = ps("cps", [P, 2, NT * EXPERTS]), ps("rps", [P, NBLK])
        bias_in, set_ok, ask_exp, exp_ok, count_ok, count_mm, hot_ok, hot_used, rows_mm, step_dve, step_pool = (
            sem(n) for n in ("bias_in", "set_ok", "ask_exp", "exp_ok", "count_ok", "count_mm", "hot_ok", "hot_used",
                             "rows_mm", "step_dve", "step_pool"))
        with nc.Block() as block:
            @block.sync
            def _(sp):
                sp.dma_start(bias[:, 0:GROUPS], b_rg.partition_broadcast(P)).then_inc(bias_in, 16)
                sp.dma_start(bias[:, GROUPS:], b_re.partition_broadcast(P)).then_inc(bias_in, 16)

            @block.gpsimd
            def _(pool):
                o = Order(pool, step_pool)
                real = dict(allow_small_or_imprecise_dtypes=True)
                o(pool.iota(rank[:], [[-1, PER_GROUP]], base=PER_GROUP, channel_multiplier=0, **real))
                o(pool.iota(thr[:], [[P, NT]], base=0, channel_multiplier=0, **real))
                o(pool.iota(blk_id[:], [[1, NBLK]], base=0, channel_multiplier=0, **real))
                o(pool.iota(row_id[:], [[1, P]], base=0, channel_multiplier=0, **real))
                o(pool.iota(token[:], [[P, NT]], base=0, channel_multiplier=1, **real))
                o(pool.memset(keep[:], 1.0))
                o(pool.memset(keep[:, :, 0:1], 0.0))
                o(pool.memset(one[:], 1.0))
                o(pool.affine_select(out=before[:], in_=one[:], compare_op=ALU.is_gt, fill=0.0, base=0,
                                     pattern=[[1, P]], channel_multiplier=-1))
                pool.sem_inc(set_ok, 1)

            @block.scalar
            def _(act):
                act.wait_ge(ask_exp, 1)
                act.activation(t4[1][:], t4[0][:], ACT.Exp).then_inc(exp_ok, 1)
                act.wait_ge(ask_exp, 2)
                act.activation(e2[:], t1[2][:], ACT.Exp).then_inc(exp_ok, 1)

            @block.tensor
            def _(pe):
                pe.wait_ge(count_ok, 1)
                flat = both[:].rearrange("p t e -> p (t e)")
                pe.matmul(cps[:, 0, :], before[:], flat, start=True, stop=True)
                pe.matmul(cps[:, 1, :], one[:], flat, start=True, stop=True).then_inc(count_mm, 1)
                for n in range(2 * NT):
                    if n % ROUND == 0:
                        pe.wait_ge(hot_ok, n // ROUND + 1)
                    last = pe.matmul(rps[:], low_hot[n // ROUND % 2][:, n % ROUND, :], high_hot[:, n, :],
                                     start=(n == 0), stop=(n == 2 * NT - 1))
                    if n % ROUND == ROUND - 1:
                        last.then_inc(hot_used, 1)

            @block.vector
            def _(dve):
                o = Order(dve, step_dve)

                def over(x, n):
                    return x.unsqueeze(2).to_broadcast([P, x.shape[1], n])

                def rows_of(x, n):
                    return x.unsqueeze(1).to_broadcast([P, n, x.shape[1]])

                def first_of(out, d, tmp, top):
                    o(dve.tensor_scalar(tmp[:], d[:], 0.0, None, ALU.is_ge))
                    o(dve.tensor_tensor(tmp[:], tmp[:], rows_of(rank[:], NT), ALU.mult))
                    o(dve.tensor_reduce(top[:], tmp[:], AX, ALU.max))
                    o(dve.tensor_tensor(out, tmp[:], over(top[:], 4), ALU.is_equal))

                dve.wait_ge(bias_in, 32)
                dve.wait_ge(set_ok, 1)
                o(dve.tensor_tensor(lg[:], logits[:], rows_of(bias[:], NT), ALU.add))
                o(dve.tensor_reduce(t1[0][:], lg[:, :, 0:GROUPS], AX, ALU.max))
                dve.tensor_tensor(t4[0][:], lg[:, :, 0:GROUPS], over(t1[0][:], GROUPS), ALU.subtract).then_inc(ask_exp, 1)
                dve.wait_ge(ask_exp, 1)
                first_of(og[:], t4[0], t4[2], t1[1])
                dve.wait_ge(exp_ok, 1)
                o(dve.tensor_reduce(t1[0][:], t4[1][:], AX, ALU.add))
                o(dve.reciprocal(pg[:], t1[0][:]))
                for g in range(GROUPS):
                    last = dve.tensor_tensor(t16[:, :, g, :], lg[:, :, GROUPS + g * PER_GROUP:GROUPS + (g + 1) * PER_GROUP],
                                             og[:, :, g:g + 1].to_broadcast([P, NT, PER_GROUP]), ALU.mult)
                o(last)
                o(dve.tensor_reduce(t4[3][:], t16[:].rearrange("p t g j -> p t j g"), AX, ALU.add))
                o(dve.tensor_reduce(t1[0][:], t4[3][:], AX, ALU.max))
                o(dve.tensor_tensor(t4[3][:], t4[3][:], over(t1[0][:], 4), ALU.subtract))
                first_of(oe[:, 0, :, :], t4[3], t4[2], t1[1])
                o(dve.scalar_tensor_tensor(out=t4[3][:], in0=oe[:, 0, :, :], scalar=NEG, in1=t4[3][:], op0=ALU.mult, op1=ALU.add))
                dve.tensor_reduce(t1[2][:], t4[3][:], AX, ALU.max).then_inc(ask_exp, 1)
                dve.wait_ge(ask_exp, 2)
                o(dve.tensor_tensor(t4[3][:], t4[3][:], over(t1[2][:], 4), ALU.subtract))
                first_of(oe[:, 1, :, :], t4[3], t4[2], t1[1])
                dve.wait_ge(exp_ok, 2)
                o(dve.tensor_scalar(t1[0][:], e2[:], 1.0, None, ALU.add))
                o(dve.reciprocal(half_gate[:], t1[0][:]))
                o(dve.tensor_tensor(half_gate[:], half_gate[:], pg[:], ALU.mult))
                dve.tensor_copy(gate[:, :, 0], half_gate[:])
                dve.tensor_tensor(gate[:, :, 1], half_gate[:], e2[:], ALU.mult)
                for k in range(2):
                    for g in range(GROUPS):
                        last = dve.tensor_tensor(pick[:, k, :, g * PER_GROUP:(g + 1) * PER_GROUP], oe[:, k, :, :],
                                                 og[:, :, g:g + 1].to_broadcast([P, NT, PER_GROUP]), ALU.mult)
                o(last)
                dve.tensor_tensor(both[:], pick[:, 0, :, :], pick[:, 1, :, :], ALU.add).then_inc(count_ok, 1)
                dve.wait_ge(count_mm, 1)
                o(dve.tensor_copy(tot[:], cps[:, 1, :].rearrange("p (t e) -> p e t", e=EXPERTS)))
                o(dve.tensor_tensor_scan(cum[:].rearrange("p e t -> p (e t)"), keep[:].rearrange("p e t -> p (e t)"),
                                         tot[:].rearrange("p e t -> p (e t)"), 0.0, ALU.mult, ALU.add))
                dve.tensor_copy(counts[:], cum[:, :, NT - 1])
                o(dve.tensor_tensor(offs[:], cum[:], tot[:], ALU.subtract))
                o(dve.tensor_tensor(tot[:], over(counts[:], NT), rows_of(thr[:], EXPERTS), ALU.is_gt))
                o(dve.tensor_reduce(nblk[:], tot[:], AX, ALU.add))
                o(dve.tensor_tensor_scan(endb[:], one[:, 0:EXPERTS], nblk[:], 0.0, ALU.mult, ALU.add))
                o(dve.tensor_tensor(startr[:], endb[:], nblk[:], ALU.subtract))
                o(dve.tensor_scalar(startr[:], startr[:], float(P), None, ALU.mult))
                o(dve.tensor_tensor(offs[:], offs[:], over(startr[:], NT), ALU.add))
                o(dve.tensor_tensor(place[:], cps[:, 0, :].rearrange("p (t e) -> p t e", e=EXPERTS),
                                    offs[:].rearrange("p e t -> p t e"), ALU.add))
                for k in range(2):
                    o(dve.tensor_tensor(part[:], place[:], pick[:, k, :, :], ALU.mult))
                    o(dve.tensor_reduce(destf[:, :, k:k + 1].rearrange("p t a -> p (t a)"), part[:], AX, ALU.add))
                o(dve.tensor_copy(dest[:], destf[:]))
                o(dve.tensor_scalar(hi_i[:], dest[:], 7, None, ALU.arith_shift_right))
                o(dve.tensor_scalar(lo_i[:], dest[:], P - 1, None, ALU.bitwise_and))
                o(dve.tensor_copy(hi[:], hi_i[:]))
                o(dve.tensor_copy(lo[:], lo_i[:]))
                hi_f, lo_f = (x[:].rearrange("p t k -> p (t k)") for x in (hi, lo))
                o(dve.tensor_tensor(high_hot[:], rows_of(blk_id[:], 2 * NT), over(hi_f, NBLK), ALU.is_equal))
                for k in range(2):
                    last = dve.tensor_tensor(high_hot[:].rearrange("p (t k) b -> p t k b", k=2)[:, :, k, :],
                                             high_hot[:].rearrange("p (t k) b -> p t k b", k=2)[:, :, k, :],
                                             over(token[:], NBLK), ALU.mult)
                o(last)
                for n in range(2 * NT // ROUND):
                    if n >= 2:
                        dve.wait_ge(hot_used, n - 1)
                    dve.tensor_tensor(low_hot[n % 2][:], rows_of(row_id[:], ROUND),
                                      over(lo_f[:, n * ROUND:(n + 1) * ROUND], P), ALU.is_equal).then_inc(hot_ok, 1)
                o(dve.tensor_scalar(tm1[:], endb[:, EXPERTS - 1:EXPERTS], -1.0, None, ALU.add))
                o(dve.tensor_scalar(bt[0][:], blk_id[:], tm1[:, 0:1], None, ALU.min))
                o(dve.tensor_tensor(wide[:], rows_of(endb[:], NBLK), over(bt[0][:], EXPERTS), ALU.is_le))
                o(dve.tensor_reduce(eb[:], wide[:], AX, ALU.add))
                o(dve.memset(ch[:, 0:1], 1.0))
                o(dve.tensor_tensor(ch[:, 1:], eb[:, 1:], eb[:, 0:NBLK - 1], ALU.not_equal))
                o(dve.memset(bt[1][:], 1.0))
                o(dve.tensor_tensor_scan(bt[2][:], bt[1][:], ch[:], 0.0, ALU.mult, ALU.add))
                o(dve.tensor_tensor(bt[0][:], ch[:], blk_id[:], ALU.mult))
                o(dve.memset(bt[1][:], 0.0))
                o(dve.memset(bt[3][:, 0:1], -1.0))
                o(dve.tensor_tensor_scan(bt[3][:, 1:], bt[0][:, 0:NBLK - 1], bt[1][:, 0:NBLK - 1], -1.0, ALU.max, ALU.add))
                o(dve.tensor_scalar(bt[3][:], bt[3][:], 1.0, None, ALU.add))
                for what, src in ((EXPERT, eb), (CHANGED, ch), (BEFORE, bt[3]), (LOADS, bt[2])):
                    dve.tensor_copy(table[:, what * NBLK:(what + 1) * NBLK], src[:])
                dve.tensor_copy(table[:, TOTAL:TOTAL + 1], endb[:, EXPERTS - 1:EXPERTS])
                dve.wait_ge(hot_used, 2 * NT // ROUND)
                dve.tensor_copy(rows[:], rps[:])


def expert_phase(nc, c, h4, w_gate, w_up, w_down, rows, table, ys):
    ND = DE // P
    GU, DN = 2 * DE, D
    DOWN = KC * GU
    ALL = DOWN + ND * DN
    with ExitStack() as ctx:
        sb, ps, sem = alloc(nc, ctx, "exp")
        raw = sb("raw", [P, ALL])
        wh, wl = sb("wh", [P, ALL], F32R), sb("wl", [P, ALL], F32R)
        xg, idx = sb("xg", [P, 2 * D], F32R), sb("idx", [P, 1], I32)
        xT = sb("xT", [P, 2, KC, P], F32R)
        sg, hid = sb("sg", [P, DE]), sb("hid", [P, DE])
        hs, hT = sb("hs", [P, 2, DE], F32R), sb("hT", [P, 2, ND, P], F32R)
        y = sb("y", [P, D])
        xps, hps = ps("xps", [P, 2, 512], F32R), ps("hps", [P, 2, DE], F32R)
        gups, yps = ps("gups", [P, 2, DE]), ps("yps", [P, 2, 512])
        names = ("x_turned x_low x_high gu_mm silu_ok hid_ok hi_ok hs_ok h_turned hT_ok hT_act down_mm y_low y_high "
                 "gu_hi gu_ok dn_hi dn_ok").split()
        s = {n: sem(n) for n in names}
        gu_dma, dn_dma, gu_raw, dn_raw, idx_ok, pool_go, x_in, y_out, passed = (sem(n) for n in (
            "gu_dma", "dn_dma", "gu_raw", "dn_raw", "idx_ok", "pool_go", "x_in", "y_out", "passed"))

        def upto(b, per=1):
            return b * per + per + 1

        def entry(eng, b, what, most):
            return eng.value_load(table[0:1, bass.ds(b + what * NBLK, 1)], min_val=0, max_val=most)

        def steps(eng, step):
            step(0, True, False)
            with eng.Fori(1, NBLK - 1) as b:
                step(b, False, False)
            step(NBLK - 1, False, True)

        with nc.Block() as block:
            @block.sync
            def _(sp):
                def load_gate_up(e):
                    gu = raw[:, 0:DOWN].rearrange("p (k m n) -> p k m n", m=2, n=DE)
                    for m, src in ((0, w_gate), (1, w_up)):
                        sp.dma_start(gu[:, :, m, :], src[bass.ds(e, 1), :, :].rearrange("a (k p) n -> p (a k) n", p=P)
                                     ).then_inc(gu_dma, 16)

                def load_down(e):
                    sp.dma_start(raw[:, DOWN:].rearrange("p (k n) -> p k n", n=D),
                                 w_down[bass.ds(e, 1), :, :].rearrange("a (k p) n -> p (a k) n", p=P)).then_inc(dn_dma, 16)

                def step(b, first, last):
                    e = entry(sp, b, EXPERT, EXPERTS - 1)
                    before = entry(sp, b, BEFORE, NBLK)
                    loads = entry(sp, b, LOADS, EXPERTS)
                    with sp.If(entry(sp, b, CHANGED, 1) >= 1):
                        sp.wait_ge(s["gu_ok"], before * KC + 1)
                        load_gate_up(e)
                        sp.wait_ge(gu_dma, loads * 32)
                        sp.sem_inc(gu_raw, 1)
                        sp.wait_ge(s["dn_ok"], before * ND + 1)
                        load_down(e)
                        sp.wait_ge(dn_dma, loads * 16)
                        sp.sem_inc(dn_raw, 1)
                    with sp.Else():
                        sp.sem_inc(gu_raw, 1)
                        sp.sem_inc(dn_raw, 1)

                steps(sp, step)

            @block.gpsimd
            def _(pool):
                def step(b, first, last):
                    if not first:
                        pool.wait_ge(s["x_turned"], upto(b - 1, 2))
                        pool.sem_inc(pool_go, 1)
                    pool.tensor_copy(idx[:], rows[:, bass.ds(b, 1)]).then_inc(idx_ok, 1)
                    pool.wait_ge(idx_ok, b + 1)
                    pool.sem_inc(pool_go, 1)
                    pool.indirect_dma_start(out=xg[:].bitcast(F32), out_offset=None, in_=h4[:, :],
                                            in_offset=bass.IndirectOffsetOnAxis(ap=idx[:, 0:1], axis=0)).then_inc(x_in, 16)

                steps(pool, step)

            @block.scalar
            def _(act):
                for n in ("x_high", "silu_ok", "hi_ok", "hT_act", "y_high", "gu_hi", "dn_hi"):
                    act.sem_inc(s[n], 1)
                act.sem_inc(y_out, 16)

                def rows_in(b, part):
                    act.wait_ge(s["x_turned"], upto(b, 2) - 1 + part)
                    act.activation(xT[:, part, 4:8, :].rearrange("p k n -> p (k n)"), xps[:, 1, :].bitcast(F32),
                                   ACT.Copy).then_inc(s["x_high"], 1)

                def round_weights(b, arrived, name, done, start, chunks, size):
                    with act.If(entry(act, b, CHANGED, 1) >= 1):
                        act.wait_ge(arrived, b + 1)
                        act.wait_ge(s[done], upto(b - 1, chunks))
                        for k in range(chunks):
                            cols = slice(start + k * size, start + (k + 1) * size)
                            act.activation(wh[:, cols], raw[:, cols], ACT.Copy).then_inc(s[name], 1)
                    with act.Else():
                        act.sem_inc(s[name], chunks)

                def step(b, first, last):
                    if first:
                        rows_in(0, 0)
                        rows_in(0, 1)
                        round_weights(0, gu_raw, "gu_hi", "gu_ok", 0, KC, GU)
                    act.wait_ge(s["gu_mm"], upto(b))
                    act.activation(sg[:], gups[:, 0, :], ACT.Silu).then_inc(s["silu_ok"], 1)
                    if not last:
                        rows_in(b + 1, 0)
                    act.wait_ge(s["hid_ok"], upto(b))
                    act.activation(hs[:, 0, :], hid[:], ACT.Copy).then_inc(s["hi_ok"], 1)
                    if not last:
                        rows_in(b + 1, 1)
                        round_weights(b + 1, gu_raw, "gu_hi", "gu_ok", 0, KC, GU)
                    if not first:
                        result(b - 1)
                    round_weights(b, dn_raw, "dn_hi", "dn_ok", DOWN, ND, DN)
                    act.wait_ge(s["h_turned"], upto(b))
                    act.activation(hT[:, 1, :, :].rearrange("p k n -> p (k n)"), hps[:, 1, :].bitcast(F32),
                                   ACT.Copy).then_inc(s["hT_act"], 1)
                    if last:
                        result(b)

                def result(b):
                    act.wait_ge(s["down_mm"], upto(b))
                    act.wait_ge(y_out, 16 * (b + 1))
                    act.activation(y[:, 512:], yps[:, 1, :], ACT.Copy).then_inc(s["y_high"], 1)
                    act.wait_ge(s["y_high"], upto(b))
                    act.wait_ge(s["y_low"], upto(b))
                    act.dma_start(ys[bass.ds(b * P, P), :], y[:]).then_inc(y_out, 16)

                steps(act, step)
                act.wait_ge(y_out, 16 * (NBLK + 1))

            @block.vector
            def _(dve):
                for n in ("x_low", "hid_ok", "hs_ok", "hT_ok", "y_low", "gu_ok", "dn_ok"):
                    dve.sem_inc(s[n], 1)

                def rows_in(b, part):
                    dve.wait_ge(s["x_turned"], upto(b, 2) - 1 + part)
                    dve.tensor_copy(xT[:, part, 0:4, :].rearrange("p k n -> p (k n)"),
                                    xps[:, 0, :].bitcast(F32)).then_inc(s["x_low"], 1)

                def rest_of_weights(b, name, hi, start, chunks, size):
                    with dve.If(entry(dve, b, CHANGED, 1) >= 1):
                        for k in range(chunks):
                            cols = slice(start + k * size, start + (k + 1) * size)
                            dve.wait_ge(s[hi], b * chunks + k + 2)
                            dve.tensor_tensor(wl[:, cols], raw[:, cols], wh[:, cols].bitcast(F32),
                                              ALU.subtract).then_inc(s[name], 1)
                    with dve.Else():
                        dve.sem_inc(s[name], chunks)

                def result(b):
                    dve.wait_ge(s["down_mm"], upto(b))
                    dve.wait_ge(y_out, 16 * (b + 1))
                    dve.tensor_copy(y[:, 0:512], yps[:, 0, :]).then_inc(s["y_low"], 1)

                def step(b, first, last):
                    if first:
                        rows_in(0, 0)
                        rows_in(0, 1)
                        rest_of_weights(0, "gu_ok", "gu_hi", 0, KC, GU)
                    dve.wait_ge(s["silu_ok"], upto(b))
                    dve.tensor_tensor(hid[:], sg[:], gups[:, 1, :], ALU.mult).then_inc(s["hid_ok"], 1)
                    if not last:
                        rows_in(b + 1, 0)
                    dve.wait_ge(s["hi_ok"], upto(b))
                    dve.tensor_tensor(hs[:, 1, :], hid[:], hs[:, 0, :].bitcast(F32), ALU.subtract).then_inc(s["hs_ok"], 1)
                    if not last:
                        rows_in(b + 1, 1)
                        rest_of_weights(b + 1, "gu_ok", "gu_hi", 0, KC, GU)
                    if not first:
                        result(b - 1)
                    rest_of_weights(b, "dn_ok", "dn_hi", DOWN, ND, DN)
                    dve.wait_ge(s["h_turned"], upto(b))
                    dve.tensor_copy(hT[:, 0, :, :].rearrange("p k n -> p (k n)"), hps[:, 0, :].bitcast(F32)).then_inc(s["hT_ok"], 1)
                    if last:
                        result(b)

                steps(dve, step)

            @block.tensor
            def _(pe):
                for n in ("x_turned", "gu_mm", "h_turned", "down_mm"):
                    pe.sem_inc(s[n], 1)
                blocks = pe.value_load(table[0:1, TOTAL:TOTAL + 1], min_val=0, max_val=NBLK)

                def rows_turned(b, part):
                    if part == 0:
                        pe.wait_ge(x_in, 16 * (b + 1))
                    for n in ("x_low", "x_high"):
                        pe.wait_ge(s[n], upto(b, 2) - 2 + part)
                    for k in range(KC):
                        last = pe.transpose(xps[:, k // 4, (k % 4) * P:(k % 4 + 1) * P],
                                            xg[:, part * D + k * P:part * D + (k + 1) * P], c.identr[:])
                    last.then_inc(s["x_turned"], 1)

                def triple(dst, left, k, cols, first, last):
                    pe.matmul(dst, left[:, 0, k, :], wh[:, cols], start=first, stop=False)
                    pe.matmul(dst, left[:, 0, k, :], wl[:, cols], start=False, stop=False)
                    return pe.matmul(dst, left[:, 1, k, :], wh[:, cols], start=False, stop=last)

                def gate_up(b):
                    for n in ("x_low", "x_high"):
                        pe.wait_ge(s[n], upto(b, 2))
                    pe.wait_ge(s["hid_ok"], upto(b - 1))
                    with pe.If(blocks > b):
                        for k in range(KC):
                            pe.wait_ge(s["gu_ok"], b * KC + k + 2)
                            for m in range(2):
                                cols = slice(k * GU + m * DE, k * GU + (m + 1) * DE)
                                last = triple(gups[:, m, :], xT, k, cols, k == 0, k == KC - 1)
                        last.then_inc(s["gu_mm"], 1)
                    with pe.Else():
                        pe.sem_inc(s["gu_mm"], 1)

                def hidden_turned(b):
                    pe.wait_ge(s["hs_ok"], upto(b))
                    pe.wait_ge(s["hi_ok"], upto(b))
                    pe.wait_ge(s["hT_ok"], upto(b - 1))
                    pe.wait_ge(s["hT_act"], upto(b - 1))
                    for part in range(2):
                        for k in range(ND):
                            last = pe.transpose(hps[:, part, k * P:(k + 1) * P], hs[:, part, k * P:(k + 1) * P], c.identr[:])
                    last.then_inc(s["h_turned"], 1)

                def down(b, half):
                    if half == 0:
                        pe.wait_ge(s["hT_ok"], upto(b))
                        pe.wait_ge(s["hT_act"], upto(b))
                        pe.wait_ge(s["y_low"], upto(b - 1))
                        pe.wait_ge(s["y_high"], upto(b - 1))
                    with pe.If(blocks > b):
                        for k in range(ND):
                            if half == 0:
                                pe.wait_ge(s["dn_ok"], b * ND + k + 2)
                            cols = slice(DOWN + k * DN + half * 512, DOWN + k * DN + half * 512 + 512)
                            last = triple(yps[:, half, :], hT, k, cols, k == 0, k == ND - 1)
                        if half == 1:
                            last.then_inc(s["down_mm"], 1)
                    with pe.Else():
                        if half == 1:
                            pe.sem_inc(s["down_mm"], 1)
                        else:
                            pe.sem_inc(passed, 1)

                def step(b, first, last):
                    if first:
                        rows_turned(0, 0)
                        rows_turned(0, 1)
                    gate_up(b)
                    if not last:
                        rows_turned(b + 1, 0)
                    if not first:
                        down(b - 1, 0)
                    if not last:
                        rows_turned(b + 1, 1)
                    if not first:
                        down(b - 1, 1)
                    hidden_turned(b)
                    if last:
                        down(b, 0)
                        down(b, 1)

                steps(pe, step)


def combine_phase(nc, c, x3, ys, dest, gate, gain, out):
    DEPTH = 4
    with ExitStack() as ctx:
        sb, ps, sem = alloc(nc, ctx, "comb")
        R = range(DEPTH)
        idx = [sb(f"idx{u}", [P, 2], I32) for u in R]
        xin, y0, y1, res = ([sb(f"{n}{u}", [P, D]) for u in R] for n in ("xin", "y0", "y1", "res"))
        gb, sq = sb("gb", [P, D]), sb("sq", [P, D])
        ss, ms, rs = ([sb(f"{n}{u}", [P, 1]) for u in R] for n in ("ss", "ms", "rs"))
        g_in, idx_ok, pool_go, sum_ok, ss_ok, ms_ok, rs_ok, done, part = (sem(n) for n in (
            "g_in", "idx_ok", "pool_go", "sum_ok", "ss_ok", "ms_ok", "rs_ok", "done", "part"))
        x_in, y0_in, y1_in, stored = ([sem(f"{n}{u}") for u in R] for n in ("x_in", "y0_in", "y1_in", "stored"))
        with nc.Block() as block:
            @block.sync
            def _(sp):
                sp.dma_start(gb[:], gain.partition_broadcast(P)).then_inc(g_in, 16)
                with sp.Fori(0, NT // DEPTH) as four:
                    for u in R:
                        t = DEPTH * four + u
                        sp.wait_ge(done, t + 1)
                        sp.dma_start(xin[u][:], x3[bass.ds(t * P, P), :]).then_inc(x_in[u], 16)

            @block.gpsimd
            def _(pool):
                def gather(t, u):
                    pool.wait_ge(done, t + 1)
                    pool.sem_inc(pool_go, 1)
                    pool.tensor_copy(idx[u][:], dest[:, bass.ds(t, 1), :].rearrange("p a k -> p (a k)")).then_inc(idx_ok, 1)
                    pool.wait_ge(idx_ok, t + 1)
                    pool.sem_inc(pool_go, 1)
                    for k, (dst, arrived) in enumerate(((y0, y0_in), (y1, y1_in))):
                        pool.indirect_dma_start(out=dst[u][:], out_offset=None, in_=ys[:, :],
                                                in_offset=bass.IndirectOffsetOnAxis(ap=idx[u][:, k:k + 1], axis=0)
                                                ).then_inc(arrived[u], 16)

                def rsqrt(t, u):
                    pool.wait_ge(ss_ok, t + 1)
                    pool.tensor_tensor(ms[u][:], ss[u][:], c.eps[:, 0:1], ALU.add).then_inc(ms_ok, 1)
                    pool.wait_ge(ms_ok, t + 1)
                    pool.tensor_tensor(rs[u][:], ms[u][:], c.half[:, 0:1], ALU.pow).then_inc(rs_ok, 1)

                for u in R:
                    gather(u, u)
                with pool.Fori(0, NT // DEPTH - 1) as four:
                    for u in R:
                        rsqrt(DEPTH * four + u, u)
                        gather(DEPTH * four + u + DEPTH, u)
                for u in R:
                    rsqrt(NT - DEPTH + u, u)

            @block.scalar
            def _(act):
                for s in stored:
                    act.sem_inc(s, 16)
                with act.Fori(0, NT // DEPTH) as four:
                    for u in R:
                        t = DEPTH * four + u
                        act.wait_ge(sum_ok, t + 1)
                        act.wait_ge(done, t + DEPTH)
                        act.activation(sq[:], res[u][:], ACT.Square, scale=D ** -0.5, accum_out=ss[u][:]).then_inc(ss_ok, 1)
                        act.wait_ge(done, t + DEPTH + 1)
                        act.dma_start(out[bass.ds(t * P, P), :], res[u][:]).then_inc(stored[u], 16)
                for s in stored:
                    act.wait_ge(s, 16 * (NT // DEPTH + 1))

            @block.vector
            def _(dve):
                dve.sem_inc(done, DEPTH)
                dve.wait_ge(g_in, 16)
                with dve.Fori(0, NT // DEPTH) as four:
                    for u in R:
                        t = DEPTH * four + u
                        dve.wait_ge(x_in[u], 16 * (four + 1))
                        dve.wait_ge(y0_in[u], 16 * (four + 1))
                        dve.scalar_tensor_tensor(out=y0[u][:], in0=y0[u][:], scalar=gate[:, bass.ds(t, 1), 0], in1=xin[u][:],
                                                 op0=ALU.mult, op1=ALU.add).then_inc(part, 1)
                        dve.wait_ge(part, t + 1)
                        dve.wait_ge(y1_in[u], 16 * (four + 1))
                        dve.wait_ge(stored[u], 16 * (four + 1))
                        dve.scalar_tensor_tensor(out=res[u][:], in0=y1[u][:], scalar=gate[:, bass.ds(t, 1), 1], in1=y0[u][:],
                                                 op0=ALU.mult, op1=ALU.add).then_inc(sum_ok, 1)
                        dve.wait_ge(rs_ok, t + 1)
                        dve.scalar_tensor_tensor(out=res[u][:], in0=res[u][:], scalar=rs[u][:, 0:1], in1=gb[:],
                                                 op0=ALU.mult, op1=ALU.mult).then_inc(done, 1)


def trunk(nc, x, mem, norm_mix_g, w_in, w_gla_a2, b_gla_a, gla_norm_g, diff_norm_g, lambda_q1, lambda_k1,
          lambda_q2, lambda_k2, w_out, norm_cross_g, norm_mem_g, w_cq, w_ckv, w_co, norm_ffn_g, w_router_grp,
          b_router_grp, w_router_exp, b_router_exp, w_e_gate, w_e_up, w_e_down, norm_final_g, out):
    x = x.rearrange("b s d -> (b s) d")
    mem = mem.rearrange("b s d -> (b s) d")
    out = out.rearrange("b s d -> (b s) d")
    w_in = w_in[0]
    x2 = nc.dram_tensor("x2", (SEQ, D), F32).ap()
    mixed = nc.dram_tensor("mixed", (SEQ, D), F32).ap()
    x3 = nc.dram_tensor("x3", (SEQ, D), F32).ap()
    h4 = nc.dram_tensor("h4", (SEQ, 2 * D), F32).ap()
    ys = nc.dram_tensor("ys", (NBLK * P, D), F32).ap()
    with ExitStack() as ctx:
        sb, ps, sem = alloc(nc, ctx, "all")

        class c:
            ident = sb("ident", [P, P])
            identr = sb("identr", [P, P], F32R)
            identb = sb("identb", [P, P], BF16)
            maskb = sb("maskb", [P, P], BF16)
            half = sb("half", [P, HEADS])
            eps = sb("eps", [P, HEADS])
            g_mix = sb("g_mix", [P, KC])
            g_cross = sb("g_cross", [P, KC])
            g_mem = sb("g_mem", [P, KC])
        c.gains = [(c.g_mix[:], norm_mix_g[0].rearrange("(k p) -> p k", p=P)),
                   (c.g_cross[:], norm_cross_g[0].rearrange("(k p) -> p k", p=P)),
                   (c.g_mem[:], norm_mem_g[0].rearrange("(k p) -> p k", p=P))]
        constants(nc, c)
        with ExitStack() as mix:
            hT = mix.enter_context(nc.sbuf_tensor("hT", [P, KC, SEQ], F32))
            norm_phase(nc, c, x, hT)
            gla_phase(nc, c, hT, w_in, w_gla_a2[0], b_gla_a[0], gla_norm_g[0], mixed)
            diff_phase(nc, c, hT, w_in, diff_norm_g[0], (lambda_q1[0], lambda_k1[0], lambda_q2[0], lambda_k2[0]), mixed)
        out_phase(nc, c, x, mixed, w_out[0], x2)
        with ExitStack() as cross:
            logits = cross.enter_context(nc.sbuf_tensor("logits", [P, NT, GROUPS + EXPERTS], F32))
            with ExitStack() as fold:
                wqk = fold.enter_context(nc.sbuf_tensor("wqk", [P, 2, KC, D], F32R))
                wvo = fold.enter_context(nc.sbuf_tensor("wvo", [P, 2, KC, D], F32R))
                memory_phase(nc, c, mem, w_cq[0], w_ckv[0], w_co[0], wqk, wvo)
                cross_phase(nc, c, x2, wqk, wvo, w_router_grp[0], w_router_exp[0],
                            norm_ffn_g[0], x3, h4, logits)
            dest = cross.enter_context(nc.sbuf_tensor("dest", [P, NT, 2], I32))
            gate = cross.enter_context(nc.sbuf_tensor("gate", [P, NT, 2], F32))
            rows = cross.enter_context(nc.sbuf_tensor("rows", [P, NBLK], I32))
            table = cross.enter_context(nc.sbuf_tensor("table", [P, TOTAL + 1], I32))
            route_phase(nc, c, b_router_grp[0], b_router_exp[0], logits, dest, gate, rows, table)
            expert_phase(nc, c, h4, w_e_gate[0], w_e_up[0], w_e_down[0], rows, table, ys)
            combine_phase(nc, c, x3, ys, dest, gate, norm_final_g, out)


_INS = ["x", "mem", "norm_mix_g", "w_in", "w_gla_a2", "b_gla_a", "gla_norm_g", "diff_norm_g", "lambda_q1",
        "lambda_k1", "lambda_q2", "lambda_k2", "w_out", "norm_cross_g", "norm_mem_g", "w_cq", "w_ckv", "w_co",
        "norm_ffn_g", "w_router_grp", "b_router_grp", "w_router_exp", "b_router_exp", "w_e_gate", "w_e_up",
        "w_e_down", "norm_final_g"]


def kernel(**inputs):
    import numpy as _np
    import concourse.bacc as _bacc
    from concourse.bass_utils import run_bass_kernel_spmd as _run

    nc = _bacc.Bacc("TRN2", target_bir_lowering=False, num_devices=1)
    arrays, args = {}, []
    for name in _INS:
        a = _np.ascontiguousarray(inputs[name])
        arrays[f"in_{name}"] = a
        args.append(nc.dram_tensor(f"in_{name}", a.shape, mybir.dt.from_np(a.dtype), kind="ExternalInput").ap())
    out = nc.dram_tensor("out", (1, SEQ, D), F32, kind="ExternalOutput").ap()
    trunk(nc, *args, out)
    r = _run(nc, [arrays], core_ids=[0])
    return r.results[0]["out"]
```
